# Optimizing a Trainium2 kernel written in Bass

```python
import math
import jax, jax.numpy as jnp
from jax import lax
import numpy as np

D_MODEL = 1024
BATCH = 1
SEQ = 1024
DEPTH = 2
DEC_BATCH = 8
DEC_SEQ = 1
PAST_LEN = 256
PAGE_SIZE = 128

N_A_LAYERS = DEPTH // 2
N_B_LAYERS = DEPTH - N_A_LAYERS
GROUP_SIZE = 16
N_GROUPS = D_MODEL // GROUP_SIZE
STATE_DIM = 64
N_HEADS = 8
HEAD_DIM = D_MODEL // N_HEADS // 2
ROT_DIM = HEAD_DIM // 4
ROPE_THETA = 500000.0
D_FF = ((8 * D_MODEL // 3 + 255) // 256) * 256
Q_BLOCK = 128
EPS = 1e-5
NEG = -1e30

kernel_name = "yoco_s5_diffattn_step"

def rmsnorm(x, g):
    xf = x.astype(jnp.float32)
    r = lax.rsqrt(jnp.mean(xf * xf, axis=-1, keepdims=True) + EPS)
    return (xf * r * g.astype(jnp.float32)).astype(x.dtype)

def rope_partial(x, pos):
    inv = ROPE_THETA ** (-jnp.arange(0, ROT_DIM, 2, dtype=jnp.float32) / ROT_DIM)
    ang = pos.astype(jnp.float32)[:, None] * inv[None, :]
    cos = jnp.cos(ang)[None, :, None, None, :]
    sin = jnp.sin(ang)[None, :, None, None, :]
    xf = x.astype(jnp.float32)
    half = ROT_DIM // 2
    x1, x2, xp = xf[..., :half], xf[..., half:ROT_DIM], xf[..., ROT_DIM:]
    out = jnp.concatenate([x1 * cos - x2 * sin, x2 * cos + x1 * sin, xp], axis=-1)
    return out.astype(x.dtype)

def swiglu(h, wg, wu, wd):
    return (jax.nn.silu(h @ wg) * (h @ wu)) @ wd

def s5_mixer(u, h0_re, h0_im, a_re, a_im, log_dt, b_re, b_im, c_re, c_im, d, w_ga, w_gb):
    bsz, seqlen, _ = u.shape
    f32 = jnp.float32
    a_re = a_re.astype(f32); a_im = a_im.astype(f32)
    dt = jnp.exp(log_dt.astype(f32))[:, None]
    mag = jnp.exp(dt * a_re)
    ang = dt * a_im
    abar_re = mag * jnp.cos(ang)
    abar_im = mag * jnp.sin(ang)
    den = a_re * a_re + a_im * a_im
    nr = abar_re - 1.0
    ni = abar_im
    f_re = (nr * a_re + ni * a_im) / den
    f_im = (ni * a_re - nr * a_im) / den
    b_re = b_re.astype(f32); b_im = b_im.astype(f32)
    bbar_re = f_re[..., None] * b_re - f_im[..., None] * b_im
    bbar_im = f_re[..., None] * b_im + f_im[..., None] * b_re
    ug = u.astype(f32).reshape(bsz, seqlen, N_GROUPS, GROUP_SIZE)
    bu_re = jnp.einsum("blgh,gph->blgp", ug, bbar_re)
    bu_im = jnp.einsum("blgh,gph->blgp", ug, bbar_im)
    ar = jnp.broadcast_to(abar_re, bu_re.shape)
    ai = jnp.broadcast_to(abar_im, bu_re.shape)

    def combine(e1, e2):
        ar1, ai1, br1, bi1 = e1
        ar2, ai2, br2, bi2 = e2
        return (ar2 * ar1 - ai2 * ai1,
                ar2 * ai1 + ai2 * ar1,
                ar2 * br1 - ai2 * bi1 + br2,
                ar2 * bi1 + ai2 * br1 + bi2)

    acum_re, acum_im, hs_re, hs_im = lax.associative_scan(combine, (ar, ai, bu_re, bu_im), axis=1)
    h0r = h0_re.astype(f32)[:, None]
    h0i = h0_im.astype(f32)[:, None]
    h_re = hs_re + acum_re * h0r - acum_im * h0i
    h_im = hs_im + acum_re * h0i + acum_im * h0r
    y = (jnp.einsum("blgp,ghp->blgh", h_re, c_re.astype(f32))
         - jnp.einsum("blgp,ghp->blgh", h_im, c_im.astype(f32)))
    y = y.reshape(bsz, seqlen, D_MODEL) + d.astype(f32) * u.astype(f32)
    z = jax.nn.gelu(y).astype(u.dtype)
    out = (z @ w_ga) * jax.nn.sigmoid(z @ w_gb)
    return out, h_re[:, -1].astype(h0_re.dtype), h_im[:, -1].astype(h0_im.dtype)

def diff_attention(q, k, v, q_pos, k_pos, lam):
    s = jnp.einsum("bqhcd,bkhcd->bhcqk", q, k, preferred_element_type=jnp.float32) * (HEAD_DIM ** -0.5)
    mask = k_pos[None, :] <= q_pos[:, None]
    s = jnp.where(mask, s, NEG)
    p = jax.nn.softmax(s, axis=-1)
    w = p[:, :, 0] - lam * p[:, :, 1]
    return jnp.einsum("bhqk,bkhe->bqhe", w.astype(v.dtype), v)

def trunk(x, pos, h0_re, h0_im, attend, p):
    bsz, seqlen, _ = x.shape
    new_re, new_im = [], []
    k = v = None
    for layer in range(DEPTH):
        h = rmsnorm(x, p["mix_norm"][layer])
        if layer < N_A_LAYERS:
            i = layer
            y, hr, hi = s5_mixer(h, h0_re[i], h0_im[i], p["ssm_a_re"][i], p["ssm_a_im"][i],
                                 p["ssm_log_dt"][i], p["ssm_b_re"][i], p["ssm_b_im"][i],
                                 p["ssm_c_re"][i], p["ssm_c_im"][i], p["ssm_d"][i],
                                 p["glu_w_a"][i], p["glu_w_b"][i])
            new_re.append(hr)
            new_im.append(hi)
        else:
            j = layer - N_A_LAYERS
            if k is None:
                kv_in = rmsnorm(x, p["kv_norm"])
                k = rope_partial((kv_in @ p["w_k"]).reshape(bsz, seqlen, N_HEADS, 2, HEAD_DIM), pos)
                v = (kv_in @ p["w_v"]).reshape(bsz, seqlen, N_HEADS, 2 * HEAD_DIM)
            q = rope_partial((h @ p["w_q"][j]).reshape(bsz, seqlen, N_HEADS, 2, HEAD_DIM), pos)
            lam_init = 0.8 - 0.6 * math.exp(-0.3 * layer)
            lam = (jnp.exp(jnp.sum(p["lambda_q1"][j].astype(jnp.float32) * p["lambda_k1"][j].astype(jnp.float32)))
                   - jnp.exp(jnp.sum(p["lambda_q2"][j].astype(jnp.float32) * p["lambda_k2"][j].astype(jnp.float32)))
                   + lam_init)
            o = attend(q, k, v, pos, lam)
            o = rmsnorm(o, p["subln"][j]) * (1.0 - lam_init)
            y = o.reshape(bsz, seqlen, D_MODEL) @ p["w_o"][j]
        x = x + y
        x = x + swiglu(rmsnorm(x, p["ffn_norm"][layer]), p["ffn_w_gate"][layer],
                       p["ffn_w_up"][layer], p["ffn_w_down"][layer])
    return rmsnorm(x, p["final_norm"]), k, v, jnp.stack(new_re), jnp.stack(new_im)

def setup_inputs(seed: int = 0) -> dict:
    key = jax.random.key(seed)
    ks = jax.random.split(key, 40)
    nrm = jax.random.normal
    n_pages = PAST_LEN // PAGE_SIZE
    n_used = DEC_BATCH * n_pages
    n_phys = n_used + max(1, n_used // 4)
    hd2 = N_HEADS * 2 * HEAD_DIM
    inp = {}
    inp["x_prompt"] = nrm(ks[0], (BATCH, SEQ, D_MODEL), jnp.float32)
    inp["x_sample"] = nrm(ks[1], (DEC_BATCH, DEC_SEQ, D_MODEL), jnp.float32)
    inp["cache_k"] = nrm(ks[2], (n_phys, PAGE_SIZE, N_HEADS, 2, HEAD_DIM), jnp.float32)
    inp["cache_v"] = nrm(ks[3], (n_phys, PAGE_SIZE, N_HEADS, 2 * HEAD_DIM), jnp.float32)
    inp["state_ssm_re"] = 0.1 * nrm(ks[4], (N_A_LAYERS, DEC_BATCH, N_GROUPS, STATE_DIM), jnp.float32)
    inp["state_ssm_im"] = 0.1 * nrm(ks[5], (N_A_LAYERS, DEC_BATCH, N_GROUPS, STATE_DIM), jnp.float32)
    inp["page_table"] = jax.random.permutation(ks[6], n_phys)[:n_used].reshape(DEC_BATCH, n_pages).astype(jnp.int32)
    inp["mix_norm"] = 1.0 + 0.01 * nrm(ks[7], (DEPTH, D_MODEL), jnp.float32)
    inp["ffn_norm"] = 1.0 + 0.01 * nrm(ks[8], (DEPTH, D_MODEL), jnp.float32)
    inp["kv_norm"] = 1.0 + 0.01 * nrm(ks[9], (D_MODEL,), jnp.float32)
    inp["final_norm"] = 1.0 + 0.01 * nrm(ks[10], (D_MODEL,), jnp.float32)
    inp["ssm_a_re"] = -0.5 + 0.01 * nrm(ks[11], (N_A_LAYERS, N_GROUPS, STATE_DIM), jnp.float32)
    inp["ssm_a_im"] = (math.pi * jnp.arange(STATE_DIM, dtype=jnp.float32)[None, None, :]
                       + 0.01 * nrm(ks[12], (N_A_LAYERS, N_GROUPS, STATE_DIM), jnp.float32))
    inp["ssm_log_dt"] = jax.random.uniform(ks[13], (N_A_LAYERS, N_GROUPS), jnp.float32,
                                           math.log(0.001), math.log(0.1))
    inp["ssm_b_re"] = nrm(ks[14], (N_A_LAYERS, N_GROUPS, STATE_DIM, GROUP_SIZE), jnp.float32) * (2 * GROUP_SIZE) ** -0.5
    inp["ssm_b_im"] = nrm(ks[15], (N_A_LAYERS, N_GROUPS, STATE_DIM, GROUP_SIZE), jnp.float32) * (2 * GROUP_SIZE) ** -0.5
    inp["ssm_c_re"] = nrm(ks[16], (N_A_LAYERS, N_GROUPS, GROUP_SIZE, STATE_DIM), jnp.float32) * STATE_DIM ** -0.5
    inp["ssm_c_im"] = nrm(ks[17], (N_A_LAYERS, N_GROUPS, GROUP_SIZE, STATE_DIM), jnp.float32) * STATE_DIM ** -0.5
    inp["ssm_d"] = nrm(ks[18], (N_A_LAYERS, D_MODEL), jnp.float32)
    inp["glu_w_a"] = nrm(ks[19], (N_A_LAYERS, D_MODEL, D_MODEL), jnp.float32) * D_MODEL ** -0.5
    inp["glu_w_b"] = nrm(ks[20], (N_A_LAYERS, D_MODEL, D_MODEL), jnp.float32) * D_MODEL ** -0.5
    inp["w_q"] = nrm(ks[21], (N_B_LAYERS, D_MODEL, hd2), jnp.float32) * D_MODEL ** -0.5
    inp["w_k"] = nrm(ks[22], (D_MODEL, hd2), jnp.float32) * D_MODEL ** -0.5
    inp["w_v"] = nrm(ks[23], (D_MODEL, hd2), jnp.float32) * D_MODEL ** -0.5
    inp["lambda_q1"] = 0.1 * nrm(ks[24], (N_B_LAYERS, HEAD_DIM), jnp.float32)
    inp["lambda_k1"] = 0.1 * nrm(ks[25], (N_B_LAYERS, HEAD_DIM), jnp.float32)
    inp["lambda_q2"] = 0.1 * nrm(ks[26], (N_B_LAYERS, HEAD_DIM), jnp.float32)
    inp["lambda_k2"] = 0.1 * nrm(ks[27], (N_B_LAYERS, HEAD_DIM), jnp.float32)
    inp["subln"] = 1.0 + 0.01 * nrm(ks[28], (N_B_LAYERS, 2 * HEAD_DIM), jnp.float32)
    inp["w_o"] = nrm(ks[29], (N_B_LAYERS, hd2, D_MODEL), jnp.float32) * hd2 ** -0.5
    inp["ffn_w_gate"] = nrm(ks[30], (DEPTH, D_MODEL, D_FF), jnp.float32) * D_MODEL ** -0.5
    inp["ffn_w_up"] = nrm(ks[31], (DEPTH, D_MODEL, D_FF), jnp.float32) * D_MODEL ** -0.5
    inp["ffn_w_down"] = nrm(ks[32], (DEPTH, D_FF, D_MODEL), jnp.float32) * D_FF ** -0.5
    return inp

def reference(x_prompt, x_sample, cache_k, cache_v, state_ssm_re, state_ssm_im, page_table,
              mix_norm, ffn_norm, kv_norm, final_norm,
              ssm_a_re, ssm_a_im, ssm_log_dt, ssm_b_re, ssm_b_im, ssm_c_re, ssm_c_im, ssm_d,
              glu_w_a, glu_w_b, w_q, w_k, w_v, lambda_q1, lambda_k1, lambda_q2, lambda_k2,
              subln, w_o, ffn_w_gate, ffn_w_up, ffn_w_down):
    p = dict(mix_norm=mix_norm, ffn_norm=ffn_norm, kv_norm=kv_norm, final_norm=final_norm,
             ssm_a_re=ssm_a_re, ssm_a_im=ssm_a_im, ssm_log_dt=ssm_log_dt,
             ssm_b_re=ssm_b_re, ssm_b_im=ssm_b_im, ssm_c_re=ssm_c_re, ssm_c_im=ssm_c_im, ssm_d=ssm_d,
             glu_w_a=glu_w_a, glu_w_b=glu_w_b, w_q=w_q, w_k=w_k, w_v=w_v,
             lambda_q1=lambda_q1, lambda_k1=lambda_k1, lambda_q2=lambda_q2, lambda_k2=lambda_k2,
             subln=subln, w_o=w_o, ffn_w_gate=ffn_w_gate, ffn_w_up=ffn_w_up, ffn_w_down=ffn_w_down)

    def attend_prompt(q, k, v, pos, lam):
        bsz, seqlen = q.shape[0], q.shape[1]
        nb = seqlen // Q_BLOCK
        qb = jnp.moveaxis(q.reshape(bsz, nb, Q_BLOCK, N_HEADS, 2, HEAD_DIM), 1, 0)
        pb = pos.reshape(nb, Q_BLOCK)
        ob = lax.map(lambda a: diff_attention(a[0], k, v, a[1], pos, lam), (qb, pb))
        return jnp.moveaxis(ob, 0, 1).reshape(bsz, seqlen, N_HEADS, 2 * HEAD_DIM)

    pos_p = jnp.arange(SEQ, dtype=jnp.int32)
    h0_p = jnp.zeros((N_A_LAYERS, x_prompt.shape[0], N_GROUPS, STATE_DIM), state_ssm_re.dtype)
    y_prompt, k_prompt, v_prompt, ssm_re_prompt, ssm_im_prompt = trunk(
        x_prompt, pos_p, h0_p, h0_p, attend_prompt, p)

    dec_b = x_sample.shape[0]
    n_pages = page_table.shape[1]
    past_len = n_pages * PAGE_SIZE
    past_k = cache_k[page_table].reshape(dec_b, past_len, N_HEADS, 2, HEAD_DIM)
    past_v = cache_v[page_table].reshape(dec_b, past_len, N_HEADS, 2 * HEAD_DIM)

    def attend_sample(q, k, v, pos, lam):
        k_all = jnp.concatenate([past_k.astype(k.dtype), k], axis=1)
        v_all = jnp.concatenate([past_v.astype(v.dtype), v], axis=1)
        k_pos = jnp.arange(past_len + q.shape[1], dtype=jnp.int32)
        return diff_attention(q, k_all, v_all, pos, k_pos, lam)

    pos_s = PAST_LEN + jnp.arange(DEC_SEQ, dtype=jnp.int32)
    y_sample, k_sample, v_sample, ssm_re_sample, ssm_im_sample = trunk(
        x_sample, pos_s, state_ssm_re, state_ssm_im, attend_sample, p)

    return (y_prompt, y_sample, k_prompt, v_prompt, ssm_re_prompt, ssm_im_prompt,
            k_sample, v_sample, ssm_re_sample, ssm_im_sample)


_drawn_inputs = setup_inputs


def setup_inputs(seed=0):
    import zlib

    import numpy as np

    out = dict(_drawn_inputs(seed))
    spreads = {}
    factors = {'mix_norm': 5.482,
     'ffn_norm': 5.882,
     'kv_norm': 21.031,
     'final_norm': 33.244,
     'ssm_a_re': 16.05,
     'lambda_q1': 5.705,
     'lambda_k1': 8.0,
     'subln': 64.0,
     'lambda_k2': 2.887}
    for name, (base, spread) in spreads.items():
        noise = np.random.default_rng([zlib.crc32(name.encode()), seed]).standard_normal(out[name].shape)
        drawn = base * np.exp(spread * noise) if base else spread * noise
        out[name] = __import__('jax').numpy.asarray(drawn.astype(out[name].dtype))
    for name, factor in factors.items():
        out[name] = (out[name] * factor).astype(out[name].dtype)
    return out
```

```python
import math
from contextlib import ExitStack

import numpy as np
import concourse.bass as bass
from concourse import mybir

F32 = mybir.dt.float32
F32R = mybir.dt.float32r
BF16 = mybir.dt.bfloat16
I32 = mybir.dt.int32
ALU = mybir.AluOpType
ACT = mybir.ActivationFunctionType
AXX = mybir.AxisListType.X
ds = bass.ds

P = 128
DM = 1024
KT = DM // P
SEQ = 1024
NS = 8
T = SEQ + NS
NC = 3
CW = T // NC
TB = CW // 4
DFF = 2816
FT = DFF // P
NIT = FT // 2
NH = 8
HC = 16
HD = 64
ROT = 16
EPS = 1e-5
PAGE = 128
NPG = 2
NG = 64
ST = 64
L = 8
NB = SEQ // L
PAIRS = NG // 2
PARTS = 4
PP = PAIRS // PARTS
GP = NG // PARTS
NW = 9
NJ, NI = 16, 8
NN = NW + NJ + NI
BW = NS + NB
HW_ = NS + 1 + NB
LAM_INIT = 0.8 - 0.6 * math.exp(-0.3)
TWO_PI = 2.0 * math.pi
MAGIC = 12582912.0
MAGIC12 = 3072.0
C1 = 6.28125
C2 = round((TWO_PI - C1) * 2.0**20) / 2.0**20
C3 = TWO_PI - C1 - C2
SIN_SCALE = 6.283185
N_UNITS = 2 * KT + 2 * (3 * FT) + 3 * KT + KT
SEG1 = 108
U_GLU, U_FFN0 = 0, 2 * KT
U_KVQ = U_FFN0 + 3 * FT
U_O = U_KVQ + 3 * KT
U_FFN1 = U_O + KT
GL0, DN0, OP0 = 3, 8, 6
POOL_STEPS, DVE_STEPS = 9, 52


def build(nc, d):
    ctx = ExitStack()
    with ctx:
        top = [((nc.sbuf_base + 31) // 32) * 32]

        def place(name, shape, dt, at=None):
            size = int(np.prod(shape[1:])) * (2 if dt == BF16 else 4)
            size = (size + 31) // 32 * 32
            if at is None:
                at = top[0]
                top[0] += size
                return nc.alloc_sbuf_tensor_at(name, shape, dt, offset=at)
            off = at[0]
            at[0] += size
            assert at[0] <= at[1], (name, at)
            return nc.alloc_sbuf_tensor_at(name, shape, dt, offset=off)

        def sem(name):
            return ctx.enter_context(nc.semaphore(name))

        X = place("X", [P, KT, T], F32)
        RAW_AT = top[0]
        w_raw = place("w_raw", [P, 4, DM], F32)
        w_hi = place("w_hi", [P, 4, DM], F32R)
        w_lo = place("w_lo", [P, 4, DM], F32R)
        ident = place("ident", [P, P], F32)
        identb = place("identb", [P, P], BF16)
        maskb = place("maskb", [P, P], BF16)
        ones = place("ones", [P, P], F32)
        gains = place("gains", [P, 6, KT], F32)
        lamv = place("lamv", [P, 4, HD], F32)
        lamt = place("lamt", [P, 8], F32)
        gsub = place("gsub", [P, 1], F32)
        eps_t = place("eps_t", [P, 1], F32)
        std = place("std", [P, NC, 4], F32)
        rstd = place("rstd", [P, NC, 4], F32)
        diag = place("diag", [TB, 4, TB], F32)
        sel = place("sel", [P, HC], F32)
        pairsel = place("pairsel", [P, 64], F32)
        evenodd = place("evenodd", [P, 2], F32)
        ptab = place("ptab", [1, NS * NPG], I32)
        nmx = place("nmx", [P, 2, 2], F32)
        sums = place("sums", [P, 2, 2], F32)
        rinv = place("rinv", [P, 4, 2], F32)
        rho = place("rho", [P, 2, 1], F32)
        oss = place("oss", [P, 64], F32)
        orst = place("orst", [P, 64], F32)
        qS = place("qS", [P, KT, NS], F32)
        kS = place("kS", [P, KT, NS], F32)
        vS = place("vS", [P, NH, NS], F32)
        dsc = place("dsc", [P, 16], F32)
        tmpd = place("tmpd", [P, 72], F32)

        ACT_AT = top[0]
        act_hi = place("act_hi", [P, KT, T], F32R)
        act_lo = place("act_lo", [P, KT, T], F32R)
        HID_AT = top[0]
        hid_hi = place("hid_hi", [P, 2, 2, T], F32R)
        hid_lo = place("hid_lo", [P, 2, 2, T], F32R)
        MISC_AT = top[0]
        END = nc.sbuf_usable_end
        misc = [MISC_AT, END]
        sq = place("sq", [P, KT, CW], F32, misc)
        tmp = place("tmp", [P, 4, CW], F32, misc)
        R = place("R", [P, T], F32, misc)
        gate = place("gate", [P, NC, CW], F32, misc)
        U = nc.alloc_sbuf_tensor_at("U", [P, KT, T], F32, offset=HID_AT)
        Z = nc.alloc_sbuf_tensor_at("Z", [P, KT, T], F32, offset=HID_AT)
        Y = nc.alloc_sbuf_tensor_at("Y", [P, KT, T], F32, offset=HID_AT)
        ra = [ACT_AT, HID_AT]
        a_in = place("a_in", [P, 3, PAIRS], F32, ra)
        b_in = place("b_in", [P, 2, PAIRS, 16], F32, ra)
        c_in = place("c_in", [P, 2, PAIRS, 16], F32, ra)
        ncr = place("ncr", [P, PAIRS, 16], F32, ra)
        h0 = place("h0", [P, 2, PAIRS, NS], F32, ra)
        hs = place("hs", [P, 2, PAIRS, NS], F32, ra)
        fin = place("fin", [P, 2, PAIRS, 1], F32, ra)
        d16 = place("d16", [16, NG], F32, ra)
        dI = place("dI", [16, GP, 16], F32, ra)
        nvec = place("nvec", [P, NN], F32, ra)
        sm = place("sm", [P, 16, PAIRS], F32, ra)
        sinT = place("sinT", [P, PAIRS, NN], F32, ra)
        cosT = place("cosT", [P, PAIRS, NN], F32, ra)
        decay = place("decay", [P, PAIRS, NW], F32, ra)
        A_re = place("A_re", [P, PAIRS, NW], F32, ra)
        A_im = place("A_im", [P, PAIRS, NW], F32, ra)
        bbar = place("bbar", [P, 3, PP, 16], F32, ra)
        W_re = place("W_re", [P, PP, L, 16], F32, ra)
        W_im = place("W_im", [P, PP, L, 16], F32, ra)
        G_re = place("G_re", [P, PP, NW, 16], F32, ra)
        G_im = place("G_im", [P, PP, NW, 16], F32, ra)
        G_t = place("G_t", [P, PP, NW, 16], F32, ra)
        CB = place("CB", [P, PP, NI, NJ], F32, ra)
        SB = place("SB", [P, PP, NI, NJ], F32, ra)
        rb = [HID_AT, END]
        RT = place("RT", [P, PP, 2, P], F32, rb)
        Vp = place("Vp", [P, 2, PP, NB], F32, rb)
        tw = place("tw", [P, 2, 4, NB], F32, rb)
        H = place("H", [P, 2, PP, HW_], F32, rb)
        TM = place("TM", [P, GP, P], F32, rb)
        ublk = place("ublk", [P, GP, BW], F32, rb)
        usp = place("usp", [16, GP, NS], F32, rb)
        zblk = place("zblk", [P, GP, BW], F32, rb)
        rc = [RAW_AT, RAW_AT + 16384]
        Kc = place("Kc", [16, GP, P], F32, rc)
        CBt = place("CBt", [P, PP, NI, NJ], F32, rc)
        W_t = place("W_t", [P, PP, L, 16], F32, rc)
        rd = [HID_AT, MISC_AT]
        ph = place("ph", [P, PAIRS, NN], F32, rd)
        pl = place("pl", [P, PAIRS, NN], F32, rd)
        re_ = [HID_AT, MISC_AT]
        stage = place("stage", [P, 3, T], F32, re_)
        roped = place("roped", [P, 2, T], F32, re_)
        rtmp = place("rtmp", [P, T], F32, re_)
        cosr = place("cosr", [P, T], F32, re_)
        sinr = place("sinr", [P, T], F32, re_)
        rf = [ACT_AT, HID_AT]
        kh = place("kh", [P, 2, SEQ], F32, rf)
        qh = place("qh", [P, 2, SEQ], F32, rf)
        vT = place("vT", [P, 2, SEQ], F32, rf)
        vtok = place("vtok", [P, 2, KT, P], F32, rf)
        prob = place("prob", [P, 2, 2, SEQ], F32, rf)
        wmix = place("wmix", [P, 2, SEQ], F32, rf)
        wT = place("wT", [P, 2, SEQ], F32, rf)
        junk = place("junk", [P, P], F32, rf)
        O = nc.alloc_sbuf_tensor_at("O", [P, NH, KT, P], F32, offset=HID_AT)
        rg = [MISC_AT, END]
        kpg = place("kpg", [P, 2, DM], F32, rg)
        qb = place("qb", [P, 2, DM], F32, rg)
        stok = place("stok", [P, NPG, NS * HC], F32, rg)
        newl = place("newl", [P, NS, HC], F32, rg)
        p2 = place("p2", [P, 2 * P + 1], F32, rg)
        wtok = place("wtok", [P, 3, 64], F32, rg)
        wnew = place("wnew", [P, P], F32, rg)
        oS = place("oS", [P, NS, NH], F32, rg)
        oS2 = place("oS2", [P, NS, NH], F32, rg)
        qrow = place("qrow", [NS, HC, 8, 8], F32, rg)
        vpg = nc.alloc_sbuf_tensor_at("vpg", [P, 4, DM], F32, offset=MISC_AT)

        pair = [ctx.enter_context(nc.psum_tensor(f"pair{i}", [P, 1024], F32)) for i in range(4)]
        bank = [pair[i // 2][:, (i % 2) * 512:(i % 2) * 512 + 512] for i in range(8)]

        const0_in, const_in = sem("const0_in"), sem("const_in")
        x_in = [sem(f"x_in{n}") for n in range(NC)]
        w_in = [sem(f"w_in{r}") for r in range(4)]
        w_split, w_used = sem("w_split"), sem("w_used")
        w_hi_done = sem("w_hi_done")
        dve_chain, pool_chain, act_chain = sem("dve_chain"), sem("pool_chain"), sem("act_chain")
        nm_sq, nm_ss, nm_std, nm_diag = sem("nm_sq"), sem("nm_ss"), sem("nm_std"), sem("nm_diag")
        nm_bc, nm_r = sem("nm_bc"), sem("nm_r")
        at_tmp, at_hi, at_lo = sem("at_tmp"), sem("at_hi"), sem("at_lo")
        u_done, u_stored = sem("u_done"), sem("u_stored")
        s5_act = sem("s5_act")
        s5_glob = sem("s5_glob")
        s5_small = sem("s5_small")
        s5_zero = sem("s5_zero")
        s5_w, s5_cs, s5_g = sem("s5_w"), sem("s5_cs"), sem("s5_g")
        s5_t, s5_rt, s5_k, s5_kc, s5_kd = (sem(x) for x in ("s5_t", "s5_rt", "s5_k", "s5_kc", "s5_kd"))
        s5_v, s5_vs, s5_vsd, s5_h = (sem(x) for x in ("s5_v", "s5_vs", "s5_vsd", "s5_h"))
        s5_y, s5_gelu = sem("s5_y"), sem("s5_gelu")
        u_in, t_in, z_out, z_in, ssm_out = (sem(x) for x in ("u_in", "t_in", "z_out", "z_in", "ssm_out"))
        z_hi, z_lo = sem("z_hi"), sem("z_lo")
        gl_ready, gl_sig, gl_mul, gl_done = (sem(x) for x in ("gl_ready", "gl_sig", "gl_mul", "gl_done"))
        gu_ready, gu_silu, hid_tmp, hid_hi_s, hid_lo_s = (
            sem(x) for x in ("gu_ready", "gu_silu", "hid_tmp", "hid_hi_s", "hid_lo_s"))
        dn_ready, dn_added = sem("dn_ready"), sem("dn_added")
        kv_ready, kv_evicted, kv_roped = sem("kv_ready"), sem("kv_evicted"), sem("kv_roped")
        kv_out = [sem(f"kv_out{i}") for i in range(3)]
        rope_in, rope_out = sem("rope_in"), sem("rope_out")
        lam_done = sem("lam_done")
        hd_in = [sem(f"hd_in{i}") for i in range(2)]
        a_vt, a_v, a_s, a_max, a_exp, a_mix = (sem(x) for x in ("a_vt", "a_v", "a_s", "a_max", "a_exp", "a_mix"))
        a_r, a_tr, a_wt, a_o, a_oa, a_oc = (sem(x) for x in ("a_r", "a_tr", "a_wt", "a_o", "a_oa", "a_oc"))
        on_std, on_w, on_tr, on_hi, on_lo = (sem(x) for x in ("on_std", "on_w", "on_tr", "on_hi", "on_lo"))
        d_smp, d_qt, d_qrow, d_qout = (sem(x) for x in ("d_smp", "d_qt", "d_qrow", "d_qout"))
        kpg_in = [sem(f"kpg_in{i}") for i in range(2)]
        d_mul, d_red = sem("d_mul"), sem("d_red")
        d_pv, d_new, d_s2, d_p2, d_p2n, d_w, d_wc = (
            sem(x) for x in ("d_pv", "d_new", "d_s2", "d_p2", "d_p2n", "d_w", "d_wc"))
        vpg_in = [sem(f"vpg_in{i}") for i in range(4)]
        d_o, d_sq, d_ssq, d_rs, d_fin = (sem(x) for x in ("d_o", "d_sq", "d_ssq", "d_rs", "d_fin"))
        op_ready, op_added = sem("op_ready"), sem("op_added")
        d_sc, d_hi, d_lo = sem("d_sc"), sem("d_hi"), sem("d_lo")
        passed = sem("passed")
        y_done, y_out = sem("y_done"), sem("y_out")

        block = ctx.enter_context(nc.Block())
        n_const = [0, 0]
        slots = [(tt % 3, tt in (0, 1, 2 * KT, 2 * KT + 1)) for tt in range(3 * KT)]
        n_out = [16 * sum(1 for s, r in slots if s == x and not r) for x in range(3)]

        def bc(ap, axis, shape):
            return ap.unsqueeze(axis).to_broadcast(shape)

        def cs(n):
            return slice(n * CW, (n + 1) * CW)

        def settle(eng):
            eng.sem_inc(passed, 1)

        class Chain:

            def __init__(self, eng, own, base=0, settle=False):
                self.eng, self.own, self.base, self.n, self.settle = eng, own, base, 0, settle

            def add(self, ins):
                self.n += 1
                ins.then_inc(self.own, 1)

            def sync(self):
                self.eng.wait_ge(self.own, self.base + self.n)
                if self.settle:
                    settle(self.eng)

            def step(self, ins):
                self.add(ins)
                self.sync()

        def attention_steps(eng, step):
            for c in range(2):
                step(c, 0, c)
            with eng.Fori(0, 3) as t:
                for c in range(2, 18):
                    step(t * 16 + c, t * 2 + c // 8, c)
            for c in range(50, 64):
                step(c, c // 8, c)

        @block.sync
        def _(sp):
            sp.sem_inc(t_in, 1)
            sp.sem_inc(z_out, 1)

            def const(dst, src, late=1):
                n_const[late] += 16
                sp.dma_start(dst, src).then_inc(const_in if late else const0_in, 16)

            const(a_in[:], d["s_abc"], 0)
            const(nvec[:], d["c_nvec"], 0)
            const(ones[:], d["c_ones"], 0)
            const(b_in[:], d["s_b"], 0)
            for n in range(NC):
                sp.dma_start(X[:, :, cs(n)], d["x_t"].rearrange("(k p) t -> p k t", p=P)[:, :, cs(n)]
                             ).then_inc(x_in[n], 16)
            const(ident[:], d["c_ident"])
            const(gains[:], d["gains"])
            const(c_in[:], d["s_c"])
            const(h0[:], d["s_h0"])
            const(d16[:], d["s_d"])
            const(identb[:], d["c_identb"])
            const(maskb[:], d["c_maskb"])
            for j in range(4):
                const(lamv[:, j, :], d["lam"][j:j + 1, :].to_broadcast([P, HD]))
            const(gsub[:], d["subln"])
            const(sel[:], d["c_sel"])
            const(pairsel[:], d["c_pairsel"])
            const(evenodd[:], d["c_evenodd"])
            const(ptab[:], d["page_table"])
            for r in range(4):
                sp.dma_start(w_raw[:, r, :], d["w"][r]).then_inc(w_in[r], 16)

            sp.wait_ge(u_done, NC)
            sp.dma_start(d["u"].rearrange("(k p) t -> p k t", p=P), U[:]).then_inc(u_stored, 16)
            sp.wait_ge(u_stored, 16)
            sp.wait_ge(s5_zero, 2)
            u_v = d["u"].rearrange("(q g h) t -> q h g t", q=PARTS, g=GP)
            z_v = d["z"].rearrange("(q g h) t -> q h g t", q=PARTS, g=GP)
            with sp.Fori(0, PARTS) as q:
                sp.wait_ge(s5_y, q * 8 + 1)
                for n in range(L):
                    s = L - 1 - n
                    sp.dma_start(ublk[16 * n:16 * n + 16, :, NS:BW],
                                 u_v[ds(q, 1), :, :, s * NB:(s + 1) * NB].rearrange("o h g t -> (o h) g t")
                                 ).then_inc(u_in, 16)
                sp.dma_start(ublk[P - 16:P, :, 0:NS],
                             u_v[ds(q, 1), :, :, SEQ:T].rearrange("o h g t -> (o h) g t")).then_inc(u_in, 16)
                sp.dma_start(usp[:], u_v[ds(q, 1), :, :, SEQ:T].rearrange("o h g t -> (o h) g t")
                             ).then_inc(u_in, 16)
                sp.wait_ge(s5_kd, q + 1)
                for n in range(L):
                    sp.dma_start(TM[16 * n:16 * n + 16, :, (L - 1 - n) * 16:P],
                                 Kc[:, :, 0:(n + 1) * 16]).then_inc(t_in, 16)
                sp.wait_ge(s5_gelu, q * 8 + 9)
                for s in range(L):
                    sp.dma_start(z_v[ds(q, 1), :, :, s * NB:(s + 1) * NB].rearrange("o h g t -> (o h) g t"),
                                 zblk[16 * s:16 * s + 16, :, NS:BW]).then_inc(z_out, 16)
                sp.dma_start(z_v[ds(q, 1), :, :, SEQ:T].rearrange("o h g t -> (o h) g t"),
                             zblk[0:16, :, 0:NS]).then_inc(z_out, 16)
            sp.wait_ge(z_out, PARTS * 9 * 16 + 1)
            sp.dma_start(Z[:], d["z"].rearrange("(k p) t -> p k t", p=P)).then_inc(z_in, 16)
            sp.wait_ge(s5_h, PARTS + 1)
            sp.dma_start(d["ssm_p"], fin[:]).then_inc(ssm_out, 16)
            sp.dma_start(d["ssm_s"], hs[:]).then_inc(ssm_out, 16)

            def load_units(first, last):
                with sp.Fori(0, (last - first) // 4) as b:
                    for r in range(4):
                        sp.wait_ge(w_split, b * 4 + (first + r - 3))
                        sp.dma_start(w_raw[:, r, :],
                                     d["w"][ds(b * 4 + (first + r), 1)].rearrange("o p n -> (o p) n")
                                     ).then_inc(w_in[r], 16)

            load_units(4, SEG1)

            for x in range(3):
                sp.wait_ge(kv_out[x], n_out[x])
            sp.wait_ge(rope_out, 64)
            sp.wait_ge(kv_evicted, 9 * KT)
            k_v = d["kt"].rearrange("m (h c j) t -> h c m j t", h=NH, c=2)
            q_v = d["qt"].rearrange("m (h c j) t -> h c m j t", h=NH, c=2)

            def load_head(h, par):
                for c in range(2):
                    for dst, src in ((kh, k_v), (qh, q_v)):
                        sp.dma_start(dst[64 * c:64 * c + 64, par, :],
                                     src[ds(h, 1), c, :, :, 0:SEQ].rearrange("o m j t -> (o m) j t")
                                     ).then_inc(hd_in[par], 16)
                sp.dma_start(vT[:, par, :], d["vt"][ds(h, 1), :, 0:SEQ].rearrange("o e t -> (o e) t")
                             ).then_inc(hd_in[par], 16)

            def load_keys(b, par):
                sp.wait_ge(d_red, b * 2 + 1)
                sp.dma_start(qb[:, par, :], d["qrow"][ds(b, 1), :].to_broadcast([P, DM])
                             ).then_inc(kpg_in[0], 16)
                for j in range(NPG):
                    page = sp.value_load(ptab[0:1, ds(b * 2 + j, 1)], min_val=0, max_val=d["n_pages"] - 1)
                    sp.dma_start(kpg[:, j, :], d["cache_k"][ds(page, 1)].rearrange("o p n -> (o p) n")
                                 ).then_inc(kpg_in[j], 16)

            for par in range(2):
                load_head(par, par)
            sp.wait_ge(d_qrow, 1)
            sp.dma_start(d["qrow"], qrow[:].rearrange("b c m j -> b (c m j)")).then_inc(d_qout, 16)
            sp.wait_ge(d_qout, 16)
            with sp.Fori(0, NH // 2 - 1) as hh:
                for par in range(2):
                    load_keys(hh * 2 + par, par)
                    sp.wait_ge(a_o, hh * 16 + (8 * par + 8))
                    load_head(hh * 2 + (par + 2), par)
            for par in range(2):
                load_keys(NS - 2 + par, par)

            sp.wait_ge(d_red, 2 * NS + 1)

            def load_values(b, par):
                for j in range(NPG):
                    page = sp.value_load(ptab[0:1, ds(b * 2 + j, 1)], min_val=0, max_val=d["n_pages"] - 1)
                    sp.dma_start(vpg[:, 2 * par + j, :], d["cache_v"][ds(page, 1)].rearrange("o p n -> (o p) n")
                                 ).then_inc(vpg_in[2 * par + j], 16)

            for par in range(2):
                load_values(par, par)
            with sp.Fori(1, NS // 2) as bb:
                for par in range(2):
                    sp.wait_ge(d_o, bb * 2 + (par - 1))
                    load_values(bb * 2 + par, par)
            load_units(SEG1, N_UNITS)
            for n in range(NC):
                sp.wait_ge(y_done, 8 * n + 8)
                sp.dma_start(d["y_t"].rearrange("(k p) t -> p k t", p=P)[:, :, cs(n)], Y[:, :, cs(n)]
                             ).then_inc(y_out, 16)
            sp.wait_ge(y_out, 16 * NC)
            sp.wait_ge(ssm_out, 32)

        @block.gpsimd
        def _(pool):
            g = nc.gpsimd

            def split(u, r, q, first):
                pool.wait_ge(w_in[r], q * 16 + 16)
                if not first:
                    pool.wait_ge(w_used, u - 2)
                    settle(pool)
                g.tensor_copy(w_hi[:, r, :], w_raw[:, r, :]).then_inc(w_hi_done, 1)
                pool.wait_ge(w_hi_done, u + 1)
                settle(pool)
                g.tensor_tensor(w_lo[:, r, :], w_raw[:, r, :], w_hi[:, r, :].bitcast(F32), ALU.subtract
                                ).then_inc(w_split, 1)

            def split_units(first, last):
                with pool.Fori(first // 4, last // 4) as b:
                    for r in range(4):
                        split(b * 4 + r, r, b, False)

            for r in range(4):
                split(r, r, 0, True)

            pool.wait_ge(s5_glob, 1)
            pool.wait_ge(w_split, 4)
            pool.wait_ge(u_stored, 16)
            g.memset(TM[:], 0.0).then_inc(s5_zero, 1)
            g.memset(ublk[:], 0.0).then_inc(s5_zero, 1)
            S4 = [P, PP, NI, NJ]
            G4 = [P, PP, NW, 16]
            with pool.Fori(0, PARTS) as q:
                c = Chain(pool, pool_chain, q * POOL_STEPS, settle=True)
                pr = ds(q * PP, PP)
                pool.wait_ge(s5_h, q + 1)
                settle(pool)

                def outer(dst, hi_t, lo_t):
                    return g.tensor_tensor(dst[:], bc(hi_t[:, pr, NW + NJ:NN], 3, S4),
                                           bc(lo_t[:, pr, NW:NW + NJ], 2, S4), ALU.mult)
                c.add(outer(CB, cosT, cosT))
                c.step(outer(CBt, sinT, sinT))
                c.step(g.tensor_tensor(CB[:], CB[:], CBt[:], ALU.subtract))
                c.add(outer(SB, sinT, cosT))
                c.step(outer(CBt, cosT, sinT))
                g.tensor_tensor(SB[:], SB[:], CBt[:], ALU.add).then_inc(s5_cs, 1)
                pool.wait_ge(s5_y, q * 8 + 1)
                settle(pool)

                def cpow(dst, cc, aa):
                    return g.tensor_tensor(dst[:], bc(cc, 2, G4), bc(aa[:, pr, :], 3, G4), ALU.mult)
                c.add(cpow(G_re, c_in[:, 0, pr, :], A_re))
                c.step(cpow(G_t, c_in[:, 1, pr, :], A_im))
                g.tensor_tensor(G_re[:], G_re[:], G_t[:], ALU.subtract).then_inc(s5_g, 1)
                pool.wait_ge(s5_g, q * 2 + 1)
                settle(pool)
                c.add(cpow(G_im, ncr[:, pr, :], A_im))
                c.add(cpow(G_t, c_in[:, 1, pr, :], A_re))
                c.sync()
                g.tensor_tensor(G_im[:], G_im[:], G_t[:], ALU.subtract).then_inc(s5_g, 1)
                assert c.n == POOL_STEPS
            split_units(4, SEG1)
            with pool.Fori(0, NS // 2) as bb:
                for par in range(2):
                    for j in range(NPG):
                        if j == 0:
                            pool.wait_ge(kpg_in[0], bb * 64 + (32 * par + 32))
                        else:
                            pool.wait_ge(kpg_in[1], bb * 32 + (16 * par + 16))
                        settle(pool)
                        g.tensor_tensor(kpg[:, j, :], kpg[:, j, :], qb[:, par, :], ALU.mult).then_inc(d_mul, 1)
            split_units(SEG1, N_UNITS)

        @block.scalar
        def _(act):
            a = nc.scalar

            def norm_stats(v, x_ready):
                for n in range(NC):
                    x_ready(n)
                    if v or n:
                        act.wait_ge(nm_ss, 3 * v + n)
                    for k in range(KT):
                        a.activation(sq[:, k, :], X[:, k, cs(n)], ACT.Square).then_inc(nm_sq, 1)
                for n in range(NC):
                    act.wait_ge(nm_ss, 3 * v + n + 1)
                    a.activation(std[0:TB, n, :], bank[2 * n + 1][0:TB, 0:4], ACT.Sqrt,
                                 scale=1.0 / DM, bias=eps_t[0:TB, :]).then_inc(nm_std, 1)

            def norm_row(v):
                for n in range(NC):
                    act.wait_ge(nm_bc, 3 * v + n + 1)
                    a.activation(R[:, cs(n)], bank[2 * n][:, 0:CW], ACT.Copy).then_inc(nm_r, 1)

            def act_high(w):
                for i in range(NC * KT):
                    n, k = i // KT, i % KT
                    act.wait_ge(at_tmp, 24 * w + i + 1)
                    a.activation(act_hi[:, k, cs(n)], tmp[:, i % 4, :], ACT.Copy).then_inc(at_hi, 1)

            act.sem_inc(s5_gelu, 1)

            act.wait_ge(const0_in, n_const[0])
            a.activation(sm[:, 0, :], a_in[:, 2, :], ACT.Exp).then_inc(s5_act, 1)
            act.wait_ge(s5_small, 1)
            a.activation(decay[:], decay[:], ACT.Exp).then_inc(s5_act, 1)
            act.wait_ge(s5_small, 2)
            a.activation(sinT[:], sinT[:], ACT.Sin, scale=SIN_SCALE)
            a.activation(cosT[:], cosT[:], ACT.Sin, scale=SIN_SCALE).then_inc(s5_act, 1)
            act.wait_ge(s5_small, 3)
            norm_stats(0, lambda n: act.wait_ge(x_in[n], 16))
            norm_row(0)
            act.wait_ge(w_split, 4)
            act.wait_ge(u_stored, 16)
            with act.Fori(0, PARTS) as q:
                for r in range(4):
                    act.wait_ge(s5_t, q * 4 + (r + 1))
                    a.activation(RT[:, 2 * r:2 * r + 2, :, :].rearrange("p a c n -> p (a c n)"),
                                 bank[4 + r], ACT.Copy).then_inc(s5_rt, 1)
                act.wait_ge(t_in, q * 128 + 1)
                for r in range(4):
                    act.wait_ge(s5_k, q * 4 + (r + 1))
                    a.activation(Kc[:].rearrange("p (a y) n -> p a y n", y=2)[:, 4 * (r // 2):4 * (r // 2) + 4, r % 2, :],
                                 bank[4 + r][0:16, :].rearrange("p (a n) -> p a n", a=4), ACT.Copy
                                 ).then_inc(s5_kc, 1)
                act.wait_ge(z_out, q * 144 + 1)
                for r in range(8):
                    act.wait_ge(s5_y, q * 8 + (r + 2))
                    a.activation(zblk[:].rearrange("p (a y) n -> p a y n", y=2)[:, 2 * (r // 2):2 * (r // 2) + 2, r % 2, :],
                                 bank[4 + r % 4][:, 0:2 * BW].rearrange("p (a n) -> p a n", a=2),
                                 ACT.Gelu_apprx_tanh).then_inc(s5_gelu, 1)
            act.wait_ge(z_in, 16)
            act.wait_ge(ssm_out, 32)
            for k in range(KT):
                a.activation(act_hi[:, k, 0:SEQ].rearrange("p (b s) -> p b s", s=L),
                             Z[:, k, 0:SEQ].rearrange("p (s b) -> p b s", s=L), ACT.Copy)
                a.activation(act_hi[:, k, SEQ:T], Z[:, k, SEQ:T], ACT.Copy).then_inc(z_hi, 1)
            with act.Fori(0, KT) as m:
                for n in range(NC):
                    act.wait_ge(gl_ready, m * 3 + (n + 1))
                    a.activation(gate[:, n, :], bank[2 * n + 1][:, 0:CW], ACT.Sigmoid).then_inc(gl_sig, 1)

            def ffn_gate(f, tile, base):
                t = tile % 2
                par = (tile // 2) % 2
                for n in range(NC):
                    i = base + (3 * tile + n)
                    act.wait_ge(gu_ready, i + 1)
                    a.activation(gate[:, n, :], bank[2 * n][:, 0:CW], ACT.Silu).then_inc(gu_silu, 1)
                    act.wait_ge(hid_tmp, i + 1)
                    a.activation(hid_hi[:, par, t, cs(n)], tmp[:, n, :], ACT.Copy).then_inc(hid_hi_s, 1)

            def ffn(f):
                for t in range(2):
                    ffn_gate(f, t, 66 * f)
                with act.Fori(0, (NIT - 1) // 2) as b:
                    for t in range(4):
                        ffn_gate(f, t + 2, b * 12 + 66 * f)

            norm_stats(1, lambda n: act.wait_ge(gl_done, GL0 + 3 * KT))
            norm_row(1)
            act_high(0)
            ffn(0)
            norm_stats(2, lambda n: act.wait_ge(dn_added, DN0 + 264))
            act.dma_start(cosr[:], d["c_cos"]).then_inc(rope_in, 16)
            act.dma_start(sinr[:], d["c_sin"]).then_inc(rope_in, 16)
            norm_row(2)
            act_high(1)
            seen = [0, 0, 0]
            for tt in range(3 * KT):
                if tt == 2 * KT:
                    act_high(2)
                slot, rot = slots[tt]
                if tt >= 3:
                    act.wait_ge(d_smp, tt - 2)
                    act.wait_ge(kv_out[slot], seen[slot])
                for n in range(NC):
                    act.wait_ge(kv_ready, 3 * tt + n + 1)
                    a.activation(stage[:, slot, cs(n)], bank[3 * (tt % 2) + n][:, 0:CW], ACT.Copy,
                                 scale=HD ** -0.5 if tt >= 2 * KT else 1.0).then_inc(kv_evicted, 1)
                which, m = (d["kt"], d["vt"], d["qt"])[tt // KT], tt % KT
                if not rot:
                    act.wait_ge(kv_evicted, 3 * tt + 3)
                    act.dma_start(which[m], stage[:, slot, :]).then_inc(kv_out[slot], 16)
                    seen[slot] += 16
                if m == 2 and tt // KT != 1:
                    act.wait_ge(kv_roped, 1 + tt // (2 * KT))
                    for x in range(2):
                        act.dma_start(which[x], roped[:, x, :]).then_inc(rope_out, 16)

            act.wait_ge(d_qt, 1)
            a.activation(qrow[:].rearrange("b c m j -> b m c j"),
                         pair[3][0:NS, :].rearrange("b (m c j) -> b m c j", m=8, c=HC), ACT.Copy
                         ).then_inc(d_qrow, 1)
            act.wait_ge(lam_done, 1)
            a.activation(lamt[:, 2:4], lamt[:, 0:2], ACT.Exp).then_inc(act_chain, 1)

            def v_rows(h, par):
                act.wait_ge(a_vt, h + 1)
                a.activation(vtok[:, par].rearrange("p b e -> p (b e)"), pair[2][:], ACT.Copy).then_inc(a_v, 1)

            def evict(v, c):
                act.wait_ge(a_tr, v + 1)
                if c:
                    act.wait_ge(a_o, v - 1)
                n = (c % 8 + 1) * P
                a.activation(wT[:, c % 2, 0:n], pair[2][:, 0:n], ACT.Copy).then_inc(a_wt, 1)

            def stats(v, h, c):
                if c >= 62:
                    act.wait_ge(a_oa, v)
                act.wait_ge(a_oc, v + 1)
                a.activation(junk[:], O[:, ds(h, 1), c % 8, :].rearrange("p o e -> p (o e)"), ACT.Square,
                             accum_out=oss[:, ds(v, 1)]).then_inc(a_oa, 1)

            def step(v, h, c):
                n = (c % 8 + 1) * P
                for x in range(2):
                    act.wait_ge(a_max, v * 2 + (x + 1))
                    if c >= 2:
                        act.wait_ge(a_mix, v - 1)
                    a.activation(prob[:, c % 2, x, 0:n], pair[x][:, 0:n], ACT.Exp, bias=nmx[:, c % 2, x:x + 1],
                                 accum_out=sums[:, c % 2, x:x + 1]).then_inc(a_exp, 1)
                if c >= 1:
                    evict(v - 1, c - 1)
                if c % 8 == 7 and c != 63:
                    v_rows(h + 1, (c // 8 + 1) % 2)
                if c >= 2:
                    stats(v - 2, h if c % 8 >= 2 else h - 1, c - 2)

            v_rows(0, 0)
            attention_steps(act, step)
            evict(63, 63)
            stats(62, 7, 62)
            stats(63, 7, 63)
            act.wait_ge(d_s2, 1)
            a.activation(p2[:], bank[4][:, 0:2 * P + 1], ACT.Exp, bias=dsc[:, 0:1], accum_out=dsc[:, 1:2]
                         ).then_inc(d_p2, 1)
            act.wait_ge(d_w, 1)
            a.activation(wtok[:].rearrange("p a b -> p (a b)"), bank[5][:, 0:192], ACT.Copy).then_inc(d_wc, 1)
            act.wait_ge(a_oa, 64)
            a.activation(orst[:], oss[:], ACT.Sqrt, scale=1.0 / P, bias=eps_t[:]).then_inc(on_std, 1)
            with act.Fori(0, NH // 2) as hh:
                for par in range(2):
                    act.wait_ge(on_tr, hh * 2 + (par + 1))
                    a.activation(act_hi[:, ds(hh * 2 + par, 1), 0:SEQ].rearrange("p o t -> p (o t)"), pair[par][:],
                                 ACT.Copy, scale=gsub[:]).then_inc(on_hi, 1)
            act.wait_ge(d_ssq, 1)
            a.activation(oS2[:].rearrange("p b h -> p (b h)"), bank[7][:, 0:64], ACT.Sqrt, scale=1.0 / P,
                         bias=eps_t[:]).then_inc(d_rs, 1)
            act.wait_ge(d_fin, 1)
            a.activation(act_hi[:, :, SEQ:T].rearrange("p h b -> p b h"), oS[:], ACT.Copy).then_inc(d_hi, 1)

            norm_stats(3, lambda n: act.wait_ge(op_added, OP0 + 3 * KT))
            norm_row(3)
            act_high(3)
            ffn(1)
            norm_stats(4, lambda n: act.wait_ge(dn_added, DN0 + 528))
            norm_row(4)

        @block.vector
        def _(dve):
            v_ = nc.vector

            def tt(out, a, b, op):
                return v_.tensor_tensor(out, a, b, op)

            def norm_diag(v):
                for n in range(NC):
                    dve.wait_ge(nm_std, 3 * v + n + 1)
                    c.step(v_.reciprocal(rstd[0:TB, n, :], std[0:TB, n, :]))
                    dve.wait_ge(nm_bc, 3 * v + n)
                    for j in range(4):
                        last = v_.tensor_scalar(diag[:, j, :], ident[0:TB, 0:TB], rstd[0:TB, n, j:j + 1],
                                                None, ALU.mult)
                    last.then_inc(nm_diag, 1)

            def scaled(out, k, n, g, sl=None, view=lambda x: x):
                cols = cs(n) if sl is None else sl
                return v_.scalar_tensor_tensor(out, view(X[:, k, cols]), gains[:, g, k:k + 1], view(R[:, cols]),
                                               ALU.mult, ALU.mult)

            def activations(v, w, g):
                def low(i):
                    dve.wait_ge(at_hi, 24 * w + i + 1)
                    n, k = i // KT, i % KT
                    tt(act_lo[:, k, cs(n)], tmp[:, i % 4, :], act_hi[:, k, cs(n)].bitcast(F32), ALU.subtract
                       ).then_inc(at_lo, 1)
                for i in range(NC * KT):
                    n, k = i // KT, i % KT
                    dve.wait_ge(nm_r, 3 * v + n + 1)
                    if w or i >= 4:
                        dve.wait_ge(at_lo, 24 * w + max(i - 3, 0))
                    scaled(tmp[:, i % 4, :], k, n, g).then_inc(at_tmp, 1)
                    if i >= 2:
                        low(i - 2)
                low(22)
                low(23)

            c = Chain(dve, dve_chain)
            dve.sem_inc(s5_h, 1)
            dve.sem_inc(d_red, 1)
            dve.sem_inc(gl_done, GL0)
            dve.sem_inc(dn_added, DN0)
            dve.sem_inc(op_added, OP0)
            dve.wait_ge(const0_in, n_const[0])
            v_.memset(eps_t[:], EPS)
            dve.wait_ge(s5_act, 1)
            dt, lam, ang, qq, rr, tq, th, tl, den, nr, fre, fim, t1, t2 = (sm[:, i, :] for i in range(14))
            a_re, a_im = a_in[:, 0, :], a_in[:, 1, :]
            c.add(tt(lam, dt, a_re, ALU.mult))
            c.step(tt(ang, dt, a_im, ALU.mult))
            S9, SN = [P, PAIRS, NW], [P, PAIRS, NN]
            tt(decay[:], bc(lam, 2, S9), bc(nvec[:, 0:NW], 1, S9), ALU.mult).then_inc(s5_small, 1)
            c.step(v_.tensor_scalar(qq, ang, 1.0 / TWO_PI, MAGIC, ALU.mult, ALU.add))
            c.step(v_.tensor_scalar(qq, qq, MAGIC, None, ALU.subtract))
            c.step(v_.scalar_tensor_tensor(rr, qq, -C1, ang, ALU.mult, ALU.add))
            c.step(v_.scalar_tensor_tensor(rr, qq, -C2, rr, ALU.mult, ALU.add))
            c.step(v_.scalar_tensor_tensor(rr, qq, -C3, rr, ALU.mult, ALU.add))
            c.step(v_.tensor_scalar(tq, rr, 1.0 / TWO_PI, None, ALU.mult))
            c.step(v_.tensor_scalar(th, tq, MAGIC12, MAGIC12, ALU.add, ALU.subtract))
            c.step(tt(tl, tq, th, ALU.subtract))
            c.add(tt(ph[:], bc(th, 2, SN), bc(nvec[:], 1, SN), ALU.mult))
            c.step(tt(pl[:], bc(tl, 2, SN), bc(nvec[:], 1, SN), ALU.mult))
            c.step(v_.tensor_scalar(cosT[:], ph[:], MAGIC, MAGIC, ALU.add, ALU.subtract))
            c.step(tt(ph[:], ph[:], cosT[:], ALU.subtract))
            c.step(tt(ph[:], ph[:], pl[:], ALU.add))
            c.step(v_.tensor_scalar(cosT[:], ph[:], MAGIC, MAGIC, ALU.add, ALU.subtract))
            c.add(tt(sinT[:], ph[:], cosT[:], ALU.subtract))
            c.step(v_.tensor_scalar(pl[:], ph[:], 0.25, None, ALU.add))
            c.step(v_.tensor_scalar(cosT[:], pl[:], MAGIC, MAGIC, ALU.add, ALU.subtract))
            tt(cosT[:], pl[:], cosT[:], ALU.subtract).then_inc(s5_small, 1)
            dve.wait_ge(s5_act, 3)
            c.add(tt(A_re[:], decay[:], cosT[:, :, 0:NW], ALU.mult))
            c.add(tt(A_im[:], decay[:], sinT[:, :, 0:NW], ALU.mult))
            c.add(tt(t1, a_re, a_re, ALU.mult))
            c.step(tt(t2, a_im, a_im, ALU.mult))
            c.step(tt(den, t1, t2, ALU.add))
            c.add(v_.reciprocal(den, den))
            c.step(v_.tensor_scalar(nr, A_re[:, :, 1], 1.0, None, ALU.subtract))
            c.add(tt(t1, nr, a_re, ALU.mult))
            c.step(tt(t2, A_im[:, :, 1], a_im, ALU.mult))
            c.step(tt(fre, t1, t2, ALU.add))
            c.add(tt(fre, fre, den, ALU.mult))
            c.add(tt(t1, A_im[:, :, 1], a_re, ALU.mult))
            c.step(tt(t2, nr, a_im, ALU.mult))
            c.step(tt(fim, t1, t2, ALU.subtract))
            c.step(tt(fim, fim, den, ALU.mult))
            dve.wait_ge(const_in, n_const[1])
            S8 = [P, PAIRS, NS]
            s8 = ph[:].rearrange("p a n -> p (a n)")[:, 0:PAIRS * NS].rearrange("p (a n) -> p a n", n=NS)
            a1r, a1i = bc(A_re[:, :, 1], 2, S8), bc(A_im[:, :, 1], 2, S8)
            c.add(tt(hs[:, 0], a1r, h0[:, 0], ALU.mult))
            c.step(tt(s8, a1i, h0[:, 1], ALU.mult))
            c.step(tt(hs[:, 0], hs[:, 0], s8, ALU.subtract))
            c.add(tt(hs[:, 1], a1r, h0[:, 1], ALU.mult))
            c.step(tt(s8, a1i, h0[:, 0], ALU.mult))
            c.add(tt(hs[:, 1], hs[:, 1], s8, ALU.add))
            v_.tensor_scalar(ncr[:], c_in[:, 0], -1.0, None, ALU.mult).then_inc(s5_glob, 1)
            lp = tmp[:, 0, 0:2 * HD].rearrange("p (a b) -> p a b", a=2)
            lv = lamv[:].rearrange("p (a b) n -> p a b n", a=2)
            c.step(tt(lp, lv[:, :, 0, :], lv[:, :, 1, :], ALU.mult))
            c.add(v_.tensor_scalar(gsub[:], gsub[:], 1.0 - LAM_INIT, None, ALU.mult))
            c.step(v_.reduce_sum(lamt[:, 0:2], lp, axis=AXX))
            v_.memset(dsc[:], 0.0).then_inc(lam_done, 1)
            v_.memset(rstd[:], 0.0).then_inc(s5_small, 1)

            norm_diag(0)
            for n in range(NC):
                dve.wait_ge(nm_r, n + 1)
                b0, b1 = n * CW // L, min((n + 1) * CW, SEQ) // L
                for k in range(KT):
                    last = v_.scalar_tensor_tensor(
                        U[:, k, 0:SEQ].rearrange("p (s b) -> p b s", s=L)[:, b0:b1, :],
                        X[:, k, b0 * L:b1 * L].rearrange("p (b s) -> p b s", s=L), gains[:, 0, k:k + 1],
                        R[:, b0 * L:b1 * L].rearrange("p (b s) -> p b s", s=L), ALU.mult, ALU.mult)
                    if n == NC - 1:
                        last = scaled(U[:, k, SEQ:T], k, n, 0, slice(SEQ, T))
                last.then_inc(u_done, 1)

            W4 = [P, PP, L, 16]
            dve.wait_ge(w_split, 4)
            dve.wait_ge(u_stored, 16)
            dve_base = c.n
            with dve.Fori(0, PARTS) as q:
                c = Chain(dve, dve_chain, q * DVE_STEPS + dve_base)
                pr = ds(q * PP, PP)
                B3 = [P, PP, 16]
                fr, fi = bc(fre[:, pr], 2, B3), bc(fim[:, pr], 2, B3)
                br, bi = b_in[:, 0, pr, :], b_in[:, 1, pr, :]
                c.add(tt(bbar[:, 0], fr, br, ALU.mult))
                c.step(tt(bbar[:, 2], fi, bi, ALU.mult))
                c.step(tt(bbar[:, 0], bbar[:, 0], bbar[:, 2], ALU.subtract))
                c.add(tt(bbar[:, 1], fr, bi, ALU.mult))
                c.step(tt(bbar[:, 2], fi, br, ALU.mult))
                c.step(tt(bbar[:, 1], bbar[:, 1], bbar[:, 2], ALU.add))
                ar, ai = bc(A_re[:, pr, 0:L], 3, W4), bc(A_im[:, pr, 0:L], 3, W4)
                b_r, b_i = bc(bbar[:, 0], 2, W4), bc(bbar[:, 1], 2, W4)
                c.add(tt(W_re[:], ar, b_r, ALU.mult))
                c.step(tt(W_t[:], ai, b_i, ALU.mult))
                c.step(tt(W_re[:], W_re[:], W_t[:], ALU.subtract))
                c.add(tt(W_im[:], ar, b_i, ALU.mult))
                c.step(tt(W_t[:], ai, b_r, ALU.mult))
                tt(W_im[:], W_im[:], W_t[:], ALU.add).then_inc(s5_w, 1)
                dve.wait_ge(s5_cs, q + 1)
                for m in range(2):
                    dve.wait_ge(s5_v, q * 2 + (m + 1))
                    cb = CB[:, 4 * m:4 * m + 4].rearrange("p a i j -> p (a i j)")
                    sb_ = SB[:, 4 * m:4 * m + 4].rearrange("p a i j -> p (a i j)")
                    v0, v1 = (Vp[:, x, 4 * m:4 * m + 4, :].rearrange("p a b -> p (a b)") for x in range(2))
                    w0, w1 = (tw[:, x].rearrange("p a b -> p (a b)") for x in range(2))
                    c.add(tt(v0, bank[2 * m], cb, ALU.mult))
                    c.add(tt(w0, bank[2 * m + 1], sb_, ALU.mult))
                    c.add(tt(v1, bank[2 * m + 1], cb, ALU.mult))
                    c.step(tt(w1, bank[2 * m], sb_, ALU.mult))
                    c.add(tt(v0, v0, w0, ALU.add))
                    c.step(tt(v1, v1, w1, ALU.subtract))
                for r in range(4):
                    dve.wait_ge(s5_vs, q * 4 + (r + 1))
                    for x in range(2):
                        st = hs[:, x, ds(q * PP + 2 * r, 2), :]
                        last = tt(st, st, bank[4 + r][:, 0:4 * NS].rearrange("p (a x b) -> p a x b", a=2, x=2)[:, :, x, :],
                                  ALU.add)
                    last.then_inc(s5_vsd, 1)
                for pp in range(PP):
                    for x in range(2):
                        row = Vp[:, x, pp, :]
                        c.add(v_.tensor_tensor_scan(row, decay[:, ds(q * PP + pp, 1), NW - 1:NW]
                                                    .rearrange("p a b -> p (a b)").to_broadcast([P, NB]),
                                                    row, 0.0, ALU.mult, ALU.add))
                c.sync()
                dve.wait_ge(s5_y, q * 8 + 1)
                for m in range(2):
                    cb = CB[:, 4 * m:4 * m + 4].rearrange("p a i j -> p a (i j)")
                    sb_ = SB[:, 4 * m:4 * m + 4].rearrange("p a i j -> p a (i j)")
                    g0, g1 = Vp[:, 0, 4 * m:4 * m + 4, :], Vp[:, 1, 4 * m:4 * m + 4, :]
                    h_r, h_i = (H[:, x, 4 * m:4 * m + 4, NS + 1:HW_] for x in range(2))
                    c.add(tt(h_r, g0, cb, ALU.mult))
                    c.add(tt(tw[:, 0], g1, sb_, ALU.mult))
                    c.add(tt(h_i, g0, sb_, ALU.mult))
                    c.step(tt(tw[:, 1], g1, cb, ALU.mult))
                    c.add(tt(h_r, h_r, tw[:, 0], ALU.subtract))
                    c.step(tt(h_i, h_i, tw[:, 1], ALU.add))
                for x in range(2):
                    v_.tensor_copy(H[:, x, :, 0:NS], h0[:, x, pr, :])
                    v_.memset(H[:, x, :, NS:NS + 1], 0.0)
                    last = v_.tensor_copy(fin[:, x, pr, :], H[:, x, :, HW_ - 1:HW_])
                last.then_inc(s5_h, 1)
                dve.wait_ge(s5_kc, q * 4 + 4)
                D3 = [16, GP, 16]
                c.step(tt(dI[:], bc(ident[0:16, 0:16], 1, D3), bc(d16[:, ds(q * GP, GP)], 2, D3), ALU.mult))
                tt(Kc[:, :, 0:16], Kc[:, :, 0:16], dI[:], ALU.add).then_inc(s5_kd, 1)
                assert c.n == DVE_STEPS, c.n
            c = Chain(dve, dve_chain, PARTS * DVE_STEPS + dve_base)

            for k in range(KT):
                dve.wait_ge(z_hi, k + 1)
                tt(act_lo[:, k, 0:SEQ].rearrange("p (b s) -> p b s", s=L),
                   Z[:, k, 0:SEQ].rearrange("p (s b) -> p b s", s=L),
                   act_hi[:, k, 0:SEQ].bitcast(F32).rearrange("p (b s) -> p b s", s=L), ALU.subtract)
                tt(act_lo[:, k, SEQ:T], Z[:, k, SEQ:T], act_hi[:, k, SEQ:T].bitcast(F32), ALU.subtract
                   ).then_inc(z_lo, 1)
            with dve.Fori(0, KT) as m:
                for n in range(NC):
                    dve.wait_ge(gl_sig, m * 3 + (n + 1))
                    tt(tmp[:, n, :], bank[2 * n][:, 0:CW], gate[:, n, :], ALU.mult).then_inc(gl_mul, 1)
                    dve.wait_ge(gl_mul, m * 3 + (n + 1))
                    x = X[:, ds(m, 1), cs(n)].rearrange("p o t -> p (o t)")
                    tt(x, x, tmp[:, n, :], ALU.add).then_inc(gl_done, 1)

            def hidden(tile, base):
                for n in range(NC):
                    i = base + (3 * tile + n)
                    if tile:
                        dve.wait_ge(hid_lo_s, i - 2)
                    dve.wait_ge(gu_silu, i + 1)
                    tt(tmp[:, n, :], gate[:, n, :], bank[2 * n + 1][:, 0:CW], ALU.mult).then_inc(hid_tmp, 1)
                    dve.wait_ge(hid_hi_s, i + 1)
                    h = (slice(None), (tile // 2) % 2, tile % 2, cs(n))
                    tt(hid_lo[h], tmp[:, n, :], hid_hi[h].bitcast(F32), ALU.subtract).then_inc(hid_lo_s, 1)

            def down(base):
                for q in range(24):
                    dve.wait_ge(dn_ready, base + (q + 1))
                    x = X[:, q % 8, cs(q // 8)]
                    tt(x, x, bank[(6 + q) % 8][:, 0:CW], ALU.add).then_inc(dn_added, 1)

            def ffn(f):
                hidden(0, 66 * f)
                hidden(1, 66 * f)
                with dve.Fori(0, (NIT - 1) // 2) as b:
                    for half in range(2):
                        hidden(2 + 2 * half, b * 12 + 66 * f)
                        hidden(3 + 2 * half, b * 12 + 66 * f)
                        down(b * 48 + (24 * half + 264 * f))
                down(240 + 264 * f)

            norm_diag(1)
            activations(1, 0, 2)
            ffn(0)
            norm_diag(2)
            activations(2, 1, 4)
            for tt_ in range(3 * KT):
                if tt_ == 2 * KT:
                    dve.wait_ge(kv_ready, 6 * KT)
                    activations(2, 2, 1)
                dve.wait_ge(kv_evicted, 3 * tt_ + 3)
                m, keep = tt_ % KT, (kS, vS, qS)[tt_ // KT]
                slot = slots[tt_][0]
                if slots[tt_][1]:
                    if m == 0:
                        continue
                    x1, x2 = stage[:, slots[tt_ - 1][0], :], stage[:, slot, :]
                    dve.wait_ge(rope_in, 32)
                    dve.wait_ge(rope_out, 32 * (tt_ // (2 * KT)))
                    c.add(tt(roped[:, 0, :], x1, cosr[:], ALU.mult))
                    c.step(tt(rtmp[:], x2, sinr[:], ALU.mult))
                    c.step(tt(roped[:, 0, :], roped[:, 0, :], rtmp[:], ALU.subtract))
                    c.add(tt(roped[:, 1, :], x2, cosr[:], ALU.mult))
                    c.step(tt(rtmp[:], x1, sinr[:], ALU.mult))
                    c.step(tt(roped[:, 1, :], roped[:, 1, :], rtmp[:], ALU.add))
                    v_.tensor_copy(keep[:, 0:2, :], roped[:, :, SEQ:T]).then_inc(d_smp, 2)
                    v_.memset(dsc[:, 2:3], 0.0).then_inc(kv_roped, 1)
                else:
                    v_.tensor_copy(keep[:, m, :], stage[:, slot, SEQ:T]).then_inc(d_smp, 1)

            dve.wait_ge(act_chain, 1)
            c.step(tt(lamt[:, 4:5], lamt[:, 3:4], lamt[:, 2:3], ALU.subtract))
            c.step(v_.tensor_scalar(lamt[:, 4:5], lamt[:, 4:5], LAM_INIT, None, ALU.subtract))
            neglam = lamt[:, 4:5]

            def row_max(v, c_, x):
                dve.wait_ge(a_s, v * 2 + (x + 1))
                n = (c_ % 8 + 1) * P
                v_.tensor_reduce(nmx[:, c_ % 2, x:x + 1], pair[x][:, 0:n], axis=AXX, op=ALU.max, negate=True
                                 ).then_inc(a_max, 1)

            def out_copy(v, h, c_):
                dve.wait_ge(a_o, v + 1)
                v_.tensor_scalar(O[:, ds(h, 1), c_ % 8, :].rearrange("p o e -> p (o e)"), bank[6 + c_ % 2][:, 0:P],
                                 rinv[:, c_ % 4, 0:1], None, ALU.mult).then_inc(a_oc, 1)

            def key_sums(b):
                for j in range(NPG):
                    dve.wait_ge(d_mul, b * 2 + (j + 1))
                    v_.reduce_sum(stok[:, j, ds(b * HC, HC)], kpg[:, j, :].rearrange("p (c d) -> p c d", d=HD),
                                  axis=AXX).then_inc(d_red, 1)

            def step(v, h, c_):
                n = (c_ % 8 + 1) * P
                if c_ != 63:
                    row_max(v + 1, c_ + 1, 0)
                dve.wait_ge(a_exp, v * 2 + 2)
                v_.reciprocal(rinv[:, c_ % 4, :], sums[:, c_ % 2, :]).then_inc(a_r, 1)
                dve.wait_ge(a_r, v * 2 + 1)
                v_.scalar_tensor_tensor(rho[:, c_ % 2, :], sums[:, c_ % 2, 0:1], neglam, rinv[:, c_ % 4, 1:2],
                                        ALU.mult, ALU.mult).then_inc(a_r, 1)
                dve.wait_ge(a_r, v * 2 + 2)
                if c_ >= 2:
                    dve.wait_ge(a_tr, v - 1)
                v_.scalar_tensor_tensor(wmix[:, c_ % 2, 0:n], prob[:, c_ % 2, 1, 0:n], rho[:, c_ % 2, :],
                                        prob[:, c_ % 2, 0, 0:n], ALU.mult, ALU.add).then_inc(a_mix, 1)
                if c_ != 63:
                    row_max(v + 1, c_ + 1, 1)
                if c_ >= 2:
                    out_copy(v - 2, h if c_ % 8 >= 2 else h - 1, c_ - 2)
                if c_ % 8 == 4:
                    key_sums(h)

            row_max(0, 0, 0)
            row_max(0, 0, 1)
            attention_steps(dve, step)
            out_copy(62, 7, 62)
            out_copy(63, 7, 63)
            dve.wait_ge(d_smp, 24)
            pr_ = tmpd[:, 0:64].rearrange("p (m b) -> p m b", m=8)
            c.step(tt(pr_, qS[:], kS[:], ALU.mult))
            c.step(v_.reduce_sum(tmpd[:, 64:72], tmpd[:, 0:64].rearrange("p (m b) -> p b m", m=8), axis=AXX))
            N3 = [P, NS, HC]
            tt(newl[:], bc(tmpd[:, 64:72], 2, N3), bc(sel[:], 1, N3), ALU.mult).then_inc(d_new, 1)
            dve.wait_ge(d_sc, 1)
            v_.tensor_reduce(dsc[:, 0:1], bank[4][:, 0:2 * P + 1], axis=AXX, op=ALU.max, negate=True).then_inc(d_s2, 1)
            dve.wait_ge(d_p2, 1)
            c.add(v_.reciprocal(dsc[:, 3:4], dsc[:, 1:2]))
            c.step(v_.scalar_tensor_tensor(dsc[:, 4:5], evenodd[:, 1:2], neglam, evenodd[:, 0:1], ALU.mult, ALU.add))
            c.step(tt(dsc[:, 5:6], dsc[:, 3:4], dsc[:, 4:5], ALU.mult))
            c.step(v_.tensor_scalar(p2[:], p2[:], dsc[:, 5:6], None, ALU.mult))
            v_.tensor_scalar(wnew[:], ones[:], p2[:, 2 * P:2 * P + 1], None, ALU.mult).then_inc(d_p2n, 1)
            dve.wait_ge(on_std, 1)
            c.step(v_.reciprocal(orst[:], orst[:]))

            def head_low(h, par):
                dve.wait_ge(on_hi, h + 1)
                v_.scalar_tensor_tensor(act_lo[:, ds(h, 1), 0:SEQ].rearrange("p o t -> p (o t)"), pair[par][:],
                                        gsub[:], act_hi[:, ds(h, 1), 0:SEQ].bitcast(F32).rearrange("p o t -> p (o t)"),
                                        ALU.mult, ALU.subtract).then_inc(on_lo, 1)

            with dve.Fori(0, NH // 2) as hh:
                for par in range(2):
                    for i in range(KT):
                        o = O[:, ds(hh * 2 + par, 1), i, :].rearrange("p o e -> p (o e)")
                        last = v_.tensor_scalar(o, o, orst[:, ds(hh * 16 + (8 * par + i), 1)], None, ALU.mult)
                    last.then_inc(on_w, 1)
                    head_low(hh * 2 + par, par)
            dve.wait_ge(d_wc, 1)
            c.step(tt(oS[:], vS[:].rearrange("p h b -> p b h"),
                      wtok[:, 2, :].rearrange("p (b h) -> p b h", b=NS), ALU.mult))
            dve.wait_ge(d_o, NS)
            c.step(tt(oS[:], oS[:], bank[6][:, 0:64].rearrange("p (b h) -> p b h", b=NS), ALU.add))
            tt(oS2[:], oS[:], oS[:], ALU.mult).then_inc(d_sq, 1)
            dve.wait_ge(d_rs, 1)
            c.step(v_.reciprocal(oS2[:], oS2[:]))
            c.step(tt(oS[:], oS[:], oS2[:], ALU.mult))
            v_.tensor_scalar(oS[:], oS[:], gsub[:], None, ALU.mult).then_inc(d_fin, 1)
            dve.wait_ge(d_hi, 1)
            tt(act_lo[:, :, SEQ:T].rearrange("p h b -> p b h"), oS[:],
               act_hi[:, :, SEQ:T].bitcast(F32).rearrange("p h b -> p b h"), ALU.subtract).then_inc(d_lo, 1)
            with dve.Fori(0, KT // 2) as mm:
                for half in range(2):
                    for n in range(NC):
                        dve.wait_ge(op_ready, mm * 6 + (3 * half + n + 1))
                        x = X[:, ds(mm * 2 + half, 1), cs(n)].rearrange("p o t -> p (o t)")
                        tt(x, x, bank[3 * half + n][:, 0:CW], ALU.add).then_inc(op_added, 1)
            norm_diag(3)
            activations(3, 3, 3)
            ffn(1)
            norm_diag(4)
            for i in range(NC * KT):
                n, k = i // KT, i % KT
                dve.wait_ge(nm_r, 3 * 4 + n + 1)
                scaled(Y[:, k, cs(n)], k, n, 5).then_inc(y_done, 1)

        @block.tensor
        def _(pe):
            t_ = nc.tensor

            def mm(out, lhsT, rhs, start, stop):
                return t_.matmul(out, lhsT, rhs, start=start, stop=stop)

            def norm(v):
                def sums_(n):
                    pe.wait_ge(nm_sq, 24 * v + 8 * n + 8)
                    for j in range(4):
                        for k in range(KT):
                            last = mm(bank[2 * n + 1][0:TB, j:j + 1], sq[:, k, j * TB:(j + 1) * TB],
                                      ones[:, 0:1], k == 0, k == KT - 1)
                    last.then_inc(nm_ss, 1)

                def spread(n):
                    pe.wait_ge(nm_diag, 3 * v + n + 1)
                    for j in range(4):
                        last = mm(bank[2 * n][:, j * TB:(j + 1) * TB], ones[0:TB, :], diag[:, j, :], True, True)
                    last.then_inc(nm_bc, 1)

                sums_(0)
                sums_(1)
                spread(0)
                sums_(2)
                spread(1)
                spread(2)

            def dense(out, slot, n, rhs_hi, rhs_lo, first=False):
                for k in range(KT):
                    wh, wl = (w[:, slot, k * P:(k + 1) * P] for w in (w_hi, w_lo))
                    ah, al = rhs_hi[:, k, cs(n)], rhs_lo[:, k, cs(n)]
                    ins = mm(out, wh, ah, k == 0, False)
                    if first and k == 0:
                        ins.then_inc(w_used, 1)
                    mm(out, wh, al, False, False)
                    last = mm(out, wl, ah, False, k == KT - 1)
                return last

            def gate_pair(n, slot_a, slot_b, rhs_hi, rhs_lo):
                last = dense(bank[2 * n][:, 0:CW], slot_a, n, rhs_hi, rhs_lo, n == 0)
                if n == NC - 1:
                    last.then_inc(w_used, 1)
                return dense(bank[2 * n + 1][:, 0:CW], slot_b, n, rhs_hi, rhs_lo)

            pe.sem_inc(s5_y, 1)
            pe.wait_ge(const0_in, n_const[0])
            pe.wait_ge(const_in, n_const[1])
            norm(0)
            with pe.Fori(0, PARTS) as q:
                pe.wait_ge(s5_w, q + 1)
                pe.wait_ge(s5_gelu, q * 8 + 1)
                for r in range(4):
                    for x in range(4):
                        src = (W_re, W_im)[x % 2][:, 2 * r + x // 2].rearrange("p n h -> p (n h)")
                        last = t_.transpose(bank[4 + r][:, x * P:(x + 1) * P], src, ident[:])
                    last.then_inc(s5_t, 1)
                pe.wait_ge(u_in, q * 160 + 160)
                pe.wait_ge(s5_rt, q * 4 + 4)
                for m in range(2):
                    for pp in range(4):
                        for x in range(2):
                            for g2 in range(2):
                                pi = 4 * m + pp
                                last = mm(bank[2 * m + x][64 * g2:64 * g2 + 64, pp * NB:(pp + 1) * NB],
                                          RT[:, pi, x, 64 * g2:64 * g2 + 64], ublk[:, 2 * pi + g2, NS:BW], True, True)
                    last.then_inc(s5_v, 1)
                for r in range(4):
                    for y in range(2):
                        for x in range(2):
                            for g2 in range(2):
                                pi = 2 * r + y
                                last = mm(bank[4 + r][64 * g2:64 * g2 + 64, (2 * y + x) * NS:(2 * y + x + 1) * NS],
                                          RT[0:16, pi, x, 64 * g2:64 * g2 + 64], usp[:, 2 * pi + g2, :], True, True)
                    last.then_inc(s5_vs, 1)
                pe.wait_ge(s5_g, q * 2 + 2)
                for r in range(4):
                    pe.wait_ge(s5_vsd, q * 4 + (r + 1))
                    settle(pe)
                    for x in range(4):
                        pi, rows = 4 * (r // 2) + x, slice(64 * (r % 2), 64 * (r % 2) + 64)
                        out = bank[4 + r][0:16, x * P:(x + 1) * P]
                        mm(out, bbar[rows, 0, pi, :], G_re[rows, pi, 0:L, :].rearrange("p n h -> p (n h)"), True, False)
                        last = mm(out, bbar[rows, 1, pi, :], G_im[rows, pi, 0:L, :].rearrange("p n h -> p (n h)"),
                                  False, True)
                    last.then_inc(s5_k, 1)
                pe.wait_ge(s5_h, q + 2)
                pe.wait_ge(t_in, q * 128 + 129)
                for r in range(8):
                    if r < 4:
                        pe.wait_ge(s5_kc, q * 4 + (r + 1))
                    else:
                        pe.wait_ge(s5_gelu, q * 8 + (r - 2))
                    for x in range(2):
                        pi, g2 = 2 * (r // 2) + x, r % 2
                        rows = slice(64 * g2, 64 * g2 + 64)
                        out = bank[4 + r % 4][:, x * BW:(x + 1) * BW]
                        mm(out, G_re[rows, pi, 1:NW, :].rearrange("p n h -> p (n h)"), H[rows, 0, pi, 0:BW], True, False)
                        mm(out, G_im[rows, pi, 1:NW, :].rearrange("p n h -> p (n h)"), H[rows, 1, pi, 0:BW], False, False)
                        last = mm(out, TM[:, 2 * pi + g2, :], ublk[:, 2 * pi + g2, :], False, True)
                    last.then_inc(s5_y, 1)

            pe.wait_ge(z_lo, KT)
            with pe.Fori(0, KT // 2) as i:
                for half in range(2):
                    pe.wait_ge(w_split, i * 4 + (2 * half + 2))
                    for n in range(NC):
                        pe.wait_ge(gl_done, i * 6 + (GL0 + 3 * half - 3 + n + 1))
                        gate_pair(n, 2 * half, 2 * half + 1, act_hi, act_lo).then_inc(gl_ready, 1)

            def ffn(f, w):
                u0, hb, db = (U_FFN0, U_FFN1)[f], 66 * f, DN0 + 264 * f

                def gate_up(b, u, tile, spare):
                    pe.wait_ge(w_split, b * 12 + (u + 2))
                    for n in range(NC):
                        if tile == 0:
                            pe.wait_ge(at_lo, 24 * w + 8 * n + 8)
                        else:
                            pe.wait_ge(hid_tmp, b * 12 + (hb + 3 * tile - 3 + n + 1))
                        if spare is not None:
                            pe.wait_ge(dn_added, b * 48 + (db + spare(n)))
                        gate_pair(n, u % 4, (u + 1) % 4, act_hi, act_lo).then_inc(gu_ready, 1)

                def down(b, u, i):
                    pe.wait_ge(w_split, b * 12 + (u + 2))
                    for q in range(24):
                        n, j = q // 8, q % 8
                        if j == 0:
                            pe.wait_ge(hid_lo_s, b * 12 + (hb + 6 * i + 3 + n + 1))
                        if q >= 8:
                            pe.wait_ge(dn_added, b * 48 + (db + 24 * i + q - 7))
                        elif i == NIT - 1:
                            pe.wait_ge(dn_added, db + 24 * (i - 1) + 17 + q)
                        elif q >= 2:
                            pe.wait_ge(hid_tmp, b * 12 + (hb + 3 * (2 * i + 3) + (q - 2) // 2 + 1))
                        out = bank[(6 + q) % 8][:, 0:CW]
                        for t in range(2):
                            wh, wl = (x[:, (u + t) % 4, j * P:(j + 1) * P] for x in (w_hi, w_lo))
                            hh, hl = (x[:, i % 2, t, cs(n)] for x in (hid_hi, hid_lo))
                            ins = mm(out, wh, hh, t == 0, False)
                            if q == 0 and t == 0:
                                ins.then_inc(w_used, 1)
                            mm(out, wh, hl, False, False)
                            last = mm(out, wl, hh, False, t == 1)
                            if q == 23 and t == 0:
                                last.then_inc(w_used, 1)
                        last.then_inc(dn_ready, 1)

                for t in range(2):
                    gate_up(0, u0 + 2 * t, t, None)
                with pe.Fori(0, (NIT - 1) // 2) as b:
                    for half in range(2):
                        u = u0 + 4 + 6 * half
                        for t in range(2):
                            spare = lambda n: 24 * half - 4 + 2 * n
                            gate_up(b, u + 2 * t, 2 + 2 * half + t, spare if t == 0 else None)
                        down(b, u + 4, half)
                down(0, u0 + 4 + 60, NIT - 1)

            norm(1)
            ffn(0, 0)

            norm(2)

            def projection(b, x, w):
                pe.wait_ge(w_split, b * 4 + (U_KVQ + x + 1))
                for n in range(NC):
                    if w:
                        pe.wait_ge(at_lo, 24 * w + 8 * n + 8)
                    pe.wait_ge(kv_evicted, b * 12 + max(3 * (x - 2) + n + 1, 0))
                    dense(bank[3 * (x % 2) + n][:, 0:CW], (U_KVQ + x) % 4, n, act_hi, act_lo,
                          n == 0).then_inc(kv_ready, 1)

            for x in range(4):
                projection(0, x, 1 if x == 0 else 0)
            with pe.Fori(0, 3) as b:
                for x in range(4, 8):
                    projection(b, x, 0)
            for x in range(16, 20):
                projection(0, x, 2 if x == 16 else 0)
            for x in range(20, 24):
                projection(0, x, 0)
            pe.wait_ge(d_smp, 3 * KT)
            for m in range(KT):
                last = t_.transpose(pair[3][0:NS, m * P:(m + 1) * P], qS[:, m, :], ident[:])
            last.then_inc(d_qt, 1)

            def values(v, h, c):
                par = (c // 8) % 2
                pe.wait_ge(hd_in[par], v * 5 + (80 * (c // 16 + 1) - 5 * c))
                for kb in range(KT):
                    last = t_.transpose(pair[2][:, kb * P:(kb + 1) * P], vT[:, par, kb * P:(kb + 1) * P], ident[:])
                last.then_inc(a_vt, 1)

            def scores(v, c, x):
                i, par, rows = c % 8, (c // 8) % 2, slice(64 * x, 64 * x + 64)
                if c:
                    pe.wait_ge(a_exp, v * 2 + (x - 1))
                q = qh[rows, par, i * P:(i + 1) * P]
                n = (i + 1) * P
                for at in range(0, n, 512):
                    end = min(at + 512, n)
                    last = mm(pair[x][:, at:end], q, kh[rows, par, at:end], True, end < n)
                last = mm(pair[x][:, n - P:n], identb[:], maskb[:], False, True)
                last.then_inc(a_s, 1)

            def outputs(v, h, c):
                pe.wait_ge(a_wt, v + 1)
                pe.wait_ge(a_v, h + 1)
                if c >= 2:
                    pe.wait_ge(a_oc, v - 1)
                for kb in range(c % 8 + 1):
                    last = mm(bank[6 + c % 2][:, 0:P], wT[:, c % 2, kb * P:(kb + 1) * P],
                              vtok[:, (c // 8) % 2, kb, :], kb == 0, kb == c % 8)
                last.then_inc(a_o, 1)

            def step(v, h, c):
                if c % 8 == 7 and c != 63:
                    pe.wait_ge(a_wt, v)
                    values(v + 1, h + 1, c + 1)
                if c != 63:
                    scores(v + 1, c + 1, 0)
                    scores(v + 1, c + 1, 1)
                if c >= 1:
                    outputs(v - 1, h if c % 8 else h - 1, c - 1)
                pe.wait_ge(a_mix, v + 1)
                pe.wait_ge(a_wt, v)
                pe.wait_ge(a_v, h + 2 if c % 8 == 7 and c != 63 else h + 1)
                for kb in range(c % 8 + 1):
                    last = t_.transpose(pair[2][:, kb * P:(kb + 1) * P], wmix[:, c % 2, kb * P:(kb + 1) * P],
                                        ident[:])
                last.then_inc(a_tr, 1)

            pe.wait_ge(kv_evicted, 9 * KT)
            values(0, 0, 0)
            scores(0, 0, 0)
            scores(0, 0, 1)
            pe.wait_ge(d_qrow, 1)
            attention_steps(pe, step)
            outputs(63, 7, 63)

            pe.wait_ge(d_red, 2 * NS + 1)
            pe.wait_ge(d_new, 1)
            for j in range(NPG):
                t_.transpose(bank[4][:, j * P:(j + 1) * P], stok[:, j, :], ident[:])
            mm(bank[4][:, 2 * P:2 * P + 1], newl[:].rearrange("p b c -> p (b c)"), ones[:, 0:1], True, True
               ).then_inc(d_sc, 1)
            pe.wait_ge(d_p2n, 1)
            for j in range(NPG):
                mm(bank[5][:, j * 64:(j + 1) * 64], p2[:, j * P:(j + 1) * P], pairsel[:], True, True)
            mm(bank[5][:, 128:192], wnew[:], pairsel[:], True, True).then_inc(d_w, 1)
            for h in range(NH):
                pe.wait_ge(on_w, h + 1)
                if h >= 2:
                    pe.wait_ge(on_lo, h - 1)
                for i in range(KT):
                    last = t_.transpose(pair[h % 2][:, i * P:(i + 1) * P], O[:, h, i, :], ident[:])
                last.then_inc(on_tr, 1)
            pe.wait_ge(d_wc, 1)
            pe.wait_ge(a_oc, 64)
            with pe.Fori(0, NS // 2) as bb:
                for par in range(2):
                    for j in range(NPG):
                        pe.wait_ge(vpg_in[2 * par + j], bb * 16 + 16)
                    for h in range(NH):
                        for j in range(NPG):
                            col = ds(bb * 16 + (8 * par + h), 1)
                            last = mm(bank[6][:, col], vpg[:, 2 * par + j, h * P:(h + 1) * P], wtok[:, j, col],
                                      j == 0, j == NPG - 1)
                    last.then_inc(d_o, 1)
            pe.wait_ge(d_sq, 1)
            mm(bank[7][:, 0:64], ones[:], oS2[:].rearrange("p b h -> p (b h)"), True, True).then_inc(d_ssq, 1)

            pe.wait_ge(on_lo, NH)
            pe.wait_ge(d_lo, 1)
            with pe.Fori(0, KT // 4) as i:
                for x in range(4):
                    pe.wait_ge(w_split, i * 4 + (U_O + x + 1))
                    for n in range(NC):
                        pe.wait_ge(op_added, i * 12 + (OP0 + 3 * (x - 2) + n + 1))
                        dense(bank[3 * (x % 2) + n][:, 0:CW], (U_O + x) % 4, n, act_hi, act_lo,
                              n == 0).then_inc(op_ready, 1)
            norm(3)
            ffn(1, 3)
            norm(4)


def constants():
    f = np.float32
    nvec = np.concatenate([np.arange(NW), L * np.arange(NJ), L * NJ * np.arange(NI)]).astype(f)
    p = np.arange(P)
    inv = (f(500000.0) ** (-np.arange(0, ROT, 2, dtype=f) / f(ROT))).astype(f)
    pos = np.concatenate([np.arange(SEQ), np.full(NS, NPG * PAGE)]).astype(f)
    ang = (pos[None, :] * inv[:, None]).astype(f).astype(np.float64)
    rows = p % 8
    return {
        "c_nvec": np.tile(nvec, (P, 1)),
        "c_ones": np.ones((P, P), f),
        "c_ident": np.eye(P, dtype=f),
        "c_identb": np.eye(P, dtype=f).astype(mybir.dt.np(BF16)),
        "c_maskb": np.where(p[None, :] > p[:, None], f(-1e30), f(0)).astype(mybir.dt.np(BF16)),
        "c_sel": (p[:, None] // 8 == np.arange(HC)[None, :]).astype(f),
        "c_pairsel": (((p // HC) * NH + (p % HC) // 2)[:, None] == np.arange(64)[None, :]).astype(f),
        "c_evenodd": np.stack([p % 2 == 0, p % 2 == 1], 1).astype(f),
        "c_cos": np.cos(ang).astype(f)[rows],
        "c_sin": np.sin(ang).astype(f)[rows],
    }


def weight_stream(glu_a, glu_b, w_k, w_v, w_q, w_o, gate, up, down):
    def tiles(w):
        return w.reshape(KT, P, -1, P).transpose(2, 1, 0, 3).reshape(-1, P, DM)

    def by_rotation(w):
        return w.reshape(DM, HC, 8, 8).transpose(0, 2, 1, 3).reshape(DM, DM)

    def ffn(i):
        g, u, dn = tiles(gate[i]), tiles(up[i]), down[i].reshape(FT, P, DM)
        out = [g[0], u[0], g[1], u[1]]
        for it in range(NIT):
            if it + 1 < NIT:
                t = 2 * it + 2
                out += [g[t], u[t], g[t + 1], u[t + 1]]
            out += [dn[2 * it], dn[2 * it + 1]]
        return out

    a, b = tiles(glu_a), tiles(glu_b)
    units = [x for m in range(KT) for x in (a[m], b[m])] + ffn(0)
    units += list(tiles(by_rotation(w_k))) + list(tiles(w_v)) + list(tiles(by_rotation(w_q)))
    units += list(tiles(w_o)) + ffn(1)
    return np.stack(units)


def kernel(x_prompt, x_sample, cache_k, cache_v, state_ssm_re, state_ssm_im, page_table,
           mix_norm, ffn_norm, kv_norm, final_norm,
           ssm_a_re, ssm_a_im, ssm_log_dt, ssm_b_re, ssm_b_im, ssm_c_re, ssm_c_im, ssm_d,
           glu_w_a, glu_w_b, w_q, w_k, w_v, lambda_q1, lambda_k1, lambda_q2, lambda_k2,
           subln, w_o, ffn_w_gate, ffn_w_up, ffn_w_down):
    import concourse.bacc as bacc
    from concourse.bass_utils import run_bass_kernel_spmd

    def np_(x):
        return np.asarray(x)

    def by_state(x):
        x = x.reshape((PAIRS, P) + x.shape[2:])
        return np.moveaxis(x, 1, 0)

    are, aim, ldt = np_(ssm_a_re)[0], np_(ssm_a_im)[0], np_(ssm_log_dt)[0]
    arrays = {
        "x_t": np.concatenate([np_(x_prompt)[0].T, np_(x_sample)[:, 0].T], axis=1),
        "gains": np.stack([np_(mix_norm)[0], np_(mix_norm)[1], np_(ffn_norm)[0], np_(ffn_norm)[1],
                           np_(kv_norm), np_(final_norm)]).reshape(6, KT, P).transpose(2, 0, 1),
        "s_abc": np.stack([by_state(are), by_state(aim),
                           by_state(np.broadcast_to(ldt[:, None], (NG, ST)))], axis=1),
        "s_b": np.stack([by_state(np_(ssm_b_re)[0]), by_state(np_(ssm_b_im)[0])], axis=1),
        "s_c": np.stack([by_state(np_(x)[0].transpose(0, 2, 1)) for x in (ssm_c_re, ssm_c_im)], axis=1),
        "s_h0": np.stack([by_state(np_(x)[0].transpose(1, 2, 0)) for x in (state_ssm_re, state_ssm_im)], axis=1),
        "s_d": np_(ssm_d)[0].reshape(NG, 16).T,
        "lam": np.concatenate([np_(lambda_q1), np_(lambda_k1), np_(lambda_q2), np_(lambda_k2)]),
        "subln": np_(subln)[0][:, None],
        "page_table": np_(page_table).reshape(1, NS * NPG),
        "cache_k": np_(cache_k).reshape(-1, PAGE, DM),
        "cache_v": np_(cache_v).reshape(-1, PAGE, DM),
        "w": weight_stream(np_(glu_w_a)[0], np_(glu_w_b)[0], np_(w_k), np_(w_v), np_(w_q)[0], np_(w_o)[0],
                           np_(ffn_w_gate), np_(ffn_w_up), np_(ffn_w_down)),
    }
    arrays.update(constants())
    outs = {"kt": (KT, P, T), "vt": (KT, P, T), "y_t": (DM, T), "ssm_p": (P, 2, PAIRS, 1),
            "ssm_s": (P, 2, PAIRS, NS)}
    scratch = {"u": (DM, T), "z": (DM, T), "qt": (KT, P, T), "qrow": (NS, DM)}

    nc = bacc.Bacc("TRN2", target_bir_lowering=False, num_devices=1)
    d = {"n_pages": arrays["cache_k"].shape[0]}
    feed = {}
    for name, a in arrays.items():
        feed[name] = np.ascontiguousarray(a)
        d[name] = nc.dram_tensor(name, a.shape, mybir.dt.from_np(a.dtype), kind="ExternalInput").ap()
    for name, shape in outs.items():
        d[name] = nc.dram_tensor(name, shape, F32, kind="ExternalOutput").ap()
    for name, shape in scratch.items():
        d[name] = nc.dram_tensor(name, shape, F32, kind="Internal").ap()
    build(nc, d)
    r = run_bass_kernel_spmd(nc, [feed], core_ids=[0]).results[0]

    k = r["kt"].reshape(KT, NH, 2, 8, T).transpose(4, 1, 2, 0, 3).reshape(T, NH, 2, HD)
    v = r["vt"].transpose(2, 0, 1)
    y = r["y_t"].T

    def states(x, n):
        return x.reshape(P, PAIRS, n).transpose(2, 1, 0).reshape(1, n, NG, ST)

    sp_, ss = r["ssm_p"], r["ssm_s"]
    return (y[None, :SEQ], y[SEQ:, None], k[None, :SEQ], v[None, :SEQ], states(sp_[:, 0], 1), states(sp_[:, 1], 1),
            k[SEQ:, None], v[SEQ:, None], states(ss[:, 0], NS), states(ss[:, 1], NS))
```

```python
import math
from contextlib import ExitStack

import numpy as np
import concourse.bass as bass
from concourse import mybir

F32 = mybir.dt.float32
F32R = mybir.dt.float32r
BF16 = mybir.dt.bfloat16
I32 = mybir.dt.int32
ALU = mybir.AluOpType
ACT = mybir.ActivationFunctionType
AXX = mybir.AxisListType.X
ds = bass.ds

P = 128
DM = 1024
KT = DM // P
SEQ = 1024
NS = 8
T = SEQ + NS
NC = 3
CW = T // NC
TB = CW // 4
DFF = 2816
FT = DFF // P
NIT = FT // 2
NH = 8
HC = 16
HD = 64
ROT = 16
EPS = 1e-5
PAGE = 128
NPG = 2
NG = 64
ST = 64
L = 8
NB = SEQ // L
PAIRS = NG // 2
PARTS = 4
PP = PAIRS // PARTS
GP = NG // PARTS
NW = 9
NJ, NI = 16, 8
NN = NW + NJ + NI
BW = NS + NB
HW_ = NS + 1 + NB
LAM_INIT = 0.8 - 0.6 * math.exp(-0.3)
TWO_PI = 2.0 * math.pi
MAGIC = 12582912.0
MAGIC12 = 3072.0
C1 = 6.28125
C2 = round((TWO_PI - C1) * 2.0**20) / 2.0**20
C3 = TWO_PI - C1 - C2
SIN_SCALE = 6.283185
N_UNITS = 2 * KT + 2 * (3 * FT) + 3 * KT + KT
SEG1 = 108
U_GLU, U_FFN0 = 0, 2 * KT
U_KVQ = U_FFN0 + 3 * FT
U_O = U_KVQ + 3 * KT
U_FFN1 = U_O + KT
GL0, DN0, OP0 = 3, 8, 6
POOL_STEPS, DVE_STEPS = 9, 52


def build(nc, d):
    ctx = ExitStack()
    with ctx:
        top = [((nc.sbuf_base + 31) // 32) * 32]

        def place(name, shape, dt, at=None):
            size = int(np.prod(shape[1:])) * (2 if dt == BF16 else 4)
            size = (size + 31) // 32 * 32
            if at is None:
                at = top[0]
                top[0] += size
                return nc.alloc_sbuf_tensor_at(name, shape, dt, offset=at)
            off = at[0]
            at[0] += size
            assert at[0] <= at[1], (name, at)
            return nc.alloc_sbuf_tensor_at(name, shape, dt, offset=off)

        def sem(name):
            return ctx.enter_context(nc.semaphore(name))

        X = place("X", [P, KT, T], F32)
        RAW_AT = top[0]
        w_raw = place("w_raw", [P, 4, DM], F32)
        w_hi = place("w_hi", [P, 4, DM], F32R)
        w_lo = place("w_lo", [P, 4, DM], F32R)
        ident = place("ident", [P, P], F32)
        identb = place("identb", [P, P], BF16)
        maskb = place("maskb", [P, P], BF16)
        ones = place("ones", [P, P], F32)
        gains = place("gains", [P, 6, KT], F32)
        lamv = place("lamv", [P, 4, HD], F32)
        lamt = place("lamt", [P, 8], F32)
        gsub = place("gsub", [P, 1], F32)
        eps_t = place("eps_t", [P, 1], F32)
        std = place("std", [P, NC, 4], F32)
        rstd = place("rstd", [P, NC, 4], F32)
        diag = place("diag", [TB, 4, TB], F32)
        sel = place("sel", [P, HC], F32)
        pairsel = place("pairsel", [P, 64], F32)
        evenodd = place("evenodd", [P, 2], F32)
        eye8 = place("eye8", [P, 64], F32)
        ptab = place("ptab", [1, NS * NPG], I32)
        nmx = place("nmx", [P, 2, 2], F32)
        sums = place("sums", [P, 2, 2], F32)
        rinv = place("rinv", [P, 4, 2], F32)
        rho = place("rho", [P, 2, 1], F32)
        oss = place("oss", [P, 64], F32)
        orst = place("orst", [P, 64], F32)
        qS = place("qS", [P, KT, NS], F32)
        kS = place("kS", [P, KT, NS], F32)
        vS = place("vS", [P, NH, NS], F32)
        dsc = place("dsc", [P, 16], F32)
        tmpd = place("tmpd", [P, 72], F32)

        ACT_AT = top[0]
        act_hi = place("act_hi", [P, KT, T], F32R)
        act_lo = place("act_lo", [P, KT, T], F32R)
        HID_AT = top[0]
        hid_hi = place("hid_hi", [P, 2, 2, T], F32R)
        hid_lo = place("hid_lo", [P, 2, 2, T], F32R)
        MISC_AT = top[0]
        END = nc.sbuf_usable_end
        misc = [MISC_AT, END]
        sq = place("sq", [P, 3, CW], F32, misc)
        acc = place("acc", [P, NC, CW], F32, misc)
        tmp = place("tmp", [P, 4, CW], F32, misc)
        R = place("R", [P, T], F32, misc)
        gate = place("gate", [P, NC, CW], F32, misc)
        U = nc.alloc_sbuf_tensor_at("U", [P, KT, T], F32, offset=HID_AT)
        Z = nc.alloc_sbuf_tensor_at("Z", [P, KT, T], F32, offset=HID_AT)
        Y = nc.alloc_sbuf_tensor_at("Y", [P, KT, T], F32, offset=ACT_AT)
        ra = [ACT_AT, HID_AT]
        a_in = place("a_in", [P, 3, PAIRS], F32, ra)
        b_in = place("b_in", [P, 2, PAIRS, 16], F32, ra)
        c_in = place("c_in", [P, 2, PAIRS, 16], F32, ra)
        ncr = place("ncr", [P, PAIRS, 16], F32, ra)
        h0 = place("h0", [P, 2, PAIRS, NS], F32, ra)
        hs = place("hs", [P, 2, PAIRS, NS], F32, ra)
        fin = place("fin", [P, 2, PAIRS, 1], F32, ra)
        d16 = place("d16", [16, NG], F32, ra)
        dI = place("dI", [16, GP, 16], F32, ra)
        nvec = place("nvec", [P, NN], F32, ra)
        sm = place("sm", [P, 16, PAIRS], F32, ra)
        sinT = place("sinT", [P, PAIRS, NN], F32, ra)
        cosT = place("cosT", [P, PAIRS, NN], F32, ra)
        decay = place("decay", [P, PAIRS, NW], F32, ra)
        A_re = place("A_re", [P, PAIRS, NW], F32, ra)
        A_im = place("A_im", [P, PAIRS, NW], F32, ra)
        bbar = place("bbar", [P, 3, PP, 16], F32, ra)
        W_re = place("W_re", [P, PP, L, 16], F32, ra)
        W_im = place("W_im", [P, PP, L, 16], F32, ra)
        G_re = place("G_re", [P, PP, NW, 16], F32, ra)
        G_im = place("G_im", [P, PP, NW, 16], F32, ra)
        G_t = place("G_t", [P, PP, NW, 16], F32, ra)
        CB = place("CB", [P, PP, NI, NJ], F32, ra)
        SB = place("SB", [P, PP, NI, NJ], F32, ra)
        rb = [HID_AT, END]
        RT = place("RT", [P, PP, 2, P], F32, rb)
        Vp = place("Vp", [P, 2, PP, NB], F32, rb)
        tw = place("tw", [P, 2, 4, NB], F32, rb)
        H = place("H", [P, 2, PP, HW_], F32, rb)
        TM = place("TM", [P, GP, P], F32, rb)
        ublk = place("ublk", [P, GP, BW], F32, rb)
        usp = place("usp", [16, GP, NS], F32, rb)
        zblk = place("zblk", [P, GP, BW], F32, rb)
        rc = [RAW_AT, RAW_AT + 16384]
        Kc = place("Kc", [16, GP, P], F32, rc)
        CBt = place("CBt", [P, PP, NI, NJ], F32, rc)
        W_t = place("W_t", [P, PP, L, 16], F32, rc)
        rd = [HID_AT, MISC_AT]
        ph = place("ph", [P, PAIRS, NN], F32, rd)
        pl = place("pl", [P, PAIRS, NN], F32, rd)
        re_ = [HID_AT, MISC_AT]
        stage = place("stage", [P, 4, T], F32, re_)
        roped = place("roped", [P, 2, T], F32, re_)
        rtmp = gate[:].rearrange("p n t -> p (n t)")
        cosr = place("cosr", [P, T], F32, re_)
        sinr = place("sinr", [P, T], F32, re_)
        rf = [ACT_AT, HID_AT]
        kh = place("kh", [P, 2, SEQ], F32, rf)
        qz = place("qz", [P, 2, 2, SEQ], F32, rf)
        vT = nc.alloc_sbuf_tensor_at("vT", [P, 2, SEQ], F32, offset=RAW_AT)
        vtok = place("vtok", [P, 2, KT, P], F32, rf)
        prob = place("prob", [P, 2, 2, SEQ], F32, rf)
        wmix = place("wmix", [P, 2, SEQ], F32, rf)
        wT = place("wT", [P, 2, SEQ], F32, rf)
        junk = place("junk", [P, P], F32, rf)
        O = nc.alloc_sbuf_tensor_at("O", [P, NH, KT, P], F32, offset=HID_AT)
        rg = [MISC_AT, END]
        kpg = place("kpg", [P, 2, DM], F32, rg)
        qb = place("qb", [P, 2, DM], F32, rg)
        stok = place("stok", [P, NPG, NS * HC], F32, rg)
        newl = place("newl", [P, NS, HC], F32, rg)
        p2 = place("p2", [P, 2 * P + 1], F32, rg)
        wtok = place("wtok", [P, 3, 64], F32, rg)
        wnew = place("wnew", [P, P], F32, rg)
        oS = nc.alloc_sbuf_tensor_at("oS", [P, NS, NH], F32, offset=HID_AT + NH * KT * P * 4)
        assert HID_AT + (NH * KT * P + NS * NH) * 4 <= MISC_AT
        oS2 = place("oS2", [P, NS, NH], F32, rg)
        qrow = place("qrow", [NS, HC, 8, 8], F32, rg)
        orow = qrow[:].rearrange("b c m j -> b (c m j)")
        wpad = nc.alloc_sbuf_tensor_at("wpad", [P, NPG, NS, NH, NS], F32, offset=RAW_AT + 8192)
        vpg = nc.alloc_sbuf_tensor_at("vpg", [P, 4, DM], F32, offset=MISC_AT)

        pair = [ctx.enter_context(nc.psum_tensor(f"pair{i}", [P, 1024], F32)) for i in range(4)]
        bank = [pair[i // 2][:, (i % 2) * 512:(i % 2) * 512 + 512] for i in range(8)]

        const0_in, const_in = sem("const0_in"), sem("const_in")
        x_in = [sem(f"x_in{n}") for n in range(NC)]
        w_in = [sem(f"w_in{r}") for r in range(4)]
        w_split, w_used = sem("w_split"), sem("w_used")
        w_hi_done = sem("w_hi_done")
        dve_chain, pool_chain, act_chain = sem("dve_chain"), sem("pool_chain"), sem("act_chain")
        nm_sq, nm_add, nm_ss, nm_std, nm_diag = sem("nm_sq"), sem("nm_add"), sem("nm_ss"), sem("nm_std"), sem("nm_diag")
        nm_bc, nm_r = sem("nm_bc"), sem("nm_r")
        at_tmp, at_hi, at_lo = sem("at_tmp"), sem("at_hi"), sem("at_lo")
        u_done, u_stored = sem("u_done"), sem("u_stored")
        s5_act = sem("s5_act")
        s5_glob = sem("s5_glob")
        s5_small = sem("s5_small")
        s5_zero = sem("s5_zero")
        s5_w, s5_cs, s5_g = sem("s5_w"), sem("s5_cs"), sem("s5_g")
        s5_t, s5_rt, s5_k, s5_kc, s5_kd = (sem(x) for x in ("s5_t", "s5_rt", "s5_k", "s5_kc", "s5_kd"))
        s5_v, s5_vs, s5_vsd, s5_h = (sem(x) for x in ("s5_v", "s5_vs", "s5_vsd", "s5_h"))
        s5_y, s5_gelu = sem("s5_y"), sem("s5_gelu")
        u_in, t_in, z_out, z_in, ssm_out = (sem(x) for x in ("u_in", "t_in", "z_out", "z_in", "ssm_out"))
        z_hi, z_lo = sem("z_hi"), sem("z_lo")
        gl_ready, gl_sig, gl_mul, gl_done = (sem(x) for x in ("gl_ready", "gl_sig", "gl_mul", "gl_done"))
        gu_ready, gu_silu, hid_tmp, hid_hi_s, hid_lo_s = (
            sem(x) for x in ("gu_ready", "gu_silu", "hid_tmp", "hid_hi_s", "hid_lo_s"))
        dn_ready, dn_added = sem("dn_ready"), sem("dn_added")
        kv_ready, kv_evicted, kv_roped = sem("kv_ready"), sem("kv_evicted"), sem("kv_roped")
        kv_out = [sem(f"kv_out{i}") for i in range(4)]
        rope_in, rope_out = sem("rope_in"), sem("rope_out")
        lam_done = sem("lam_done")
        hd_in = [sem(f"hd_in{i}") for i in range(2)]
        a_vt, a_v, a_s, a_max, a_exp, a_mix = (sem(x) for x in ("a_vt", "a_v", "a_s", "a_max", "a_exp", "a_mix"))
        a_r, a_tr, a_wt, a_o, a_oa, a_oc = (sem(x) for x in ("a_r", "a_tr", "a_wt", "a_o", "a_oa", "a_oc"))
        on_std, on_w, on_tr, on_hi, on_lo = (sem(x) for x in ("on_std", "on_w", "on_tr", "on_hi", "on_lo"))
        d_smp, d_qt, d_qrow, d_qout = (sem(x) for x in ("d_smp", "d_qt", "d_qrow", "d_qout"))
        kpg_in = [sem(f"kpg_in{i}") for i in range(2)]
        d_mul, d_red = sem("d_mul"), sem("d_red")
        d_pv, d_new, d_s2, d_p2, d_p2n, d_w, d_wc = (
            sem(x) for x in ("d_pv", "d_new", "d_s2", "d_p2", "d_p2n", "d_w", "d_wc"))
        vpg_in = [sem(f"vpg_in{i}") for i in range(4)]
        d_o, d_sq, d_ssq, d_rs, d_fin = (sem(x) for x in ("d_o", "d_sq", "d_ssq", "d_rs", "d_fin"))
        op_ready, op_added = sem("op_ready"), sem("op_added")
        d_wp, d_row, d_ot = sem("d_wp"), sem("d_row"), sem("d_ot")
        q_zero, on_r, on_p = sem("q_zero"), sem("on_r"), sem("on_p")
        d_sc, d_hi, d_lo = sem("d_sc"), sem("d_hi"), sem("d_lo")
        passed = sem("passed")
        y_done, y_out = sem("y_done"), sem("y_out")

        block = ctx.enter_context(nc.Block())
        n_const = [0, 0]
        slots = [(tt % 4, tt in (0, 1, 2 * KT, 2 * KT + 1)) for tt in range(3 * KT)]
        n_out = [16 * sum(1 for s, r in slots if s == x and not r) for x in range(4)]

        def bc(ap, axis, shape):
            return ap.unsqueeze(axis).to_broadcast(shape)

        def cs(n):
            return slice(n * CW, (n + 1) * CW)

        def settle(eng):
            eng.sem_inc(passed, 1)

        class Chain:

            def __init__(self, eng, own, base=0, settle=False):
                self.eng, self.own, self.base, self.n, self.settle = eng, own, base, 0, settle

            def add(self, ins):
                self.n += 1
                ins.then_inc(self.own, 1)

            def sync(self):
                self.eng.wait_ge(self.own, self.base + self.n)
                if self.settle:
                    settle(self.eng)

            def step(self, ins):
                self.add(ins)
                self.sync()

        def attention_steps(eng, step):
            for c in range(2):
                step(c, 0, c)
            with eng.Fori(0, 3) as t:
                for c in range(2, 18):
                    step(t * 16 + c, t * 2 + c // 8, c)
            for c in range(50, 64):
                step(c, c // 8, c)

        @block.sync
        def _(sp):
            sp.sem_inc(t_in, 1)
            sp.sem_inc(z_out, 1)

            def const(dst, src, late=1):
                n_const[late] += 16
                sp.dma_start(dst, src).then_inc(const_in if late else const0_in, 16)

            const(a_in[:], d["s_abc"], 0)
            const(nvec[:], d["c_nvec"], 0)
            const(ones[:], d["c_ones"], 0)
            const(b_in[:], d["s_b"], 0)
            for n in range(NC):
                sp.dma_start(X[:, :, cs(n)], d["x_t"].rearrange("(k p) t -> p k t", p=P)[:, :, cs(n)]
                             ).then_inc(x_in[n], 16)
            const(ident[:], d["c_ident"])
            const(gains[:], d["gains"])
            const(c_in[:], d["s_c"])
            const(h0[:], d["s_h0"])
            const(d16[:], d["s_d"])
            const(identb[:], d["c_identb"])
            const(maskb[:], d["c_maskb"])
            for j in range(4):
                const(lamv[:, j, :], d["lam"][j:j + 1, :].to_broadcast([P, HD]))
            const(gsub[:], d["subln"])
            const(sel[:], d["c_sel"])
            const(pairsel[:], d["c_pairsel"])
            const(evenodd[:], d["c_evenodd"])
            const(eye8[:], d["c_eye8"])
            const(ptab[:], d["page_table"])
            for r in range(4):
                sp.dma_start(w_raw[:, r, :], d["w"][r]).then_inc(w_in[r], 16)

            sp.wait_ge(u_done, NC)
            sp.dma_start(d["u"].rearrange("(k p) t -> p k t", p=P), U[:]).then_inc(u_stored, 16)
            sp.wait_ge(u_stored, 16)
            sp.wait_ge(s5_zero, 2)
            u_v = d["u"].rearrange("(q g h) t -> q h g t", q=PARTS, g=GP)
            z_v = d["z"].rearrange("(q g h) t -> q h g t", q=PARTS, g=GP)
            with sp.Fori(0, PARTS) as q:
                sp.wait_ge(s5_y, q * 8 + 1)
                for n in range(L):
                    s = L - 1 - n
                    sp.dma_start(ublk[16 * n:16 * n + 16, :, NS:BW],
                                 u_v[ds(q, 1), :, :, s * NB:(s + 1) * NB].rearrange("o h g t -> (o h) g t")
                                 ).then_inc(u_in, 16)
                sp.dma_start(ublk[P - 16:P, :, 0:NS],
                             u_v[ds(q, 1), :, :, SEQ:T].rearrange("o h g t -> (o h) g t")).then_inc(u_in, 16)
                sp.dma_start(usp[:], u_v[ds(q, 1), :, :, SEQ:T].rearrange("o h g t -> (o h) g t")
                             ).then_inc(u_in, 16)
                sp.wait_ge(s5_kd, q + 1)
                for n in range(L):
                    sp.dma_start(TM[16 * n:16 * n + 16, :, (L - 1 - n) * 16:P],
                                 Kc[:, :, 0:(n + 1) * 16]).then_inc(t_in, 16)
                sp.wait_ge(s5_gelu, q * 8 + 9)
                for s in range(L):
                    sp.dma_start(z_v[ds(q, 1), :, :, s * NB:(s + 1) * NB].rearrange("o h g t -> (o h) g t"),
                                 zblk[16 * s:16 * s + 16, :, NS:BW]).then_inc(z_out, 16)
                sp.dma_start(z_v[ds(q, 1), :, :, SEQ:T].rearrange("o h g t -> (o h) g t"),
                             zblk[0:16, :, 0:NS]).then_inc(z_out, 16)
            sp.wait_ge(z_out, PARTS * 9 * 16 + 1)
            sp.dma_start(Z[:], d["z"].rearrange("(k p) t -> p k t", p=P)).then_inc(z_in, 16)
            sp.wait_ge(s5_h, PARTS + 1)
            sp.dma_start(d["ssm_p"], fin[:]).then_inc(ssm_out, 16)
            sp.dma_start(d["ssm_s"], hs[:]).then_inc(ssm_out, 16)

            def load_units(first, last):
                with sp.Fori(0, (last - first) // 4) as b:
                    for r in range(4):
                        sp.wait_ge(w_split, b * 4 + (first + r - 3))
                        sp.dma_start(w_raw[:, r, :],
                                     d["w"][ds(b * 4 + (first + r), 1)].rearrange("o p n -> (o p) n")
                                     ).then_inc(w_in[r], 16)

            load_units(4, SEG1)

            for x in range(4):
                sp.wait_ge(kv_out[x], n_out[x])
            sp.wait_ge(rope_out, 64)
            sp.wait_ge(kv_evicted, 6 * 3 * KT // 2)
            sp.wait_ge(w_split, SEG1)
            k_v = d["kt"].rearrange("m (h c j) t -> h c m j t", h=NH, c=2)
            q_v = d["qt"].rearrange("m (h c j) t -> h c m j t", h=NH, c=2)

            def load_head(h, par):
                for c in range(2):
                    rows = slice(64 * c, 64 * c + 64)
                    for dst, src in ((kh[rows, par, :], k_v), (qz[rows, par, c, :], q_v)):
                        sp.dma_start(dst,
                                     src[ds(h, 1), c, :, :, 0:SEQ].rearrange("o m j t -> (o m) j t")
                                     ).then_inc(hd_in[par], 16)
                sp.dma_start(vT[:, par, :], d["vt"][ds(h, 1), :, 0:SEQ].rearrange("o e t -> (o e) t")
                             ).then_inc(hd_in[par], 16)

            def load_keys(b, par):
                sp.wait_ge(d_red, b * 2 + 1)
                sp.dma_start(qb[:, par, :], d["qrow"][ds(b, 1), :].to_broadcast([P, DM])
                             ).then_inc(kpg_in[0], 16)
                for j in range(NPG):
                    page = sp.value_load(ptab[0:1, ds(b * 2 + j, 1)], min_val=0, max_val=d["n_pages"] - 1)
                    sp.dma_start(kpg[:, j, :], d["cache_k"][ds(page, 1)].rearrange("o p n -> (o p) n")
                                 ).then_inc(kpg_in[j], 16)

            for par in range(2):
                load_head(par, par)
            sp.wait_ge(d_qrow, 1)
            sp.dma_start(d["qrow"], qrow[:].rearrange("b c m j -> b (c m j)")).then_inc(d_qout, 16)
            sp.wait_ge(d_qout, 16)
            with sp.Fori(0, NH // 2 - 1) as hh:
                for par in range(2):
                    load_keys(hh * 2 + par, par)
                    sp.wait_ge(a_o, hh * 16 + (8 * par + 8))
                    load_head(hh * 2 + (par + 2), par)
            for par in range(2):
                load_keys(NS - 2 + par, par)

            sp.wait_ge(d_red, 2 * NS + 1)

            def load_values(b, par):
                for j in range(NPG):
                    page = sp.value_load(ptab[0:1, ds(b * 2 + j, 1)], min_val=0, max_val=d["n_pages"] - 1)
                    sp.dma_start(vpg[:, 2 * par + j, :], d["cache_v"][ds(page, 1)].rearrange("o p n -> (o p) n")
                                 ).then_inc(vpg_in[2 * par + j], 16)

            def load_unit(u):
                sp.dma_start(w_raw[:, u % 4, :], d["w"][u]).then_inc(w_in[u % 4], 16)

            for par in range(2):
                load_values(par, par)
            sp.wait_ge(a_vt, NH)
            load_unit(SEG1)
            load_unit(SEG1 + 1)
            for b in range(2, NS):
                sp.wait_ge(d_o, b - 1)
                load_values(b, b % 2)
            sp.wait_ge(d_o, NS)
            load_unit(SEG1 + 2)
            load_unit(SEG1 + 3)
            load_units(SEG1 + 4, N_UNITS)
            for n in range(NC):
                sp.wait_ge(y_done, 8 * n + 8)
                sp.dma_start(d["y_t"].rearrange("(k p) t -> p k t", p=P)[:, :, cs(n)], Y[:, :, cs(n)]
                             ).then_inc(y_out, 16)
            sp.wait_ge(y_out, 16 * NC)
            sp.wait_ge(ssm_out, 32)

        @block.gpsimd
        def _(pool):
            g = nc.gpsimd

            def split(u, r, q, first):
                pool.wait_ge(w_in[r], q * 16 + 16)
                if not first:
                    pool.wait_ge(w_used, u - 2)
                    settle(pool)
                g.tensor_copy(w_hi[:, r, :], w_raw[:, r, :]).then_inc(w_hi_done, 1)
                pool.wait_ge(w_hi_done, u + 1)
                settle(pool)
                g.tensor_tensor(w_lo[:, r, :], w_raw[:, r, :], w_hi[:, r, :].bitcast(F32), ALU.subtract
                                ).then_inc(w_split, 1)

            def split_units(first, last):
                with pool.Fori(first // 4, last // 4) as b:
                    for r in range(4):
                        split(b * 4 + r, r, b, False)

            for r in range(4):
                split(r, r, 0, True)

            pool.wait_ge(s5_glob, 1)
            pool.wait_ge(w_split, 4)
            pool.wait_ge(u_stored, 16)
            g.memset(TM[:], 0.0).then_inc(s5_zero, 1)
            g.memset(ublk[:], 0.0).then_inc(s5_zero, 1)
            S4 = [P, PP, NI, NJ]
            G4 = [P, PP, NW, 16]
            with pool.Fori(0, PARTS) as q:
                c = Chain(pool, pool_chain, q * POOL_STEPS, settle=True)
                pr = ds(q * PP, PP)
                pool.wait_ge(s5_h, q + 1)
                settle(pool)

                def outer(dst, hi_t, lo_t):
                    return g.tensor_tensor(dst[:], bc(hi_t[:, pr, NW + NJ:NN], 3, S4),
                                           bc(lo_t[:, pr, NW:NW + NJ], 2, S4), ALU.mult)
                c.add(outer(CB, cosT, cosT))
                c.step(outer(CBt, sinT, sinT))
                c.step(g.tensor_tensor(CB[:], CB[:], CBt[:], ALU.subtract))
                c.add(outer(SB, sinT, cosT))
                c.step(outer(CBt, cosT, sinT))
                g.tensor_tensor(SB[:], SB[:], CBt[:], ALU.add).then_inc(s5_cs, 1)
                pool.wait_ge(s5_y, q * 8 + 1)
                settle(pool)

                def cpow(dst, cc, aa):
                    return g.tensor_tensor(dst[:], bc(cc, 2, G4), bc(aa[:, pr, :], 3, G4), ALU.mult)
                c.add(cpow(G_re, c_in[:, 0, pr, :], A_re))
                c.step(cpow(G_t, c_in[:, 1, pr, :], A_im))
                g.tensor_tensor(G_re[:], G_re[:], G_t[:], ALU.subtract).then_inc(s5_g, 1)
                pool.wait_ge(s5_g, q * 2 + 1)
                settle(pool)
                c.add(cpow(G_im, ncr[:, pr, :], A_im))
                c.add(cpow(G_t, c_in[:, 1, pr, :], A_re))
                c.sync()
                g.tensor_tensor(G_im[:], G_im[:], G_t[:], ALU.subtract).then_inc(s5_g, 1)
                assert c.n == POOL_STEPS
            split_units(4, SEG1)
            pool.wait_ge(kv_ready, 9 * KT // 2)
            pool.wait_ge(w_split, SEG1)
            g.memset(qz[64:P, :, 0, :], 0.0).then_inc(q_zero, 1)
            pool.wait_ge(q_zero, 1)
            g.memset(qz[0:64, :, 1, :], 0.0).then_inc(q_zero, 1)
            pool.wait_ge(q_zero, 2)
            with pool.Fori(0, NS // 2) as bb:
                for par in range(2):
                    for j in range(NPG):
                        if j == 0:
                            pool.wait_ge(kpg_in[0], bb * 64 + (32 * par + 32))
                        else:
                            pool.wait_ge(kpg_in[1], bb * 32 + (16 * par + 16))
                        settle(pool)
                        g.tensor_tensor(kpg[:, j, :], kpg[:, j, :], qb[:, par, :], ALU.mult).then_inc(d_mul, 1)
            pool.wait_ge(on_r, 1)
            for h in range(6):
                g.tensor_tensor(O[:, h], O[:, h], bc(orst[:, 8 * h:8 * h + 8], 2, [P, KT, P]), ALU.mult
                                ).then_inc(on_p, 1)
            split_units(SEG1, N_UNITS)

        @block.scalar
        def _(act):
            a = nc.scalar

            def square(v, i, k, n):
                if v or i >= 3:
                    act.wait_ge(nm_add, i + (24 * v - 2))
                a.activation(sq[:, n if v == 1 else i % 3, :], X[:, k, cs(n)], ACT.Square).then_inc(nm_sq, 1)

            def root(v, n):
                act.wait_ge(nm_ss, 3 * v + n + 1)
                a.activation(std[0:TB, n, :], bank[7][0:TB, 4 * n:4 * n + 4], ACT.Sqrt,
                             scale=1.0 / DM, bias=eps_t[0:TB, :]).then_inc(nm_std, 1)

            def row(v, n):
                act.wait_ge(nm_bc, 3 * v + n + 1)
                a.activation(R[:, cs(n)], bank[6][:, 0:CW], ACT.Copy).then_inc(nm_r, 1)

            def high(w, first, last):
                for i in range(first, last):
                    n, k = i // KT, i % KT
                    act.wait_ge(at_tmp, 24 * w + i + 1)
                    a.activation(act_hi[:, k, cs(n)], tmp[:, i % 4, :], ACT.Copy).then_inc(at_hi, 1)

            def norm_after(v, w, chunk):
                chunk(0)
                root(v, 0)
                chunk(1)
                row(v, 0)
                high(w, 0, 4)
                root(v, 1)
                high(w, 4, 8)
                chunk(2)
                row(v, 1)
                high(w, 8, 16)
                root(v, 2)
                row(v, 2)
                high(w, 16, 24)

            act.sem_inc(s5_gelu, 1)

            act.wait_ge(const0_in, n_const[0])
            a.activation(sm[:, 0, :], a_in[:, 2, :], ACT.Exp).then_inc(s5_act, 1)
            act.wait_ge(s5_small, 1)
            a.activation(decay[:], decay[:], ACT.Exp).then_inc(s5_act, 1)
            act.wait_ge(s5_small, 2)
            a.activation(sinT[:], sinT[:], ACT.Sin, scale=SIN_SCALE)
            a.activation(cosT[:], cosT[:], ACT.Sin, scale=SIN_SCALE).then_inc(s5_act, 1)
            act.wait_ge(s5_small, 3)
            for n in range(NC):
                act.wait_ge(x_in[n], 16)
                for k in range(KT):
                    square(0, n * KT + k, k, n)
                root(0, n)
                if n:
                    row(0, n - 1)
            row(0, 2)
            act.wait_ge(w_split, 4)
            act.wait_ge(u_stored, 16)
            with act.Fori(0, PARTS) as q:
                for r in range(4):
                    act.wait_ge(s5_t, q * 4 + (r + 1))
                    a.activation(RT[:, 2 * r:2 * r + 2, :, :].rearrange("p a c n -> p (a c n)"),
                                 bank[4 + r], ACT.Copy).then_inc(s5_rt, 1)
                act.wait_ge(t_in, q * 128 + 1)
                for r in range(4):
                    act.wait_ge(s5_k, q * 4 + (r + 1))
                    a.activation(Kc[:].rearrange("p (a y) n -> p a y n", y=2)[:, 4 * (r // 2):4 * (r // 2) + 4, r % 2, :],
                                 bank[4 + r][0:16, :].rearrange("p (a n) -> p a n", a=4), ACT.Copy
                                 ).then_inc(s5_kc, 1)
                act.wait_ge(z_out, q * 144 + 1)
                for r in range(8):
                    act.wait_ge(s5_y, q * 8 + (r + 2))
                    a.activation(zblk[:].rearrange("p (a y) n -> p a y n", y=2)[:, 2 * (r // 2):2 * (r // 2) + 2, r % 2, :],
                                 bank[4 + r % 4][:, 0:2 * BW].rearrange("p (a n) -> p a n", a=2),
                                 ACT.Gelu_apprx_tanh).then_inc(s5_gelu, 1)
            act.wait_ge(z_in, 16)
            act.wait_ge(ssm_out, 32)
            for k in range(KT):
                a.activation(act_hi[:, k, 0:SEQ].rearrange("p (b s) -> p b s", s=L),
                             Z[:, k, 0:SEQ].rearrange("p (s b) -> p b s", s=L), ACT.Copy)
                a.activation(act_hi[:, k, SEQ:T], Z[:, k, SEQ:T], ACT.Copy).then_inc(z_hi, 1)
            def glu(m, n):
                act.wait_ge(gl_ready, m * 3 + (n + 1))
                a.activation(gate[:, n, :], bank[2 * n + 1][:, 0:CW], ACT.Sigmoid).then_inc(gl_sig, 1)
                act.wait_ge(gl_done, m * 3 + (GL0 + n + 1))
                act.wait_ge(nm_add, m * 3 + (24 + n - 2))
                settle(act)
                a.activation(sq[:, n, :], X[:, ds(m, 1), cs(n)].rearrange("p o t -> p (o t)"), ACT.Square
                             ).then_inc(nm_sq, 1)

            with act.Fori(0, KT - 1) as m:
                for n in range(NC):
                    glu(m, n)

            def ffn_gate(f, tile, base):
                t = tile % 2
                par = (tile // 2) % 2
                for n in range(NC):
                    i = base + (3 * tile + n)
                    act.wait_ge(gu_ready, i + 1)
                    a.activation(gate[:, n, :], bank[2 * n][:, 0:CW], ACT.Silu).then_inc(gu_silu, 1)
                    act.wait_ge(hid_tmp, i + 1)
                    a.activation(hid_hi[:, par, t, cs(n)], tmp[:, n, :], ACT.Copy).then_inc(hid_hi_s, 1)

            def ffn(f):
                for t in range(2):
                    ffn_gate(f, t, 66 * f)
                with act.Fori(0, (NIT - 1) // 2) as b:
                    for t in range(4):
                        ffn_gate(f, t + 2, b * 12 + 66 * f)

            def norm_after_down(f, v, w):
                for q in range(24):
                    act.wait_ge(dn_added, DN0 + 240 + 264 * f + q + 1)
                    square(v, q, q % 8, q // 8)
                    if q == 12:
                        root(v, 0)
                    if q == 15:
                        row(v, 0)
                    if q == 20:
                        root(v, 1)
                    if q >= 16 and w:
                        high(w, q - 16, q - 15)
                row(v, 1)
                if w:
                    high(w, 8, 16)
                root(v, 2)
                row(v, 2)
                if w:
                    high(w, 16, 24)

            norm_after(1, 0, lambda n: glu(KT - 1, n))
            ffn(0)
            norm_after_down(0, 2, 1)
            act.dma_start(cosr[:], d["c_cos"]).then_inc(rope_in, 16)
            act.dma_start(sinr[:], d["c_sin"]).then_inc(rope_in, 16)
            seen = [0, 0, 0, 0]
            for tt in range(3 * KT):
                if tt % 2 == 0:
                    p = tt // 2
                    if p >= 2:
                        act.wait_ge(d_smp, tt - 2)
                        for x in range(2):
                            act.wait_ge(kv_out[slots[tt + x][0]], seen[slots[tt + x][0]])
                    for n in range(NC):
                        act.wait_ge(kv_ready, 3 * p + n + 1)
                        for x in range(2):
                            a.activation(stage[:, slots[tt + x][0], cs(n)], bank[2 * n + x][:, 0:CW], ACT.Copy,
                                         scale=HD ** -0.5 if tt >= 2 * KT else 1.0).then_inc(kv_evicted, 1)
                        if p == KT - 1:
                            high(2, n * KT, n * KT + KT)
                slot, rot = slots[tt]
                which, m = (d["kt"], d["vt"], d["qt"])[tt // KT], tt % KT
                if not rot:
                    act.wait_ge(kv_evicted, 6 * (tt // 2) + 6)
                    act.dma_start(which[m], stage[:, slot, :]).then_inc(kv_out[slot], 16)
                    seen[slot] += 16
                if m == 2 and tt // KT != 1:
                    act.wait_ge(kv_roped, 1 + tt // (2 * KT))
                    for x in range(2):
                        act.dma_start(which[x], roped[:, x, :]).then_inc(rope_out, 16)

            act.wait_ge(d_qt, 1)
            a.activation(qrow[:].rearrange("b c m j -> b m c j"),
                         pair[3][0:NS, :].rearrange("b (m c j) -> b m c j", m=8, c=HC), ACT.Copy
                         ).then_inc(d_qrow, 1)
            act.wait_ge(lam_done, 1)
            a.activation(lamt[:, 2:4], lamt[:, 0:2], ACT.Exp).then_inc(act_chain, 1)

            def v_rows(h, par):
                act.wait_ge(a_vt, h + 1)
                a.activation(vtok[:, par].rearrange("p b e -> p (b e)"), pair[2][:], ACT.Copy).then_inc(a_v, 1)

            def evict(v, c):
                act.wait_ge(a_tr, v + 1)
                if c:
                    act.wait_ge(a_o, v - 1)
                n = (c % 8 + 1) * P
                a.activation(wT[:, c % 2, 0:n], pair[2][:, 0:n], ACT.Copy).then_inc(a_wt, 1)

            def stats(v, h, c):
                if c >= 62:
                    act.wait_ge(a_oa, v)
                act.wait_ge(a_oc, v + 1)
                a.activation(junk[:], O[:, ds(h, 1), c % 8, :].rearrange("p o e -> p (o e)"), ACT.Square,
                             accum_out=oss[:, ds(v, 1)]).then_inc(a_oa, 1)

            def step(v, h, c):
                n = (c % 8 + 1) * P
                for x in range(2):
                    act.wait_ge(a_max, v * 2 + (x + 1))
                    if c >= 2:
                        act.wait_ge(a_mix, v - 1)
                    a.activation(prob[:, c % 2, x, 0:n], pair[x][:, 0:n], ACT.Exp, bias=nmx[:, c % 2, x:x + 1],
                                 accum_out=sums[:, c % 2, x:x + 1]).then_inc(a_exp, 1)
                if c >= 1:
                    evict(v - 1, c - 1)
                if c % 8 == 7 and c != 63:
                    v_rows(h + 1, (c // 8 + 1) % 2)
                if c >= 2:
                    stats(v - 2, h if c % 8 >= 2 else h - 1, c - 2)
                if c == 50:
                    rms(0, 48)

            def rms(first, last):
                act.wait_ge(a_oa, last)
                a.activation(orst[:, first:last], oss[:, first:last], ACT.Sqrt, scale=1.0 / P, bias=eps_t[:]
                             ).then_inc(on_std, 1)

            v_rows(0, 0)
            attention_steps(act, step)
            evict(63, 63)
            stats(62, 7, 62)
            stats(63, 7, 63)
            act.wait_ge(d_s2, 1)
            a.activation(p2[:], bank[4][:, 0:2 * P + 1], ACT.Exp, bias=dsc[:, 0:1], accum_out=dsc[:, 1:2]
                         ).then_inc(d_p2, 1)

            def head_high(h):
                act.wait_ge(on_tr, h + 1)
                a.activation(act_hi[:, h, 0:SEQ], pair[h % 2][:], ACT.Copy, scale=gsub[:]).then_inc(on_hi, 1)

            head_high(0)
            act.wait_ge(d_w, 1)
            a.activation(wtok[:].rearrange("p a b -> p (a b)"), bank[5][:, 0:192], ACT.Copy).then_inc(d_wc, 1)
            head_high(1)
            rms(48, 64)
            for h in range(2, NH):
                head_high(h)
            act.wait_ge(d_o, NS)
            a.activation(orow, pair[2][0:NS, :], ACT.Copy).then_inc(d_row, 1)
            act.wait_ge(d_ssq, 1)
            a.activation(oS2[:].rearrange("p b h -> p (b h)"), bank[7][:, 0:64], ACT.Sqrt, scale=1.0 / P,
                         bias=eps_t[:]).then_inc(d_rs, 1)
            act.wait_ge(d_fin, 1)
            a.activation(act_hi[:, :, SEQ:T].rearrange("p h b -> p b h"), oS[:], ACT.Copy).then_inc(d_hi, 1)

            def squares_of_pair(p, n):
                for x in range(2):
                    act.wait_ge(op_added, OP0 + 6 * p + 2 * n + x + 1)
                    square(3, 6 * p + 2 * n + x, 2 * p + x, n)

            for p in range(KT // 2 - 1):
                for n in range(NC):
                    squares_of_pair(p, n)
            norm_after(3, 3, lambda n: squares_of_pair(KT // 2 - 1, n))
            ffn(1)
            norm_after_down(1, 4, 0)

        @block.vector
        def _(dve):
            v_ = nc.vector

            def tt(out, a, b, op):
                return v_.tensor_tensor(out, a, b, op)

            def add_square(v, i, n, wait=None):
                dve.wait_ge(nm_sq, i + (24 * v + 1))
                if wait is not None:
                    dve.wait_ge(nm_add, wait)
                slot = n if v == 1 else i % 3
                tt(acc[:, n, :], acc[:, n, :], sq[:, slot, :], ALU.add).then_inc(nm_add, 1)

            def clear_sums(v):
                if v:
                    dve.wait_ge(nm_ss, 3 * v)
                c.step(v_.memset(acc[:], 0.0))

            def diagonal(v, n):
                dve.wait_ge(nm_std, 3 * v + n + 1)
                c.step(v_.reciprocal(rstd[0:TB, n, :], std[0:TB, n, :]))
                if v or n:
                    dve.wait_ge(nm_bc, 3 * v + n)
                for j in range(4):
                    last = v_.tensor_scalar(diag[:, j, :], ident[0:TB, 0:TB], rstd[0:TB, n, j:j + 1],
                                            None, ALU.mult)
                last.then_inc(nm_diag, 1)

            def scaled(out, k, n, g, sl=None, view=lambda x: x):
                cols = cs(n) if sl is None else sl
                return v_.scalar_tensor_tensor(out, view(X[:, k, cols]), gains[:, g, k:k + 1], view(R[:, cols]),
                                               ALU.mult, ALU.mult)

            def normalise(v, w, g, first, last):
                def low(i):
                    dve.wait_ge(at_hi, 24 * w + i + 1)
                    n, k = i // KT, i % KT
                    tt(act_lo[:, k, cs(n)], tmp[:, i % 4, :], act_hi[:, k, cs(n)].bitcast(F32), ALU.subtract
                       ).then_inc(at_lo, 1)
                for i in range(first, last):
                    n, k = i // KT, i % KT
                    dve.wait_ge(nm_r, 3 * v + n + 1)
                    if w or i >= 4:
                        dve.wait_ge(at_lo, 24 * w + max(i - 3, 0))
                    scaled(tmp[:, i % 4, :], k, n, g).then_inc(at_tmp, 1)
                    if k >= 2:
                        low(i - 2)
                    if k == KT - 1:
                        low(i - 1)
                        low(i)

            def norm_after(v, w, g, chunk):
                chunk(0)
                diagonal(v, 0)
                chunk(1)
                normalise(v, w, g, 0, 4)
                diagonal(v, 1)
                normalise(v, w, g, 4, 8)
                chunk(2)
                normalise(v, w, g, 8, 16)
                diagonal(v, 2)
                normalise(v, w, g, 16, 24)

            def norm_after_down(f, v, normal):
                clear_sums(v)
                base, i0 = 240 + 264 * f, 24 * v

                def square(q):
                    add_square(v, q, q // 8, i0 + q if q % 8 else None)
                for q in range(24):
                    dve.wait_ge(dn_ready, base + (q + 1))
                    x = X[:, q % 8, cs(q // 8)]
                    tt(x, x, bank[q % 6][:, 0:CW], ALU.add).then_inc(dn_added, 1)
                    if q:
                        square(q - 1)
                    if q == 13:
                        diagonal(v, 0)
                    if q >= 16:
                        normal(q - 16, q - 15)
                    if q == 21:
                        diagonal(v, 1)
                square(23)
                normal(8, 16)
                diagonal(v, 2)
                normal(16, 24)

            c = Chain(dve, dve_chain)
            dve.sem_inc(s5_h, 1)
            dve.sem_inc(d_red, 1)
            dve.sem_inc(gl_done, GL0)
            dve.sem_inc(dn_added, DN0)
            dve.sem_inc(op_added, OP0)
            dve.wait_ge(const0_in, n_const[0])
            v_.memset(eps_t[:], EPS)
            dve.wait_ge(s5_act, 1)
            dt, lam, ang, qq, rr, tq, th, tl, den, nr, fre, fim, t1, t2 = (sm[:, i, :] for i in range(14))
            a_re, a_im = a_in[:, 0, :], a_in[:, 1, :]
            c.add(tt(lam, dt, a_re, ALU.mult))
            c.step(tt(ang, dt, a_im, ALU.mult))
            S9, SN = [P, PAIRS, NW], [P, PAIRS, NN]
            tt(decay[:], bc(lam, 2, S9), bc(nvec[:, 0:NW], 1, S9), ALU.mult).then_inc(s5_small, 1)
            c.step(v_.tensor_scalar(qq, ang, 1.0 / TWO_PI, MAGIC, ALU.mult, ALU.add))
            c.step(v_.tensor_scalar(qq, qq, MAGIC, None, ALU.subtract))
            c.step(v_.scalar_tensor_tensor(rr, qq, -C1, ang, ALU.mult, ALU.add))
            c.step(v_.scalar_tensor_tensor(rr, qq, -C2, rr, ALU.mult, ALU.add))
            c.step(v_.scalar_tensor_tensor(rr, qq, -C3, rr, ALU.mult, ALU.add))
            c.step(v_.tensor_scalar(tq, rr, 1.0 / TWO_PI, None, ALU.mult))
            c.step(v_.tensor_scalar(th, tq, MAGIC12, MAGIC12, ALU.add, ALU.subtract))
            c.step(tt(tl, tq, th, ALU.subtract))
            c.add(tt(ph[:], bc(th, 2, SN), bc(nvec[:], 1, SN), ALU.mult))
            c.step(tt(pl[:], bc(tl, 2, SN), bc(nvec[:], 1, SN), ALU.mult))
            c.step(v_.tensor_scalar(cosT[:], ph[:], MAGIC, MAGIC, ALU.add, ALU.subtract))
            c.step(tt(ph[:], ph[:], cosT[:], ALU.subtract))
            c.step(tt(ph[:], ph[:], pl[:], ALU.add))
            c.step(v_.tensor_scalar(cosT[:], ph[:], MAGIC, MAGIC, ALU.add, ALU.subtract))
            c.add(tt(sinT[:], ph[:], cosT[:], ALU.subtract))
            c.step(v_.tensor_scalar(pl[:], ph[:], 0.25, None, ALU.add))
            c.step(v_.tensor_scalar(cosT[:], pl[:], MAGIC, MAGIC, ALU.add, ALU.subtract))
            tt(cosT[:], pl[:], cosT[:], ALU.subtract).then_inc(s5_small, 1)
            dve.wait_ge(s5_act, 3)
            c.add(tt(A_re[:], decay[:], cosT[:, :, 0:NW], ALU.mult))
            c.add(tt(A_im[:], decay[:], sinT[:, :, 0:NW], ALU.mult))
            c.add(tt(t1, a_re, a_re, ALU.mult))
            c.step(tt(t2, a_im, a_im, ALU.mult))
            c.step(tt(den, t1, t2, ALU.add))
            c.add(v_.reciprocal(den, den))
            c.step(v_.tensor_scalar(nr, A_re[:, :, 1], 1.0, None, ALU.subtract))
            c.add(tt(t1, nr, a_re, ALU.mult))
            c.step(tt(t2, A_im[:, :, 1], a_im, ALU.mult))
            c.step(tt(fre, t1, t2, ALU.add))
            c.add(tt(fre, fre, den, ALU.mult))
            c.add(tt(t1, A_im[:, :, 1], a_re, ALU.mult))
            c.step(tt(t2, nr, a_im, ALU.mult))
            c.step(tt(fim, t1, t2, ALU.subtract))
            c.step(tt(fim, fim, den, ALU.mult))
            dve.wait_ge(const_in, n_const[1])
            S8 = [P, PAIRS, NS]
            s8 = ph[:].rearrange("p a n -> p (a n)")[:, 0:PAIRS * NS].rearrange("p (a n) -> p a n", n=NS)
            a1r, a1i = bc(A_re[:, :, 1], 2, S8), bc(A_im[:, :, 1], 2, S8)
            c.add(tt(hs[:, 0], a1r, h0[:, 0], ALU.mult))
            c.step(tt(s8, a1i, h0[:, 1], ALU.mult))
            c.step(tt(hs[:, 0], hs[:, 0], s8, ALU.subtract))
            c.add(tt(hs[:, 1], a1r, h0[:, 1], ALU.mult))
            c.step(tt(s8, a1i, h0[:, 0], ALU.mult))
            c.add(tt(hs[:, 1], hs[:, 1], s8, ALU.add))
            v_.tensor_scalar(ncr[:], c_in[:, 0], -1.0, None, ALU.mult).then_inc(s5_glob, 1)
            lp = tmp[:, 0, 0:2 * HD].rearrange("p (a b) -> p a b", a=2)
            lv = lamv[:].rearrange("p (a b) n -> p a b n", a=2)
            c.step(tt(lp, lv[:, :, 0, :], lv[:, :, 1, :], ALU.mult))
            c.add(v_.tensor_scalar(gsub[:], gsub[:], 1.0 - LAM_INIT, None, ALU.mult))
            c.step(v_.reduce_sum(lamt[:, 0:2], lp, axis=AXX))
            v_.memset(dsc[:], 0.0).then_inc(lam_done, 1)
            v_.memset(rstd[:], 0.0).then_inc(s5_small, 1)

            def inputs(n):
                dve.wait_ge(nm_r, n + 1)
                b0, b1 = n * CW // L, min((n + 1) * CW, SEQ) // L
                for k in range(KT):
                    last = v_.scalar_tensor_tensor(
                        U[:, k, 0:SEQ].rearrange("p (s b) -> p b s", s=L)[:, b0:b1, :],
                        X[:, k, b0 * L:b1 * L].rearrange("p (b s) -> p b s", s=L), gains[:, 0, k:k + 1],
                        R[:, b0 * L:b1 * L].rearrange("p (b s) -> p b s", s=L), ALU.mult, ALU.mult)
                    if n == NC - 1:
                        last = scaled(U[:, k, SEQ:T], k, n, 0, slice(SEQ, T))
                last.then_inc(u_done, 1)

            c.step(v_.memset(acc[:], 0.0))
            for n in range(NC):
                for k in range(KT):
                    add_square(0, n * KT + k, n, n * KT + k if k else None)
                diagonal(0, n)
                if n:
                    inputs(n - 1)
            inputs(2)
            W4 = [P, PP, L, 16]
            dve.wait_ge(w_split, 4)
            dve.wait_ge(u_stored, 16)
            dve_base = c.n
            with dve.Fori(0, PARTS) as q:
                c = Chain(dve, dve_chain, q * DVE_STEPS + dve_base)
                pr = ds(q * PP, PP)
                B3 = [P, PP, 16]
                fr, fi = bc(fre[:, pr], 2, B3), bc(fim[:, pr], 2, B3)
                br, bi = b_in[:, 0, pr, :], b_in[:, 1, pr, :]
                c.add(tt(bbar[:, 0], fr, br, ALU.mult))
                c.step(tt(bbar[:, 2], fi, bi, ALU.mult))
                c.step(tt(bbar[:, 0], bbar[:, 0], bbar[:, 2], ALU.subtract))
                c.add(tt(bbar[:, 1], fr, bi, ALU.mult))
                c.step(tt(bbar[:, 2], fi, br, ALU.mult))
                c.step(tt(bbar[:, 1], bbar[:, 1], bbar[:, 2], ALU.add))
                ar, ai = bc(A_re[:, pr, 0:L], 3, W4), bc(A_im[:, pr, 0:L], 3, W4)
                b_r, b_i = bc(bbar[:, 0], 2, W4), bc(bbar[:, 1], 2, W4)
                c.add(tt(W_re[:], ar, b_r, ALU.mult))
                c.step(tt(W_t[:], ai, b_i, ALU.mult))
                c.step(tt(W_re[:], W_re[:], W_t[:], ALU.subtract))
                c.add(tt(W_im[:], ar, b_i, ALU.mult))
                c.step(tt(W_t[:], ai, b_r, ALU.mult))
                tt(W_im[:], W_im[:], W_t[:], ALU.add).then_inc(s5_w, 1)
                dve.wait_ge(s5_cs, q + 1)
                for m in range(2):
                    dve.wait_ge(s5_v, q * 2 + (m + 1))
                    cb = CB[:, 4 * m:4 * m + 4].rearrange("p a i j -> p (a i j)")
                    sb_ = SB[:, 4 * m:4 * m + 4].rearrange("p a i j -> p (a i j)")
                    v0, v1 = (Vp[:, x, 4 * m:4 * m + 4, :].rearrange("p a b -> p (a b)") for x in range(2))
                    w0, w1 = (tw[:, x].rearrange("p a b -> p (a b)") for x in range(2))
                    c.add(tt(v0, bank[2 * m], cb, ALU.mult))
                    c.add(tt(w0, bank[2 * m + 1], sb_, ALU.mult))
                    c.add(tt(v1, bank[2 * m + 1], cb, ALU.mult))
                    c.step(tt(w1, bank[2 * m], sb_, ALU.mult))
                    c.add(tt(v0, v0, w0, ALU.add))
                    c.step(tt(v1, v1, w1, ALU.subtract))
                for r in range(4):
                    dve.wait_ge(s5_vs, q * 4 + (r + 1))
                    for x in range(2):
                        st = hs[:, x, ds(q * PP + 2 * r, 2), :]
                        last = tt(st, st, bank[4 + r][:, 0:4 * NS].rearrange("p (a x b) -> p a x b", a=2, x=2)[:, :, x, :],
                                  ALU.add)
                    last.then_inc(s5_vsd, 1)
                for pp in range(PP):
                    for x in range(2):
                        row = Vp[:, x, pp, :]
                        c.add(v_.tensor_tensor_scan(row, decay[:, ds(q * PP + pp, 1), NW - 1:NW]
                                                    .rearrange("p a b -> p (a b)").to_broadcast([P, NB]),
                                                    row, 0.0, ALU.mult, ALU.add))
                c.sync()
                dve.wait_ge(s5_y, q * 8 + 1)
                for m in range(2):
                    cb = CB[:, 4 * m:4 * m + 4].rearrange("p a i j -> p a (i j)")
                    sb_ = SB[:, 4 * m:4 * m + 4].rearrange("p a i j -> p a (i j)")
                    g0, g1 = Vp[:, 0, 4 * m:4 * m + 4, :], Vp[:, 1, 4 * m:4 * m + 4, :]
                    h_r, h_i = (H[:, x, 4 * m:4 * m + 4, NS + 1:HW_] for x in range(2))
                    c.add(tt(h_r, g0, cb, ALU.mult))
                    c.add(tt(tw[:, 0], g1, sb_, ALU.mult))
                    c.add(tt(h_i, g0, sb_, ALU.mult))
                    c.step(tt(tw[:, 1], g1, cb, ALU.mult))
                    c.add(tt(h_r, h_r, tw[:, 0], ALU.subtract))
                    c.step(tt(h_i, h_i, tw[:, 1], ALU.add))
                for x in range(2):
                    v_.tensor_copy(H[:, x, :, 0:NS], h0[:, x, pr, :])
                    v_.memset(H[:, x, :, NS:NS + 1], 0.0)
                    last = v_.tensor_copy(fin[:, x, pr, :], H[:, x, :, HW_ - 1:HW_])
                last.then_inc(s5_h, 1)
                dve.wait_ge(s5_kc, q * 4 + 4)
                D3 = [16, GP, 16]
                c.step(tt(dI[:], bc(ident[0:16, 0:16], 1, D3), bc(d16[:, ds(q * GP, GP)], 2, D3), ALU.mult))
                tt(Kc[:, :, 0:16], Kc[:, :, 0:16], dI[:], ALU.add).then_inc(s5_kd, 1)
                assert c.n == DVE_STEPS, c.n
            c = Chain(dve, dve_chain, PARTS * DVE_STEPS + dve_base)

            for k in range(KT):
                dve.wait_ge(z_hi, k + 1)
                tt(act_lo[:, k, 0:SEQ].rearrange("p (b s) -> p b s", s=L),
                   Z[:, k, 0:SEQ].rearrange("p (s b) -> p b s", s=L),
                   act_hi[:, k, 0:SEQ].bitcast(F32).rearrange("p (b s) -> p b s", s=L), ALU.subtract)
                tt(act_lo[:, k, SEQ:T], Z[:, k, SEQ:T], act_hi[:, k, SEQ:T].bitcast(F32), ALU.subtract
                   ).then_inc(z_lo, 1)
            def glu(m, n, last=False):
                dve.wait_ge(gl_sig, m * 3 + (n + 1))
                if last and n == 2:
                    dve.wait_ge(at_lo, KT)
                tt(tmp[:, n, :], bank[2 * n][:, 0:CW], gate[:, n, :], ALU.mult).then_inc(gl_mul, 1)
                dve.wait_ge(gl_mul, m * 3 + (n + 1))
                x = X[:, ds(m, 1), cs(n)].rearrange("p o t -> p (o t)")
                tt(x, x, tmp[:, n, :], ALU.add).then_inc(gl_done, 1)
                dve.wait_ge(nm_add, m * 3 + (24 + n - 2))
                add_square(1, m * 3 + n, n)

            clear_sums(1)
            with dve.Fori(0, KT - 1) as m:
                for n in range(NC):
                    glu(m, n)

            def hidden(tile, base):
                for n in range(NC):
                    i = base + (3 * tile + n)
                    if tile:
                        dve.wait_ge(hid_lo_s, i - 2)
                    dve.wait_ge(gu_silu, i + 1)
                    tt(tmp[:, n, :], gate[:, n, :], bank[2 * n + 1][:, 0:CW], ALU.mult).then_inc(hid_tmp, 1)
                    dve.wait_ge(hid_hi_s, i + 1)
                    h = (slice(None), (tile // 2) % 2, tile % 2, cs(n))
                    tt(hid_lo[h], tmp[:, n, :], hid_hi[h].bitcast(F32), ALU.subtract).then_inc(hid_lo_s, 1)

            def down(base):
                for q in range(24):
                    dve.wait_ge(dn_ready, base + (q + 1))
                    x = X[:, q % 8, cs(q // 8)]
                    tt(x, x, bank[(6 + q) % 8][:, 0:CW], ALU.add).then_inc(dn_added, 1)

            def ffn(f, v, normal):
                hidden(0, 66 * f)
                hidden(1, 66 * f)
                with dve.Fori(0, (NIT - 1) // 2) as b:
                    for half in range(2):
                        hidden(2 + 2 * half, b * 12 + 66 * f)
                        hidden(3 + 2 * half, b * 12 + 66 * f)
                        down(b * 48 + (24 * half + 264 * f))
                norm_after_down(f, v, normal)

            norm_after(1, 0, 2, lambda n: glu(KT - 1, n, True))
            ffn(0, 2, lambda first, last: normalise(2, 1, 4, first, last))
            for tt_ in range(3 * KT):
                if tt_ == 2 * KT - 2:
                    for n in range(NC):
                        dve.wait_ge(kv_ready, 3 * KT - 3 + n + 1)
                        normalise(2, 2, 1, n * KT, n * KT + KT)
                dve.wait_ge(kv_evicted, 6 * (tt_ // 2) + 6)
                m, keep = tt_ % KT, (kS, vS, qS)[tt_ // KT]
                slot = slots[tt_][0]
                if slots[tt_][1]:
                    if m == 0:
                        continue
                    x1, x2 = stage[:, slots[tt_ - 1][0], :], stage[:, slot, :]
                    dve.wait_ge(rope_in, 32)
                    dve.wait_ge(rope_out, 32 * (tt_ // (2 * KT)))
                    c.add(tt(roped[:, 0, :], x1, cosr[:], ALU.mult))
                    c.step(tt(rtmp[:], x2, sinr[:], ALU.mult))
                    c.step(tt(roped[:, 0, :], roped[:, 0, :], rtmp[:], ALU.subtract))
                    c.add(tt(roped[:, 1, :], x2, cosr[:], ALU.mult))
                    c.step(tt(rtmp[:], x1, sinr[:], ALU.mult))
                    c.step(tt(roped[:, 1, :], roped[:, 1, :], rtmp[:], ALU.add))
                    v_.tensor_copy(keep[:, 0:2, :], roped[:, :, SEQ:T]).then_inc(d_smp, 2)
                    v_.memset(dsc[:, 2:3], 0.0).then_inc(kv_roped, 1)
                else:
                    v_.tensor_copy(keep[:, m, :], stage[:, slot, SEQ:T]).then_inc(d_smp, 1)

            dve.wait_ge(act_chain, 1)
            c.step(tt(lamt[:, 4:5], lamt[:, 3:4], lamt[:, 2:3], ALU.subtract))
            c.step(v_.tensor_scalar(lamt[:, 4:5], lamt[:, 4:5], LAM_INIT, None, ALU.subtract))
            neglam = lamt[:, 4:5]

            def row_max(v, c_, x):
                dve.wait_ge(a_s, v * 2 + (x + 1))
                n = (c_ % 8 + 1) * P
                v_.tensor_reduce(nmx[:, c_ % 2, x:x + 1], pair[x][:, 0:n], axis=AXX, op=ALU.max, negate=True
                                 ).then_inc(a_max, 1)

            def out_copy(v, h, c_):
                dve.wait_ge(a_o, v + 1)
                v_.tensor_scalar(O[:, ds(h, 1), c_ % 8, :].rearrange("p o e -> p (o e)"), bank[6 + c_ % 2][:, 0:P],
                                 rinv[:, c_ % 4, 0:1], None, ALU.mult).then_inc(a_oc, 1)

            def key_sums(b):
                for j in range(NPG):
                    dve.wait_ge(d_mul, b * 2 + (j + 1))
                    v_.reduce_sum(stok[:, j, ds(b * HC, HC)], kpg[:, j, :].rearrange("p (c d) -> p c d", d=HD),
                                  axis=AXX).then_inc(d_red, 1)

            def step(v, h, c_):
                n = (c_ % 8 + 1) * P
                if c_ != 63:
                    row_max(v + 1, c_ + 1, 0)
                dve.wait_ge(a_exp, v * 2 + 2)
                v_.reciprocal(rinv[:, c_ % 4, :], sums[:, c_ % 2, :]).then_inc(a_r, 1)
                dve.wait_ge(a_r, v * 2 + 1)
                v_.scalar_tensor_tensor(rho[:, c_ % 2, :], sums[:, c_ % 2, 0:1], neglam, rinv[:, c_ % 4, 1:2],
                                        ALU.mult, ALU.mult).then_inc(a_r, 1)
                dve.wait_ge(a_r, v * 2 + 2)
                if c_ >= 2:
                    dve.wait_ge(a_tr, v - 1)
                v_.scalar_tensor_tensor(wmix[:, c_ % 2, 0:n], prob[:, c_ % 2, 1, 0:n], rho[:, c_ % 2, :],
                                        prob[:, c_ % 2, 0, 0:n], ALU.mult, ALU.add).then_inc(a_mix, 1)
                if c_ != 63:
                    row_max(v + 1, c_ + 1, 1)
                if c_ >= 2:
                    out_copy(v - 2, h if c_ % 8 >= 2 else h - 1, c_ - 2)
                if c_ == 52:
                    dve.wait_ge(on_std, 1)
                    v_.reciprocal(orst[:, 0:48], orst[:, 0:48]).then_inc(on_r, 1)
                if (c_ % 8 == 4 and c_ <= 52) or c_ == 55:
                    key_sums(h if c_ <= 52 else NS - 1)

            row_max(0, 0, 0)
            row_max(0, 0, 1)
            attention_steps(dve, step)
            out_copy(62, 7, 62)
            out_copy(63, 7, 63)
            dve.wait_ge(d_smp, 24)
            pr_ = tmpd[:, 0:64].rearrange("p (m b) -> p m b", m=8)
            c.step(tt(pr_, qS[:], kS[:], ALU.mult))
            c.step(v_.reduce_sum(tmpd[:, 64:72], tmpd[:, 0:64].rearrange("p (m b) -> p b m", m=8), axis=AXX))
            N3 = [P, NS, HC]
            tt(newl[:], bc(tmpd[:, 64:72], 2, N3), bc(sel[:], 1, N3), ALU.mult).then_inc(d_new, 1)
            dve.wait_ge(d_sc, 1)
            v_.tensor_reduce(dsc[:, 0:1], bank[4][:, 0:2 * P + 1], axis=AXX, op=ALU.max, negate=True).then_inc(d_s2, 1)
            dve.wait_ge(d_p2, 1)
            c.add(v_.reciprocal(dsc[:, 3:4], dsc[:, 1:2]))
            c.step(v_.scalar_tensor_tensor(dsc[:, 4:5], evenodd[:, 1:2], neglam, evenodd[:, 0:1], ALU.mult, ALU.add))
            c.step(tt(dsc[:, 5:6], dsc[:, 3:4], dsc[:, 4:5], ALU.mult))
            c.step(v_.tensor_scalar(p2[:], p2[:], dsc[:, 5:6], None, ALU.mult))
            v_.tensor_scalar(wnew[:], ones[:], p2[:, 2 * P:2 * P + 1], None, ALU.mult).then_inc(d_p2n, 1)

            def head_low(h):
                dve.wait_ge(on_hi, h + 1)
                v_.scalar_tensor_tensor(act_lo[:, h, 0:SEQ], pair[h % 2][:], gsub[:],
                                        act_hi[:, h, 0:SEQ].bitcast(F32), ALU.mult, ALU.subtract).then_inc(on_lo, 1)

            head_low(0)
            dve.wait_ge(d_wc, 1)
            for j in range(NPG):
                W5 = [P, NS, NH, NS]
                last = tt(wpad[:, j], bc(wtok[:, j, :].rearrange("p (b h) -> p b h", b=NS), 3, W5),
                          bc(eye8[:].rearrange("p (b m) -> p b m", b=NS), 2, W5), ALU.mult)
            last.then_inc(d_wp, 1)
            head_low(1)
            dve.wait_ge(on_std, 2)
            c.step(v_.reciprocal(orst[:, 48:64], orst[:, 48:64]))
            for h in (6, 7):
                tt(O[:, h], O[:, h], bc(orst[:, 8 * h:8 * h + 8], 2, [P, KT, P]), ALU.mult).then_inc(on_w, 1)
            for h in range(2, NH):
                head_low(h)
            c.step(tt(oS[:], vS[:].rearrange("p h b -> p b h"),
                      wtok[:, 2, :].rearrange("p (b h) -> p b h", b=NS), ALU.mult))
            dve.wait_ge(d_ot, 1)
            c.step(tt(oS[:], oS[:], bank[6][:, 0:64].rearrange("p (h b) -> p b h", b=NS), ALU.add))
            tt(oS2[:], oS[:], oS[:], ALU.mult).then_inc(d_sq, 1)
            dve.wait_ge(d_rs, 1)
            c.step(v_.reciprocal(oS2[:], oS2[:]))
            c.step(tt(oS[:], oS[:], oS2[:], ALU.mult))
            v_.tensor_scalar(oS[:], oS[:], gsub[:], None, ALU.mult).then_inc(d_fin, 1)
            dve.wait_ge(d_hi, 1)
            tt(act_lo[:, :, SEQ:T].rearrange("p h b -> p b h"), oS[:],
               act_hi[:, :, SEQ:T].bitcast(F32).rearrange("p h b -> p b h"), ALU.subtract).then_inc(d_lo, 1)
            clear_sums(3)

            def out_pair(p, n):
                dve.wait_ge(op_ready, 3 * p + n + 1)
                for x in range(2):
                    o = X[:, 2 * p + x, cs(n)]
                    tt(o, o, bank[2 * n + x][:, 0:CW], ALU.add).then_inc(op_added, 1)
                for x in range(2):
                    i = 6 * p + 2 * n + x
                    dve.wait_ge(nm_add, 72 + i)
                    add_square(3, i, n)

            for p in range(KT // 2 - 1):
                for n in range(NC):
                    out_pair(p, n)
            norm_after(3, 3, 3, lambda n: out_pair(KT // 2 - 1, n))

            def final(first, last):
                for i in range(first, last):
                    n, k = i // KT, i % KT
                    dve.wait_ge(nm_r, 3 * 4 + n + 1)
                    scaled(Y[:, k, cs(n)], k, n, 5).then_inc(y_done, 1)

            ffn(1, 4, final)

        @block.tensor
        def _(pe):
            t_ = nc.tensor

            def mm(out, lhsT, rhs, start, stop):
                return t_.matmul(out, lhsT, rhs, start=start, stop=stop)

            def sums(v, n, items):
                pe.wait_ge(nm_add, 24 * v + items)
                if v or n:
                    pe.wait_ge(nm_std, 3 * v + n)
                for j in range(4):
                    last = mm(bank[7][0:TB, 4 * n + j:4 * n + j + 1], acc[:, n, j * TB:(j + 1) * TB],
                              ones[:, 0:1], True, True)
                last.then_inc(nm_ss, 1)

            def spread(v, n):
                pe.wait_ge(nm_diag, 3 * v + n + 1)
                if v or n:
                    pe.wait_ge(nm_r, 3 * v + n)
                for j in range(4):
                    last = mm(bank[6][:, j * TB:(j + 1) * TB], ones[0:TB, :], diag[:, j, :], True, True)
                last.then_inc(nm_bc, 1)

            def norm_beside(v, items):
                return ({(1, 0): lambda: sums(v, 0, items[0]), (1, 1): lambda: spread(v, 0),
                         (2, 0): lambda: sums(v, 1, items[1]), (2, 1): lambda: spread(v, 1)},
                        {(0, 0): lambda: sums(v, 2, 24), (0, 1): lambda: spread(v, 2)})

            def dense(out, slot, n, rhs_hi, rhs_lo, first=False):
                for k in range(KT):
                    wh, wl = (w[:, slot, k * P:(k + 1) * P] for w in (w_hi, w_lo))
                    ah, al = rhs_hi[:, k, cs(n)], rhs_lo[:, k, cs(n)]
                    ins = mm(out, wh, ah, k == 0, False)
                    if first and k == 0:
                        ins.then_inc(w_used, 1)
                    mm(out, wh, al, False, False)
                    last = mm(out, wl, ah, False, k == KT - 1)
                return last

            def pair_of_units(n, u, ready, beside={}, release=True):
                last = dense(bank[2 * n][:, 0:CW], u % 4, n, act_hi, act_lo, n == 0 and release)
                if n == NC - 1:
                    last.then_inc(w_used, 1)
                if (n, 0) in beside:
                    beside[n, 0]()
                dense(bank[2 * n + 1][:, 0:CW], (u + 1) % 4, n, act_hi, act_lo).then_inc(ready, 1)
                if (n, 1) in beside:
                    beside[n, 1]()

            pe.sem_inc(s5_y, 1)
            pe.wait_ge(const0_in, n_const[0])
            pe.wait_ge(const_in, n_const[1])
            for n in range(NC):
                sums(0, n, KT * n + KT)
                spread(0, n)
            with pe.Fori(0, PARTS) as q:
                pe.wait_ge(s5_w, q + 1)
                pe.wait_ge(s5_gelu, q * 8 + 1)
                for r in range(4):
                    for x in range(4):
                        src = (W_re, W_im)[x % 2][:, 2 * r + x // 2].rearrange("p n h -> p (n h)")
                        last = t_.transpose(bank[4 + r][:, x * P:(x + 1) * P], src, ident[:])
                    last.then_inc(s5_t, 1)
                pe.wait_ge(u_in, q * 160 + 160)
                pe.wait_ge(s5_rt, q * 4 + 4)
                for m in range(2):
                    for pp in range(4):
                        for x in range(2):
                            for g2 in range(2):
                                pi = 4 * m + pp
                                last = mm(bank[2 * m + x][64 * g2:64 * g2 + 64, pp * NB:(pp + 1) * NB],
                                          RT[:, pi, x, 64 * g2:64 * g2 + 64], ublk[:, 2 * pi + g2, NS:BW], True, True)
                    last.then_inc(s5_v, 1)
                for r in range(4):
                    for y in range(2):
                        for x in range(2):
                            for g2 in range(2):
                                pi = 2 * r + y
                                last = mm(bank[4 + r][64 * g2:64 * g2 + 64, (2 * y + x) * NS:(2 * y + x + 1) * NS],
                                          RT[0:16, pi, x, 64 * g2:64 * g2 + 64], usp[:, 2 * pi + g2, :], True, True)
                    last.then_inc(s5_vs, 1)
                pe.wait_ge(s5_g, q * 2 + 2)
                for r in range(4):
                    pe.wait_ge(s5_vsd, q * 4 + (r + 1))
                    settle(pe)
                    for x in range(4):
                        pi, rows = 4 * (r // 2) + x, slice(64 * (r % 2), 64 * (r % 2) + 64)
                        out = bank[4 + r][0:16, x * P:(x + 1) * P]
                        mm(out, bbar[rows, 0, pi, :], G_re[rows, pi, 0:L, :].rearrange("p n h -> p (n h)"), True, False)
                        last = mm(out, bbar[rows, 1, pi, :], G_im[rows, pi, 0:L, :].rearrange("p n h -> p (n h)"),
                                  False, True)
                    last.then_inc(s5_k, 1)
                pe.wait_ge(s5_h, q + 2)
                pe.wait_ge(t_in, q * 128 + 129)
                for r in range(8):
                    if r < 4:
                        pe.wait_ge(s5_kc, q * 4 + (r + 1))
                    else:
                        pe.wait_ge(s5_gelu, q * 8 + (r - 2))
                    for x in range(2):
                        pi, g2 = 2 * (r // 2) + x, r % 2
                        rows = slice(64 * g2, 64 * g2 + 64)
                        out = bank[4 + r % 4][:, x * BW:(x + 1) * BW]
                        mm(out, G_re[rows, pi, 1:NW, :].rearrange("p n h -> p (n h)"), H[rows, 0, pi, 0:BW], True, False)
                        mm(out, G_im[rows, pi, 1:NW, :].rearrange("p n h -> p (n h)"), H[rows, 1, pi, 0:BW], False, False)
                        last = mm(out, TM[:, 2 * pi + g2, :], ublk[:, 2 * pi + g2, :], False, True)
                    last.then_inc(s5_y, 1)

            pe.wait_ge(z_lo, KT)
            def glu(i, half, beside={}):
                pe.wait_ge(w_split, i * 4 + (2 * half + 2))
                for n in range(NC):
                    pe.wait_ge(gl_done, i * 6 + (GL0 + 3 * half - 3 + n + 1))
                    pair_of_units(n, 2 * half, gl_ready, beside)

            with pe.Fori(0, KT // 2 - 1) as i:
                for half in range(2):
                    glu(i, half)
            glu(KT // 2 - 1, 0)
            last_chunks, first_chunks = norm_beside(1, (22, 23))
            glu(KT // 2 - 1, 1, last_chunks)

            def ffn(f, w, first_chunks, v):
                u0, hb, db = (U_FFN0, U_FFN1)[f], 66 * f, DN0 + 264 * f

                def gate_up(b, u, tile, spare, beside={}):
                    pe.wait_ge(w_split, b * 12 + (u + 2))
                    for n in range(NC):
                        if tile == 0:
                            pe.wait_ge(at_lo, 24 * w + 8 * n + 8)
                        else:
                            pe.wait_ge(hid_tmp, b * 12 + (hb + 3 * tile - 3 + n + 1))
                        if spare is not None:
                            pe.wait_ge(dn_added, b * 48 + (db + spare(n)))
                        pair_of_units(n, u, gu_ready, beside)

                def down(b, u, i):
                    pe.wait_ge(w_split, b * 12 + (u + 2))
                    for q in range(24):
                        n, j = q // 8, q % 8
                        if j == 0:
                            pe.wait_ge(hid_lo_s, b * 12 + (hb + 6 * i + 3 + n + 1))
                        if q >= 8:
                            pe.wait_ge(dn_added, b * 48 + (db + 24 * i + q - 7))
                        elif q >= 2:
                            pe.wait_ge(hid_tmp, b * 12 + (hb + 3 * (2 * i + 3) + (q - 2) // 2 + 1))
                        down_tile(bank[(6 + q) % 8][:, 0:CW], u, i, q)

                def down_tile(out, u, i, q):
                        n, j = q // 8, q % 8
                        for t in range(2):
                            wh, wl = (x[:, (u + t) % 4, j * P:(j + 1) * P] for x in (w_hi, w_lo))
                            hh, hl = (x[:, i % 2, t, cs(n)] for x in (hid_hi, hid_lo))
                            ins = mm(out, wh, hh, t == 0, False)
                            if q == 0 and t == 0:
                                ins.then_inc(w_used, 1)
                            mm(out, wh, hl, False, False)
                            last = mm(out, wl, hh, False, t == 1)
                            if q == 23 and t == 0:
                                last.then_inc(w_used, 1)
                        last.then_inc(dn_ready, 1)

                def down_last(u, i):
                    pe.wait_ge(w_split, u + 2)
                    for q in range(24):
                        if q % 8 == 0:
                            pe.wait_ge(hid_lo_s, hb + 6 * i + 3 + q // 8 + 1)
                        pe.wait_ge(dn_added, db + 24 * i + (q - 5 if q >= 6 else q - 5))
                        down_tile(bank[q % 6][:, 0:CW], u, i, q)
                        if q == 11:
                            sums(v, 0, 8)
                        if q == 15:
                            spread(v, 0)
                        if q == 19:
                            sums(v, 1, 16)
                        if q == 23:
                            spread(v, 1)

                for t in range(2):
                    gate_up(0, u0 + 2 * t, t, None, first_chunks if t == 0 else {})
                with pe.Fori(0, (NIT - 1) // 2) as b:
                    for half in range(2):
                        u = u0 + 4 + 6 * half
                        for t in range(2):
                            spare = (lambda n: 24 * half - 4 + 2 * n)
                            gate_up(b, u + 2 * t, 2 + 2 * half + t, spare if t == 0 else None)
                        down(b, u + 4, half)
                down_last(u0 + 4 + 60, NIT - 1)

            ffn(0, 0, first_chunks, 2)

            def projections(b, x, w=0, beside={}):
                pe.wait_ge(w_split, b * 4 + (U_KVQ + x + 2))
                for n in range(NC):
                    if w:
                        pe.wait_ge(at_lo, 24 * w + 8 * n + 8)
                    if x >= 2:
                        pe.wait_ge(kv_evicted, b * 12 + (3 * (x - 2) + 2 * n + 2))
                    pair_of_units(n, U_KVQ + x, kv_ready, beside)

            pe.wait_ge(dn_added, DN0 + 264)
            projections(0, 0, 1, {(0, 0): lambda: sums(2, 2, 24), (0, 1): lambda: spread(2, 2)})
            with pe.Fori(0, 3) as b:
                for x in (2, 4):
                    projections(b, x)
            for x in (14, 16, 18, 20, 22):
                projections(0, x, 2 if x == 16 else 0)
            pe.wait_ge(d_smp, 3 * KT)
            for m in range(KT):
                last = t_.transpose(pair[3][0:NS, m * P:(m + 1) * P], qS[:, m, :], ident[:])
                if m == 0:
                    last.then_inc(w_used, 1)
            last.then_inc(d_qt, 1)

            def values(v, h, c):
                par = (c // 8) % 2
                pe.wait_ge(hd_in[par], v * 5 + (80 * (c // 16 + 1) - 5 * c))
                for kb in range(KT):
                    last = t_.transpose(pair[2][:, kb * P:(kb + 1) * P], vT[:, par, kb * P:(kb + 1) * P], ident[:])
                last.then_inc(a_vt, 1)

            def scores(v, c, x):
                i, par = c % 8, (c // 8) % 2
                if c:
                    pe.wait_ge(a_exp, v * 2 + (x - 1))
                q = qz[:, par, x, i * P:(i + 1) * P]
                n = (i + 1) * P
                for at in range(0, n, 512):
                    end = min(at + 512, n)
                    last = mm(pair[x][:, at:end], q, kh[:, par, at:end], True, end < n)
                last = mm(pair[x][:, n - P:n], identb[:], maskb[:], False, True)
                last.then_inc(a_s, 1)

            def outputs(v, h, c):
                pe.wait_ge(a_wt, v + 1)
                pe.wait_ge(a_v, h + 1)
                if c >= 2:
                    pe.wait_ge(a_oc, v - 1)
                for kb in range(c % 8 + 1):
                    last = mm(bank[6 + c % 2][:, 0:P], wT[:, c % 2, kb * P:(kb + 1) * P],
                              vtok[:, (c // 8) % 2, kb, :], kb == 0, kb == c % 8)
                last.then_inc(a_o, 1)

            def step(v, h, c):
                if c % 8 == 7 and c != 63:
                    pe.wait_ge(a_wt, v)
                    values(v + 1, h + 1, c + 1)
                if c != 63:
                    scores(v + 1, c + 1, 0)
                    scores(v + 1, c + 1, 1)
                if c >= 1:
                    outputs(v - 1, h if c % 8 else h - 1, c - 1)
                pe.wait_ge(a_mix, v + 1)
                pe.wait_ge(a_wt, v)
                pe.wait_ge(a_v, h + 2 if c % 8 == 7 and c != 63 else h + 1)
                for kb in range(c % 8 + 1):
                    last = t_.transpose(pair[2][:, kb * P:(kb + 1) * P], wmix[:, c % 2, kb * P:(kb + 1) * P],
                                        ident[:])
                last.then_inc(a_tr, 1)

            pe.wait_ge(kv_evicted, 9 * KT)
            pe.wait_ge(q_zero, 2)
            values(0, 0, 0)
            scores(0, 0, 0)
            scores(0, 0, 1)
            pe.wait_ge(d_qrow, 1)
            attention_steps(pe, step)
            outputs(63, 7, 63)

            pe.wait_ge(d_red, 2 * NS + 1)
            pe.wait_ge(d_new, 1)
            for j in range(NPG):
                t_.transpose(bank[4][:, j * P:(j + 1) * P], stok[:, j, :], ident[:])
            mm(bank[4][:, 2 * P:2 * P + 1], newl[:].rearrange("p b c -> p (b c)"), ones[:, 0:1], True, True
               ).then_inc(d_sc, 1)

            def head(h):
                if h < 6:
                    pe.wait_ge(on_p, h + 1)
                else:
                    pe.wait_ge(on_w, h - 5)
                if h >= 2:
                    pe.wait_ge(on_lo, h - 1)
                for i in range(KT):
                    last = t_.transpose(pair[h % 2][:, i * P:(i + 1) * P], O[:, h, i, :], ident[:])
                last.then_inc(on_tr, 1)

            def sample_values(b):
                for j in range(NPG):
                    pe.wait_ge(vpg_in[2 * (b % 2) + j], 16 * (b // 2) + 16)
                    for h in range(NH):
                        last = mm(pair[2][0:NS, h * P:(h + 1) * P], wpad[:, j, b, h, :],
                                  vpg[:, 2 * (b % 2) + j, h * P:(h + 1) * P],
                                  b == 0 and j == 0 and h % 4 == 0, b == NS - 1 and j == NPG - 1 and h % 4 == 3)
                last.then_inc(d_o, 1)

            head(0)
            head(1)
            pe.wait_ge(d_p2n, 1)
            for j in range(NPG):
                mm(bank[5][:, j * 64:(j + 1) * 64], p2[:, j * P:(j + 1) * P], pairsel[:], True, True)
            mm(bank[5][:, 128:192], wnew[:], pairsel[:], True, True).then_inc(d_w, 1)
            pe.wait_ge(d_wp, 1)
            for b in range(NS):
                sample_values(b)
                if b + 2 < NH:
                    head(b + 2)
            pe.wait_ge(d_row, 1)
            for h in range(NH):
                last = t_.transpose(bank[6][:, h * NS:(h + 1) * NS], orow[:, h * P:(h + 1) * P], ident[0:NS, 0:NS])
            last.then_inc(d_ot, 1)
            pe.wait_ge(d_sq, 1)
            mm(bank[7][:, 0:64], ones[:], oS2[:].rearrange("p b h -> p (b h)"), True, True).then_inc(d_ssq, 1)

            pe.wait_ge(on_lo, NH)
            pe.wait_ge(d_lo, 1)
            last_chunks, first_chunks = norm_beside(3, (20, 22))
            for p in range(KT // 2):
                pe.wait_ge(w_split, U_O + 2 * p + 2)
                for n in range(NC):
                    pe.wait_ge(op_added, OP0 + 6 * (p - 1) + 2 * n + 2)
                    pair_of_units(n, U_O + 2 * p, op_ready, last_chunks if p == KT // 2 - 1 else {}, p > 0)
            ffn(1, 3, first_chunks, 4)
            sums(4, 2, 24)
            spread(4, 2)


def constants():
    f = np.float32
    nvec = np.concatenate([np.arange(NW), L * np.arange(NJ), L * NJ * np.arange(NI)]).astype(f)
    p = np.arange(P)
    inv = (f(500000.0) ** (-np.arange(0, ROT, 2, dtype=f) / f(ROT))).astype(f)
    pos = np.concatenate([np.arange(SEQ), np.full(NS, NPG * PAGE)]).astype(f)
    ang = (pos[None, :] * inv[:, None]).astype(f).astype(np.float64)
    rows = p % 8
    return {
        "c_nvec": np.tile(nvec, (P, 1)),
        "c_ones": np.ones((P, P), f),
        "c_ident": np.eye(P, dtype=f),
        "c_identb": np.eye(P, dtype=f).astype(mybir.dt.np(BF16)),
        "c_maskb": np.where(p[None, :] > p[:, None], f(-1e30), f(0)).astype(mybir.dt.np(BF16)),
        "c_sel": (p[:, None] // 8 == np.arange(HC)[None, :]).astype(f),
        "c_pairsel": (((p // HC) * NH + (p % HC) // 2)[:, None] == np.arange(64)[None, :]).astype(f),
        "c_evenodd": np.stack([p % 2 == 0, p % 2 == 1], 1).astype(f),
        "c_eye8": np.tile(np.eye(NS, dtype=f).reshape(1, 64), (P, 1)),
        "c_cos": np.cos(ang).astype(f)[rows],
        "c_sin": np.sin(ang).astype(f)[rows],
    }


def weight_stream(glu_a, glu_b, w_k, w_v, w_q, w_o, gate, up, down):
    def tiles(w):
        return w.reshape(KT, P, -1, P).transpose(2, 1, 0, 3).reshape(-1, P, DM)

    def by_rotation(w):
        return w.reshape(DM, HC, 8, 8).transpose(0, 2, 1, 3).reshape(DM, DM)

    def ffn(i):
        g, u, dn = tiles(gate[i]), tiles(up[i]), down[i].reshape(FT, P, DM)
        out = [g[0], u[0], g[1], u[1]]
        for it in range(NIT):
            if it + 1 < NIT:
                t = 2 * it + 2
                out += [g[t], u[t], g[t + 1], u[t + 1]]
            out += [dn[2 * it], dn[2 * it + 1]]
        return out

    a, b = tiles(glu_a), tiles(glu_b)
    units = [x for m in range(KT) for x in (a[m], b[m])] + ffn(0)
    units += list(tiles(by_rotation(w_k))) + list(tiles(w_v)) + list(tiles(by_rotation(w_q)))
    units += list(tiles(w_o)) + ffn(1)
    return np.stack(units)


def kernel(x_prompt, x_sample, cache_k, cache_v, state_ssm_re, state_ssm_im, page_table,
           mix_norm, ffn_norm, kv_norm, final_norm,
           ssm_a_re, ssm_a_im, ssm_log_dt, ssm_b_re, ssm_b_im, ssm_c_re, ssm_c_im, ssm_d,
           glu_w_a, glu_w_b, w_q, w_k, w_v, lambda_q1, lambda_k1, lambda_q2, lambda_k2,
           subln, w_o, ffn_w_gate, ffn_w_up, ffn_w_down):
    import concourse.bacc as bacc
    from concourse.bass_utils import run_bass_kernel_spmd

    def np_(x):
        return np.asarray(x)

    def by_state(x):
        x = x.reshape((PAIRS, P) + x.shape[2:])
        return np.moveaxis(x, 1, 0)

    are, aim, ldt = np_(ssm_a_re)[0], np_(ssm_a_im)[0], np_(ssm_log_dt)[0]
    arrays = {
        "x_t": np.concatenate([np_(x_prompt)[0].T, np_(x_sample)[:, 0].T], axis=1),
        "gains": np.stack([np_(mix_norm)[0], np_(mix_norm)[1], np_(ffn_norm)[0], np_(ffn_norm)[1],
                           np_(kv_norm), np_(final_norm)]).reshape(6, KT, P).transpose(2, 0, 1),
        "s_abc": np.stack([by_state(are), by_state(aim),
                           by_state(np.broadcast_to(ldt[:, None], (NG, ST)))], axis=1),
        "s_b": np.stack([by_state(np_(ssm_b_re)[0]), by_state(np_(ssm_b_im)[0])], axis=1),
        "s_c": np.stack([by_state(np_(x)[0].transpose(0, 2, 1)) for x in (ssm_c_re, ssm_c_im)], axis=1),
        "s_h0": np.stack([by_state(np_(x)[0].transpose(1, 2, 0)) for x in (state_ssm_re, state_ssm_im)], axis=1),
        "s_d": np_(ssm_d)[0].reshape(NG, 16).T,
        "lam": np.concatenate([np_(lambda_q1), np_(lambda_k1), np_(lambda_q2), np_(lambda_k2)]),
        "subln": np_(subln)[0][:, None],
        "page_table": np_(page_table).reshape(1, NS * NPG),
        "cache_k": np_(cache_k).reshape(-1, PAGE, DM),
        "cache_v": np_(cache_v).reshape(-1, PAGE, DM),
        "w": weight_stream(np_(glu_w_a)[0], np_(glu_w_b)[0], np_(w_k), np_(w_v), np_(w_q)[0], np_(w_o)[0],
                           np_(ffn_w_gate), np_(ffn_w_up), np_(ffn_w_down)),
    }
    arrays.update(constants())
    outs = {"kt": (KT, P, T), "vt": (KT, P, T), "y_t": (DM, T), "ssm_p": (P, 2, PAIRS, 1),
            "ssm_s": (P, 2, PAIRS, NS)}
    scratch = {"u": (DM, T), "z": (DM, T), "qt": (KT, P, T), "qrow": (NS, DM)}

    nc = bacc.Bacc("TRN2", target_bir_lowering=False, num_devices=1)
    d = {"n_pages": arrays["cache_k"].shape[0]}
    feed = {}
    for name, a in arrays.items():
        feed[name] = np.ascontiguousarray(a)
        d[name] = nc.dram_tensor(name, a.shape, mybir.dt.from_np(a.dtype), kind="ExternalInput").ap()
    for name, shape in outs.items():
        d[name] = nc.dram_tensor(name, shape, F32, kind="ExternalOutput").ap()
    for name, shape in scratch.items():
        d[name] = nc.dram_tensor(name, shape, F32, kind="Internal").ap()
    build(nc, d)
    r = run_bass_kernel_spmd(nc, [feed], core_ids=[0]).results[0]

    k = r["kt"].reshape(KT, NH, 2, 8, T).transpose(4, 1, 2, 0, 3).reshape(T, NH, 2, HD)
    v = r["vt"].transpose(2, 0, 1)
    y = r["y_t"].T

    def states(x, n):
        return x.reshape(P, PAIRS, n).transpose(2, 1, 0).reshape(1, n, NG, ST)

    sp_, ss = r["ssm_p"], r["ssm_s"]
    return (y[None, :SEQ], y[SEQ:, None], k[None, :SEQ], v[None, :SEQ], states(sp_[:, 0], 1), states(sp_[:, 1], 1),
            k[SEQ:, None], v[SEQ:, None], states(ss[:, 0], NS), states(ss[:, 1], NS))
```

```python
import math
from contextlib import ExitStack

import numpy as np
import concourse.bass as bass
from concourse import mybir

F32 = mybir.dt.float32
F32R = mybir.dt.float32r
BF16 = mybir.dt.bfloat16
I32 = mybir.dt.int32
ALU = mybir.AluOpType
ACT = mybir.ActivationFunctionType
AXX = mybir.AxisListType.X
ds = bass.ds

P = 128
DM = 1024
KT = DM // P
SEQ = 1024
NS = 8
T = SEQ + NS
NC = 3
CW = T // NC
TB = CW // 4
DFF = 2816
FT = DFF // P
NIT = FT // 2
NH = 8
HC = 16
HD = 64
ROT = 16
EPS = 1e-5
PAGE = 128
NPG = 2
NG = 64
ST = 64
L = 8
NB = SEQ // L
PAIRS = NG // 2
PARTS = 4
PP = PAIRS // PARTS
GP = NG // PARTS
KQ = KT // PARTS
NW = 9
NJ, NI = 16, 8
NN = NW + NJ + NI
BW = NS + NB
HW_ = NS + 1 + NB
LAM_INIT = 0.8 - 0.6 * math.exp(-0.3)
TWO_PI = 2.0 * math.pi
MAGIC = 12582912.0
MAGIC12 = 3072.0
C1 = 6.28125
C2 = round((TWO_PI - C1) * 2.0**20) / 2.0**20
C3 = TWO_PI - C1 - C2
SIN_SCALE = 6.283185
N_UNITS = 2 * KT + 2 * (3 * FT) + 3 * KT + KT
SEG1 = 108
U_GLU, U_FFN0 = 0, 2 * KT
U_KVQ = U_FFN0 + 3 * FT
U_O = U_KVQ + 3 * KT
U_FFN1 = U_O + KT
GL0, DN0, OP0 = 3, 8, 6


def build(nc, d):
    ctx = ExitStack()
    with ctx:
        top = [((nc.sbuf_base + 31) // 32) * 32]

        def place(name, shape, dt, at=None):
            size = int(np.prod(shape[1:])) * (2 if dt == BF16 else 4)
            size = (size + 31) // 32 * 32
            if at is None:
                at = top[0]
                top[0] += size
                return nc.alloc_sbuf_tensor_at(name, shape, dt, offset=at)
            off = at[0]
            at[0] += size
            assert at[0] <= at[1], (name, at)
            return nc.alloc_sbuf_tensor_at(name, shape, dt, offset=off)

        def sem(name):
            return ctx.enter_context(nc.semaphore(name))

        X = place("X", [P, KT, T], F32)
        RAW_AT = top[0]
        w_raw = place("w_raw", [P, 4, DM], F32)
        w_hi = place("w_hi", [P, 4, DM], F32R)
        w_lo = place("w_lo", [P, 4, DM], F32R)
        ident = place("ident", [P, P], F32)
        identb = place("identb", [P, P], BF16)
        maskb = place("maskb", [P, P], BF16)
        ones = place("ones", [P, P], F32)
        gains = place("gains", [P, 6, KT], F32)
        lamv = place("lamv", [P, 4, HD], F32)
        lamt = place("lamt", [P, 8], F32)
        gsub = place("gsub", [P, 1], F32)
        eps_t = place("eps_t", [P, 1], F32)
        std = place("std", [P, NC, 4], F32)
        rstd = place("rstd", [P, NC, 4], F32)
        diag = place("diag", [TB, 4, TB], F32)
        sel = place("sel", [P, HC], F32)
        pairsel = place("pairsel", [P, 64], F32)
        evenodd = place("evenodd", [P, 2], F32)
        eye8 = place("eye8", [P, 64], F32)
        ptab = place("ptab", [1, NS * NPG], I32)
        nmx = place("nmx", [P, 2, 2], F32)
        sums = place("sums", [P, 2, 2], F32)
        rinv = place("rinv", [P, 4, 2], F32)
        rho = place("rho", [P, 2, 1], F32)
        oss = place("oss", [P, 64], F32)
        orst = place("orst", [P, 64], F32)
        qS = place("qS", [P, KT, NS], F32)
        kS = place("kS", [P, KT, NS], F32)
        vS = place("vS", [P, NH, NS], F32)
        dsc = place("dsc", [P, 16], F32)
        tmpd = place("tmpd", [P, 72], F32)

        ACT_AT = top[0]
        act_hi = place("act_hi", [P, KT, T], F32R)
        act_lo = place("act_lo", [P, KT, T], F32R)
        HID_AT = top[0]
        hid_hi = place("hid_hi", [P, 2, 2, T], F32R)
        hid_lo = place("hid_lo", [P, 2, 2, T], F32R)
        MISC_AT = top[0]
        END = nc.sbuf_usable_end
        misc = [MISC_AT, END]
        sq = place("sq", [P, 3, CW], F32, misc)
        acc = place("acc", [P, NC, CW], F32, misc)
        tmp = place("tmp", [P, 4, CW], F32, misc)
        R = place("R", [P, T], F32, misc)
        gate = place("gate", [P, NC, CW], F32, misc)
        U = nc.alloc_sbuf_tensor_at("U", [P, KT, T], F32, offset=HID_AT)
        Z = nc.alloc_sbuf_tensor_at("Z", [P, KT, T], F32, offset=HID_AT)
        Y = nc.alloc_sbuf_tensor_at("Y", [P, KT, T], F32, offset=ACT_AT)
        ra = [ACT_AT, HID_AT]
        a_in = place("a_in", [P, 3, PAIRS], F32, ra)
        b_in = place("b_in", [P, 2, PAIRS, 16], F32, ra)
        c_in = place("c_in", [P, 2, PAIRS, 16], F32, ra)
        ncr = place("ncr", [P, PAIRS, 16], F32, ra)
        h0 = place("h0", [P, 2, PAIRS, NS], F32, ra)
        hs = place("hs", [P, 2, PAIRS, NS], F32, ra)
        fin = place("fin", [P, 2, PAIRS, 1], F32, ra)
        d16 = place("d16", [16, NG], F32, ra)
        dI = place("dI", [16, GP, 16], F32, ra)
        nvec = place("nvec", [P, NN], F32, ra)
        sm = place("sm", [P, 16, PAIRS], F32, ra)
        sinT = place("sinT", [P, PAIRS, NN], F32, ra)
        cosT = place("cosT", [P, PAIRS, NN], F32, ra)
        decay = place("decay", [P, PAIRS, NW], F32, ra)
        A_re = place("A_re", [P, PAIRS, NW], F32, ra)
        A_im = place("A_im", [P, PAIRS, NW], F32, ra)
        bbar = place("bbar", [P, 2, 3, PP, 16], F32, ra)
        W_re = place("W_re", [P, PP, L, 16], F32, ra)
        W_im = place("W_im", [P, PP, L, 16], F32, ra)
        G_t = place("G_t", [P, PP, NW, 16], F32, ra)
        CB = place("CB", [P, PP, NI, NJ], F32, ra)
        SB = place("SB", [P, PP, NI, NJ], F32, ra)
        rb = [HID_AT, END]
        assert PP * 2 * P <= KQ * T
        RT = place("RT", [P, PP, 2, P], F32, rb)
        Vp = place("Vp", [P, 2, PP, NB], F32, rb)
        tw = place("tw", [P, 2, 4, NB], F32, rb)
        TM = place("TM", [P, GP, P], F32, rb)
        usp = place("usp", [16, GP, NS], F32, rb)
        zblk = place("zblk", [P, GP, BW], F32, rb)
        rw = [RAW_AT + 16384, ACT_AT]
        G_r = [place(f"G_re{i}", [P, PP, NW, 16], F32, x) for i, x in ((0, rw), (1, ra))]
        G_i = [place(f"G_im{i}", [P, PP, NW, 16], F32, x) for i, x in ((0, rw), (1, ra))]
        H = [place(f"H{i}", [P, 2, PP, HW_], F32, x) for i, x in ((0, rw), (1, rb))]
        ublk = [place(f"ublk{i}", [P, GP, BW], F32, x) for i, x in ((0, rw), (1, rb))]
        bpad = place("bpad", [P, 2, 2, PP, 2, 16], F32, rw)
        assert rw[0] <= RAW_AT + 3 * 16384
        rc = [RAW_AT, RAW_AT + 16384]
        Kc = place("Kc", [16, GP, P], F32, rc)
        CBt = place("CBt", [P, PP, NI, NJ], F32, rc)
        W_t = place("W_t", [P, PP, L, 16], F32, rc)
        rd = [HID_AT, MISC_AT]
        ph = place("ph", [P, PAIRS, NN], F32, rd)
        pl = place("pl", [P, PAIRS, NN], F32, rd)
        re_ = [HID_AT, MISC_AT]
        stage = place("stage", [P, 4, T], F32, re_)
        roped = place("roped", [P, 2, T], F32, re_)
        rtmp = gate[:].rearrange("p n t -> p (n t)")
        cosr = place("cosr", [P, T], F32, re_)
        sinr = place("sinr", [P, T], F32, re_)
        rf = [ACT_AT, HID_AT]
        kh = place("kh", [P, 2, SEQ], F32, rf)
        qz = place("qz", [P, 2, 2, SEQ], F32, rf)
        vT = nc.alloc_sbuf_tensor_at("vT", [P, 2, SEQ], F32, offset=RAW_AT)
        vtok = place("vtok", [P, 2, KT, P], F32, rf)
        prob = place("prob", [P, 2, 2, SEQ], F32, rf)
        wmix = place("wmix", [P, 2, SEQ], F32, rf)
        wT = place("wT", [P, 2, SEQ], F32, rf)
        junk = place("junk", [P, P], F32, rf)
        O = nc.alloc_sbuf_tensor_at("O", [P, NH, KT, P], F32, offset=HID_AT)
        rg = [MISC_AT, END]
        kpg = place("kpg", [P, 2, DM], F32, rg)
        qb = place("qb", [P, 2, DM], F32, rg)
        stok = place("stok", [P, NPG, NS * HC], F32, rg)
        newl = place("newl", [P, NS, HC], F32, rg)
        p2 = place("p2", [P, 2 * P + 1], F32, rg)
        wtok = place("wtok", [P, 3, 64], F32, rg)
        wnew = place("wnew", [P, P], F32, rg)
        oS = nc.alloc_sbuf_tensor_at("oS", [P, NS, NH], F32, offset=HID_AT + NH * KT * P * 4)
        assert HID_AT + (NH * KT * P + NS * NH) * 4 <= MISC_AT
        oS2 = place("oS2", [P, NS, NH], F32, rg)
        qrow = place("qrow", [NS, HC, 8, 8], F32, rg)
        orow = qrow[:].rearrange("b c m j -> b (c m j)")
        wpad = nc.alloc_sbuf_tensor_at("wpad", [P, NPG, NS, NH, NS], F32, offset=RAW_AT + 8192)
        vpg = nc.alloc_sbuf_tensor_at("vpg", [P, 4, DM], F32, offset=MISC_AT)

        pair = [ctx.enter_context(nc.psum_tensor(f"pair{i}", [P, 1024], F32)) for i in range(4)]
        bank = [pair[i // 2][:, (i % 2) * 512:(i % 2) * 512 + 512] for i in range(8)]

        const0_in, const_in = sem("const0_in"), sem("const_in")
        x_in = [sem(f"x_in{n}") for n in range(NC)]
        w_in = [sem(f"w_in{r}") for r in range(4)]
        w_split, w_used = sem("w_split"), sem("w_used")
        w_hi_done = sem("w_hi_done")
        dve_chain, pool_chain, act_chain = sem("dve_chain"), sem("pool_chain"), sem("act_chain")
        nm_sq, nm_add, nm_ss, nm_std, nm_diag = sem("nm_sq"), sem("nm_add"), sem("nm_ss"), sem("nm_std"), sem("nm_diag")
        nm_bc, nm_r = sem("nm_bc"), sem("nm_r")
        at_tmp, at_hi, at_lo = sem("at_tmp"), sem("at_hi"), sem("at_lo")
        u_done, u0_stored, u_stored = sem("u_done"), sem("u0_stored"), sem("u_stored")
        s5_act = sem("s5_act")
        s5_glob = sem("s5_glob")
        s5_small = sem("s5_small")
        s5_zero = sem("s5_zero")
        s5_w, s5_cs, s5_g = sem("s5_w"), sem("s5_cs"), sem("s5_g")
        s5_t, s5_rt, s5_k, s5_kc, s5_kd = (sem(x) for x in ("s5_t", "s5_rt", "s5_k", "s5_kc", "s5_kd"))
        s5_v, s5_vs, s5_vsd, s5_h = (sem(x) for x in ("s5_v", "s5_vs", "s5_vsd", "s5_h"))
        s5_y, s5_gelu = sem("s5_y"), sem("s5_gelu")
        u_in = [sem(f"u_in{i}") for i in range(2)]
        s5_ti = sem("s5_ti")
        z_in = [sem(f"z_in{i}") for i in range(3)]
        t_in, z_out, ssm_out = (sem(x) for x in ("t_in", "z_out", "ssm_out"))
        z_hi, z_lo = sem("z_hi"), sem("z_lo")
        gl_ready, gl_sig, gl_mul, gl_done = (sem(x) for x in ("gl_ready", "gl_sig", "gl_mul", "gl_done"))
        gu_ready, gu_silu, hid_tmp, hid_hi_s, hid_lo_s = (
            sem(x) for x in ("gu_ready", "gu_silu", "hid_tmp", "hid_hi_s", "hid_lo_s"))
        dn_ready, dn_added = sem("dn_ready"), sem("dn_added")
        kv_ready, kv_evicted, kv_roped = sem("kv_ready"), sem("kv_evicted"), sem("kv_roped")
        kv_out = [sem(f"kv_out{i}") for i in range(4)]
        rope_in, rope_out = sem("rope_in"), sem("rope_out")
        lam_done = sem("lam_done")
        hd_in = [sem(f"hd_in{i}") for i in range(2)]
        a_vt, a_v, a_s, a_max, a_exp, a_mix = (sem(x) for x in ("a_vt", "a_v", "a_s", "a_max", "a_exp", "a_mix"))
        a_r, a_tr, a_wt, a_o, a_oa, a_oc = (sem(x) for x in ("a_r", "a_tr", "a_wt", "a_o", "a_oa", "a_oc"))
        on_std, on_w, on_tr, on_hi, on_lo = (sem(x) for x in ("on_std", "on_w", "on_tr", "on_hi", "on_lo"))
        d_smp, d_qt, d_qrow, d_qout = (sem(x) for x in ("d_smp", "d_qt", "d_qrow", "d_qout"))
        kpg_in = [sem(f"kpg_in{i}") for i in range(2)]
        d_mul, d_red = sem("d_mul"), sem("d_red")
        d_pv, d_new, d_s2, d_p2, d_p2n, d_w, d_wc = (
            sem(x) for x in ("d_pv", "d_new", "d_s2", "d_p2", "d_p2n", "d_w", "d_wc"))
        vpg_in = [sem(f"vpg_in{i}") for i in range(4)]
        d_o, d_sq, d_ssq, d_rs, d_fin = (sem(x) for x in ("d_o", "d_sq", "d_ssq", "d_rs", "d_fin"))
        op_ready, op_added = sem("op_ready"), sem("op_added")
        d_wp, d_row, d_ot = sem("d_wp"), sem("d_row"), sem("d_ot")
        q_zero, on_r, on_p = sem("q_zero"), sem("on_r"), sem("on_p")
        d_sc, d_hi, d_lo = sem("d_sc"), sem("d_hi"), sem("d_lo")
        passed = sem("passed")
        y_done, y_out = sem("y_done"), sem("y_out")

        block = ctx.enter_context(nc.Block())
        n_const = [0, 0]
        slots = [(tt % 4, tt in (0, 1, 2 * KT, 2 * KT + 1)) for tt in range(3 * KT)]
        n_out = [16 * sum(1 for s, r in slots if s == x and not r) for x in range(4)]

        def bc(ap, axis, shape):
            return ap.unsqueeze(axis).to_broadcast(shape)

        def cs(n):
            return slice(n * CW, (n + 1) * CW)

        def settle(eng):
            eng.sem_inc(passed, 1)

        class Chain:

            def __init__(self, eng, own, base=0, settle=False):
                self.eng, self.own, self.base, self.n, self.settle = eng, own, base, 0, settle

            def add(self, ins):
                self.n += 1
                ins.then_inc(self.own, 1)

            def sync(self):
                self.eng.wait_ge(self.own, self.base + self.n)
                if self.settle:
                    settle(self.eng)

            def step(self, ins):
                self.add(ins)
                self.sync()

        def attention_steps(eng, step):
            for c in range(3):
                step(c, 0, c)
            with eng.Fori(0, 3) as t:
                for c in range(3, 19):
                    step(t * 16 + c, t * 2 + c // 8, c)
            for c in range(51, 64):
                step(c, c // 8, c)

        @block.sync
        def _(sp):
            def const(dst, src, late=1):
                n_const[late] += 16
                sp.dma_start(dst, src).then_inc(const_in if late else const0_in, 16)

            const(a_in[:], d["s_abc"], 0)
            const(nvec[:], d["c_nvec"], 0)
            const(ones[:], d["c_ones"], 0)
            const(b_in[:], d["s_b"], 0)
            for n in range(NC):
                sp.dma_start(X[:, :, cs(n)], d["x_t"].rearrange("(k p) t -> p k t", p=P)[:, :, cs(n)]
                             ).then_inc(x_in[n], 16)
            const(ident[:], d["c_ident"])
            const(gains[:], d["gains"])
            const(c_in[:], d["s_c"])
            const(h0[:], d["s_h0"])
            const(d16[:], d["s_d"])
            const(identb[:], d["c_identb"])
            const(maskb[:], d["c_maskb"])
            for j in range(4):
                const(lamv[:, j, :], d["lam"][j:j + 1, :].to_broadcast([P, HD]))
            const(gsub[:], d["subln"])
            const(sel[:], d["c_sel"])
            const(pairsel[:], d["c_pairsel"])
            const(evenodd[:], d["c_evenodd"])
            const(eye8[:], d["c_eye8"])
            const(ptab[:], d["page_table"])

            u_t = d["u"].rearrange("(k p) t -> p k t", p=P)
            sp.wait_ge(u_done, NC)
            sp.dma_start(u_t[:, 0:KQ], U[:, 0:KQ]).then_inc(u0_stored, 16)
            sp.wait_ge(u0_stored, 16)
            sp.wait_ge(s5_zero, 1)
            u_v = d["u"].rearrange("(q g h) t -> q h g t", q=PARTS, g=GP)
            z_v = d["z"].rearrange("(q g h) t -> q h g t", q=PARTS, g=GP)

            def load_inputs(q):
                ub = ublk[q % 2]
                if q >= 2:
                    sp.wait_ge(s5_y, 8 * (q - 1))
                for n in range(L):
                    s = L - 1 - n
                    sp.dma_start(ub[16 * n:16 * n + 16, :, NS:BW], u_v[q, :, :, s * NB:(s + 1) * NB]
                                 ).then_inc(u_in[q % 2], 16)
                sp.dma_start(ub[P - 16:P, :, 0:NS], u_v[q, :, :, SEQ:T]).then_inc(u_in[q % 2], 16)
                if q == 0:
                    sp.wait_ge(u_done, NC + 1)
                    sp.dma_start(u_t[:, KQ:KT], U[:, KQ:KT]).then_inc(u_stored, 16)
                    sp.wait_ge(u_stored, 16)
                else:
                    sp.wait_ge(s5_vs, 4 * q)
                sp.dma_start(usp[:], u_v[q, :, :, SEQ:T]).then_inc(u_in[q % 2], 16)

            load_inputs(0)
            sp.wait_ge(s5_zero, 2)
            load_inputs(1)
            for q in range(PARTS):
                sp.wait_ge(s5_kd, q + 1)
                if q:
                    sp.wait_ge(s5_y, 8 * q)
                for n in range(L):
                    sp.dma_start(TM[16 * n:16 * n + 16, :, (L - 1 - n) * 16:P],
                                 Kc[:, :, 0:(n + 1) * 16]).then_inc(t_in, 16)
                if q == PARTS - 1:
                    sp.wait_ge(t_in, 128 * PARTS)
                    sp.wait_ge(s5_cs, PARTS)
                    for r in range(4):
                        sp.dma_start(w_raw[:, r, :], d["w"][r]).then_inc(w_in[r], 16)
                if q + 2 < PARTS:
                    load_inputs(q + 2)
                if q == PARTS - 1:
                    sp.wait_ge(s5_h, PARTS)
                    sp.dma_start(d["ssm_p"], fin[:]).then_inc(ssm_out, 16)
                    sp.dma_start(d["ssm_s"], hs[:]).then_inc(ssm_out, 16)
                    sp.wait_ge(z_out, 144 * (PARTS - 1))
                    sp.dma_start(Z[:, 0:4], d["z"].rearrange("(k p) t -> p k t", p=P)[:, 0:4]).then_inc(z_in[0], 16)
                sp.wait_ge(s5_gelu, 8 * q + 8)
                for s in range(L):
                    sp.dma_start(z_v[q, :, :, s * NB:(s + 1) * NB], zblk[16 * s:16 * s + 16, :, NS:BW]
                                 ).then_inc(z_out, 16)
                sp.dma_start(z_v[q, :, :, SEQ:T], zblk[0:16, :, 0:NS]).then_inc(z_out, 16)
            sp.wait_ge(z_out, PARTS * 9 * 16)
            for x in (1, 2):
                k = slice(2 * x + 2, 2 * x + 4)
                sp.dma_start(Z[:, k], d["z"].rearrange("(k p) t -> p k t", p=P)[:, k]).then_inc(z_in[x], 16)

            def load_units(first, last):
                with sp.Fori(0, (last - first) // 4) as b:
                    for r in range(4):
                        sp.wait_ge(w_split, b * 4 + (first + r - 3))
                        sp.dma_start(w_raw[:, r, :],
                                     d["w"][ds(b * 4 + (first + r), 1)].rearrange("o p n -> (o p) n")
                                     ).then_inc(w_in[r], 16)

            load_units(4, SEG1)

            for x in range(4):
                sp.wait_ge(kv_out[x], n_out[x])
            sp.wait_ge(rope_out, 64)
            sp.wait_ge(kv_evicted, 6 * 3 * KT // 2)
            sp.wait_ge(w_split, SEG1)
            k_v = d["kt"].rearrange("m (h c j) t -> h c m j t", h=NH, c=2)
            q_v = d["qt"].rearrange("m (h c j) t -> h c m j t", h=NH, c=2)

            def load_head(h, par):
                for c in range(2):
                    rows = slice(64 * c, 64 * c + 64)
                    for dst, src in ((kh[rows, par, :], k_v), (qz[rows, par, c, :], q_v)):
                        sp.dma_start(dst,
                                     src[ds(h, 1), c, :, :, 0:SEQ].rearrange("o m j t -> (o m) j t")
                                     ).then_inc(hd_in[par], 16)
                sp.dma_start(vT[:, par, :], d["vt"][ds(h, 1), :, 0:SEQ].rearrange("o e t -> (o e) t")
                             ).then_inc(hd_in[par], 16)

            def load_keys(b, par):
                sp.wait_ge(d_red, b * 2 + 1)
                sp.dma_start(qb[:, par, :], d["qrow"][ds(b, 1), :].to_broadcast([P, DM])
                             ).then_inc(kpg_in[0], 16)
                for j in range(NPG):
                    page = sp.value_load(ptab[0:1, ds(b * 2 + j, 1)], min_val=0, max_val=d["n_pages"] - 1)
                    sp.dma_start(kpg[:, j, :], d["cache_k"][ds(page, 1)].rearrange("o p n -> (o p) n")
                                 ).then_inc(kpg_in[j], 16)

            for par in range(2):
                load_head(par, par)
            sp.wait_ge(d_qrow, 1)
            sp.dma_start(d["qrow"], qrow[:].rearrange("b c m j -> b (c m j)")).then_inc(d_qout, 16)
            sp.wait_ge(d_qout, 16)
            with sp.Fori(0, NH // 2 - 1) as hh:
                for par in range(2):
                    load_keys(hh * 2 + par, par)
                    sp.wait_ge(a_o, hh * 16 + (8 * par + 8))
                    load_head(hh * 2 + (par + 2), par)
            for par in range(2):
                load_keys(NS - 2 + par, par)

            sp.wait_ge(d_red, 2 * NS + 1)

            def load_values(b, par):
                for j in range(NPG):
                    page = sp.value_load(ptab[0:1, ds(b * 2 + j, 1)], min_val=0, max_val=d["n_pages"] - 1)
                    sp.dma_start(vpg[:, 2 * par + j, :], d["cache_v"][ds(page, 1)].rearrange("o p n -> (o p) n")
                                 ).then_inc(vpg_in[2 * par + j], 16)

            def load_unit(u):
                sp.dma_start(w_raw[:, u % 4, :], d["w"][u]).then_inc(w_in[u % 4], 16)

            for par in range(2):
                load_values(par, par)
            sp.wait_ge(a_vt, NH)
            load_unit(SEG1)
            load_unit(SEG1 + 1)
            for b in range(2, NS):
                sp.wait_ge(d_o, b - 1)
                load_values(b, b % 2)
            sp.wait_ge(d_o, NS)
            load_unit(SEG1 + 2)
            load_unit(SEG1 + 3)
            load_units(SEG1 + 4, N_UNITS)
            for n in range(NC):
                sp.wait_ge(y_done, 8 * n + 8)
                sp.dma_start(d["y_t"].rearrange("(k p) t -> p k t", p=P)[:, :, cs(n)], Y[:, :, cs(n)]
                             ).then_inc(y_out, 16)
            sp.wait_ge(y_out, 16 * NC)
            sp.wait_ge(ssm_out, 32)

        @block.gpsimd
        def _(pool):
            g = nc.gpsimd

            def split(u, r, q, first):
                pool.wait_ge(w_in[r], q * 16 + 16)
                if not first:
                    pool.wait_ge(w_used, u - 2)
                    settle(pool)
                g.tensor_copy(w_hi[:, r, :], w_raw[:, r, :]).then_inc(w_hi_done, 1)
                pool.wait_ge(w_hi_done, u + 1)
                settle(pool)
                g.tensor_tensor(w_lo[:, r, :], w_raw[:, r, :], w_hi[:, r, :].bitcast(F32), ALU.subtract
                                ).then_inc(w_split, 1)

            def split_units(first, last):
                with pool.Fori(first // 4, last // 4) as b:
                    for r in range(4):
                        split(b * 4 + r, r, b, False)

            pool.wait_ge(s5_glob, 1)
            S4 = [P, PP, NI, NJ]
            G4 = [P, PP, NW, 16]
            c = Chain(pool, pool_chain)
            for q in range(PARTS):
                pr = slice(q * PP, q * PP + PP)
                G_re, G_im = G_r[q % 2], G_i[q % 2]
                if q:
                    pool.wait_ge(s5_h, q)

                def outer(dst, hi_t, lo_t):
                    return g.tensor_tensor(dst[:], bc(hi_t[:, pr, NW + NJ:NN], 3, S4),
                                           bc(lo_t[:, pr, NW:NW + NJ], 2, S4), ALU.mult)
                c.add(outer(CB, cosT, cosT))
                c.step(outer(CBt, sinT, sinT))
                c.step(g.tensor_tensor(CB[:], CB[:], CBt[:], ALU.subtract))
                c.add(outer(SB, sinT, cosT))
                c.step(outer(CBt, cosT, sinT))
                g.tensor_tensor(SB[:], SB[:], CBt[:], ALU.add).then_inc(s5_cs, 1)
                if q >= 2:
                    pool.wait_ge(s5_y, 8 * (q - 1))

                def cpow(dst, cc, aa):
                    return g.tensor_tensor(dst[:], bc(cc, 2, G4), bc(aa[:, pr, :], 3, G4), ALU.mult)
                c.add(cpow(G_re, c_in[:, 0, pr, :], A_re))
                c.step(cpow(G_t, c_in[:, 1, pr, :], A_im))
                g.tensor_tensor(G_re[:], G_re[:], G_t[:], ALU.subtract).then_inc(s5_g, 1)
                pool.wait_ge(s5_g, 2 * q + 1)
                c.add(cpow(G_im, ncr[:, pr, :], A_im))
                c.add(cpow(G_t, c_in[:, 1, pr, :], A_re))
                c.sync()
                g.tensor_tensor(G_im[:], G_im[:], G_t[:], ALU.subtract).then_inc(s5_g, 1)
                pool.wait_ge(s5_g, 2 * q + 2)
                if q == 0:
                    g.memset(ublk[0][:], 0.0).then_inc(s5_zero, 1)
                    pool.wait_ge(u_stored, 16)
                    c.step(g.memset(ublk[1][:], 0.0))
                    g.memset(TM[:], 0.0).then_inc(s5_zero, 1)
            pool.wait_ge(s5_y, 8 * (PARTS - 1))
            pool.wait_ge(s5_k, 4 * PARTS)
            for r in range(4):
                split(r, r, 0, True)
            split_units(4, SEG1)
            pool.wait_ge(kv_ready, 9 * KT // 2)
            pool.wait_ge(w_split, SEG1)
            g.memset(qz[64:P, :, 0, :], 0.0).then_inc(q_zero, 1)
            pool.wait_ge(q_zero, 1)
            g.memset(qz[0:64, :, 1, :], 0.0).then_inc(q_zero, 1)
            pool.wait_ge(q_zero, 2)
            with pool.Fori(0, NS // 2) as bb:
                for par in range(2):
                    for j in range(NPG):
                        if j == 0:
                            pool.wait_ge(kpg_in[0], bb * 64 + (32 * par + 32))
                        else:
                            pool.wait_ge(kpg_in[1], bb * 32 + (16 * par + 16))
                        settle(pool)
                        g.tensor_tensor(kpg[:, j, :], kpg[:, j, :], qb[:, par, :], ALU.mult).then_inc(d_mul, 1)
            pool.wait_ge(on_r, 1)
            for h in range(6):
                g.tensor_tensor(O[:, h], O[:, h], bc(orst[:, 8 * h:8 * h + 8], 2, [P, KT, P]), ALU.mult
                                ).then_inc(on_p, 1)
            split_units(SEG1, N_UNITS)

        @block.scalar
        def _(act):
            a = nc.scalar

            def square(v, i, k, n):
                if v or i >= 3:
                    act.wait_ge(nm_add, i + (24 * v - 2))
                a.activation(sq[:, n if v == 1 else i % 3, :], X[:, k, cs(n)], ACT.Square).then_inc(nm_sq, 1)

            def root(v, n):
                act.wait_ge(nm_ss, 3 * v + n + 1)
                a.activation(std[0:TB, n, :], bank[7][0:TB, 4 * n:4 * n + 4], ACT.Sqrt,
                             scale=1.0 / DM, bias=eps_t[0:TB, :]).then_inc(nm_std, 1)

            def row(v, n):
                act.wait_ge(nm_bc, 3 * v + n + 1)
                a.activation(R[:, cs(n)], bank[6][:, 0:CW], ACT.Copy).then_inc(nm_r, 1)

            def high(w, first, last):
                for i in range(first, last):
                    n, k = i // KT, i % KT
                    act.wait_ge(at_tmp, 24 * w + i + 1)
                    a.activation(act_hi[:, k, cs(n)], tmp[:, i % 4, :], ACT.Copy).then_inc(at_hi, 1)

            def norm_after(v, w, chunk):
                chunk(0)
                root(v, 0)
                chunk(1)
                row(v, 0)
                high(w, 0, 4)
                root(v, 1)
                high(w, 4, 8)
                chunk(2)
                row(v, 1)
                high(w, 8, 16)
                root(v, 2)
                row(v, 2)
                high(w, 16, 24)

            act.wait_ge(const0_in, n_const[0])
            a.activation(sm[:, 0, :], a_in[:, 2, :], ACT.Exp).then_inc(s5_act, 1)
            act.wait_ge(s5_small, 1)
            a.activation(decay[:], decay[:], ACT.Exp).then_inc(s5_act, 1)
            act.wait_ge(s5_small, 2)
            a.activation(sinT[:], sinT[:], ACT.Sin, scale=SIN_SCALE)
            a.activation(cosT[:], cosT[:], ACT.Sin, scale=SIN_SCALE).then_inc(s5_act, 1)
            act.wait_ge(s5_small, 3)
            for n in range(NC):
                act.wait_ge(x_in[n], 16)
                for k in range(KT):
                    square(0, n * KT + k, k, n)
                root(0, n)
                if n:
                    row(0, n - 1)
            row(0, 2)
            act.wait_ge(u0_stored, 16)

            def turned(q):
                if q:
                    act.wait_ge(s5_vs, 4 * q)
                for r in range(4):
                    act.wait_ge(s5_t, 4 * q + r + 1)
                    a.activation(RT[:, 2 * r:2 * r + 2, :, :].rearrange("p a c n -> p (a c n)"),
                                 bank[4 + r], ACT.Copy).then_inc(s5_rt, 1)

            def kernel_out(q):
                if q:
                    act.wait_ge(t_in, 128 * q)
                for r in range(4):
                    act.wait_ge(s5_k, 4 * q + r + 1)
                    a.activation(Kc[:].rearrange("p (a y) n -> p a y n", y=2)[:, 4 * (r // 2):4 * (r // 2) + 4, r % 2, :],
                                 bank[4 + r][0:16, :].rearrange("p (a n) -> p a n", a=4), ACT.Copy
                                 ).then_inc(s5_kc, 1)

            def gelu(q):
                if q:
                    act.wait_ge(z_out, 144 * q)
                for r in range(8):
                    act.wait_ge(s5_y, 8 * q + r + 1)
                    a.activation(zblk[:].rearrange("p (a y) n -> p a y n", y=2)[:, 2 * (r // 2):2 * (r // 2) + 2, r % 2, :],
                                 bank[4 + r % 4][:, 0:2 * BW].rearrange("p (a n) -> p a n", a=2),
                                 ACT.Gelu_apprx_tanh).then_inc(s5_gelu, 1)

            turned(0)
            kernel_out(0)
            for q in range(PARTS):
                if q + 1 < PARTS:
                    turned(q + 1)
                gelu(q)
                if q + 1 < PARTS:
                    kernel_out(q + 1)
            act.wait_ge(ssm_out, 32)
            for k in range(KT):
                act.wait_ge(z_in[max(k // 2 - 1, 0)], 16)
                a.activation(act_hi[:, k, 0:SEQ].rearrange("p (b s) -> p b s", s=L),
                             Z[:, k, 0:SEQ].rearrange("p (s b) -> p b s", s=L), ACT.Copy)
                a.activation(act_hi[:, k, SEQ:T], Z[:, k, SEQ:T], ACT.Copy).then_inc(z_hi, 1)
            def glu(m, n):
                act.wait_ge(gl_ready, m * 3 + (n + 1))
                a.activation(gate[:, n, :], bank[2 * n + 1][:, 0:CW], ACT.Sigmoid).then_inc(gl_sig, 1)
                act.wait_ge(gl_done, m * 3 + (GL0 + n + 1))
                act.wait_ge(nm_add, m * 3 + (24 + n - 2))
                settle(act)
                a.activation(sq[:, n, :], X[:, ds(m, 1), cs(n)].rearrange("p o t -> p (o t)"), ACT.Square
                             ).then_inc(nm_sq, 1)

            with act.Fori(0, KT - 1) as m:
                for n in range(NC):
                    glu(m, n)

            def ffn_gate(f, tile, base):
                t = tile % 2
                par = (tile // 2) % 2
                for n in range(NC):
                    i = base + (3 * tile + n)
                    act.wait_ge(gu_ready, i + 1)
                    a.activation(gate[:, n, :], bank[2 * n][:, 0:CW], ACT.Silu).then_inc(gu_silu, 1)
                    act.wait_ge(hid_tmp, i + 1)
                    a.activation(hid_hi[:, par, t, cs(n)], tmp[:, n, :], ACT.Copy).then_inc(hid_hi_s, 1)

            def ffn(f):
                for t in range(2):
                    ffn_gate(f, t, 66 * f)
                with act.Fori(0, (NIT - 1) // 2) as b:
                    for t in range(4):
                        ffn_gate(f, t + 2, b * 12 + 66 * f)

            def norm_after_down(f, v, w):
                for q in range(24):
                    act.wait_ge(dn_added, DN0 + 240 + 264 * f + q + 1)
                    square(v, q, q % 8, q // 8)
                    if q == 12:
                        root(v, 0)
                    if q == 15:
                        row(v, 0)
                    if q == 20:
                        root(v, 1)
                    if q >= 16 and w:
                        high(w, q - 16, q - 15)
                row(v, 1)
                if w:
                    high(w, 8, 16)
                root(v, 2)
                row(v, 2)
                if w:
                    high(w, 16, 24)

            norm_after(1, 0, lambda n: glu(KT - 1, n))
            ffn(0)
            norm_after_down(0, 2, 1)
            act.dma_start(cosr[:], d["c_cos"]).then_inc(rope_in, 16)
            act.dma_start(sinr[:], d["c_sin"]).then_inc(rope_in, 16)
            seen = [0, 0, 0, 0]
            for tt in range(3 * KT):
                if tt % 2 == 0:
                    p = tt // 2
                    if p >= 2:
                        act.wait_ge(d_smp, tt - 2)
                        for x in range(2):
                            act.wait_ge(kv_out[slots[tt + x][0]], seen[slots[tt + x][0]])
                    for n in range(NC):
                        act.wait_ge(kv_ready, 3 * p + n + 1)
                        for x in range(2):
                            a.activation(stage[:, slots[tt + x][0], cs(n)], bank[2 * n + x][:, 0:CW], ACT.Copy,
                                         scale=HD ** -0.5 if tt >= 2 * KT else 1.0).then_inc(kv_evicted, 1)
                        if p == KT - 1:
                            high(2, n * KT, n * KT + KT)
                slot, rot = slots[tt]
                which, m = (d["kt"], d["vt"], d["qt"])[tt // KT], tt % KT
                if not rot:
                    act.wait_ge(kv_evicted, 6 * (tt // 2) + 6)
                    act.dma_start(which[m], stage[:, slot, :]).then_inc(kv_out[slot], 16)
                    seen[slot] += 16
                if m == 2 and tt // KT != 1:
                    act.wait_ge(kv_roped, 1 + tt // (2 * KT))
                    for x in range(2):
                        act.dma_start(which[x], roped[:, x, :]).then_inc(rope_out, 16)

            act.wait_ge(d_qt, 1)
            a.activation(qrow[:].rearrange("b c m j -> b m c j"),
                         pair[3][0:NS, :].rearrange("b (m c j) -> b m c j", m=8, c=HC), ACT.Copy
                         ).then_inc(d_qrow, 1)
            act.wait_ge(lam_done, 1)
            a.activation(lamt[:, 2:4], lamt[:, 0:2], ACT.Exp).then_inc(act_chain, 1)

            def v_rows(h, par):
                act.wait_ge(a_vt, h + 1)
                a.activation(vtok[:, par].rearrange("p b e -> p (b e)"), pair[2][:], ACT.Copy).then_inc(a_v, 1)

            def evict(v, c):
                act.wait_ge(a_tr, v + 1)
                if c:
                    act.wait_ge(a_o, v - 1)
                n = (c % 8 + 1) * P
                a.activation(wT[:, c % 2, 0:n], pair[2][:, 0:n], ACT.Copy).then_inc(a_wt, 1)

            def stats(v, h, c):
                act.wait_ge(a_oa, v + 1)
                act.wait_ge(a_oc, v + 1)
                a.activation(junk[:], O[:, ds(h, 1), c % 8, :].rearrange("p o e -> p (o e)"), ACT.Square,
                             accum_out=oss[:, ds(v, 1)]).then_inc(a_oa, 1)

            def step(v, h, c):
                n = (c % 8 + 1) * P
                for x in range(2):
                    act.wait_ge(a_max, v * 2 + (x + 1))
                    if c >= 2:
                        act.wait_ge(a_mix, v - 1)
                    a.activation(prob[:, c % 2, x, 0:n], pair[x][:, 0:n], ACT.Exp, bias=nmx[:, c % 2, x:x + 1],
                                 accum_out=sums[:, c % 2, x:x + 1]).then_inc(a_exp, 1)
                if c >= 2:
                    evict(v - 2, c - 2)
                if c % 8 == 7 and c != 63:
                    v_rows(h + 1, (c // 8 + 1) % 2)
                if c >= 3:
                    stats(v - 3, h if c % 8 >= 3 else h - 1, c - 3)
                if c == 51:
                    rms(0, 48)

            def rms(first, last):
                act.wait_ge(a_oa, last + 1)
                a.activation(orst[:, first:last], oss[:, first:last], ACT.Sqrt, scale=1.0 / P, bias=eps_t[:]
                             ).then_inc(on_std, 1)

            act.sem_inc(a_oa, 1)
            v_rows(0, 0)
            attention_steps(act, step)
            evict(62, 62)
            evict(63, 63)
            stats(61, 7, 61)
            stats(62, 7, 62)
            stats(63, 7, 63)
            act.wait_ge(d_s2, 1)
            a.activation(p2[:], bank[4][:, 0:2 * P + 1], ACT.Exp, bias=dsc[:, 0:1], accum_out=dsc[:, 1:2]
                         ).then_inc(d_p2, 1)

            def head_high(h):
                act.wait_ge(on_tr, h + 1)
                a.activation(act_hi[:, h, 0:SEQ], pair[h % 2][:], ACT.Copy, scale=gsub[:]).then_inc(on_hi, 1)

            head_high(0)
            act.wait_ge(d_w, 1)
            a.activation(wtok[:].rearrange("p a b -> p (a b)"), bank[5][:, 0:192], ACT.Copy).then_inc(d_wc, 1)
            head_high(1)
            rms(48, 64)
            for h in range(2, NH):
                head_high(h)
            act.wait_ge(d_o, NS)
            a.activation(orow, pair[2][0:NS, :], ACT.Copy).then_inc(d_row, 1)
            act.wait_ge(d_ssq, 1)
            a.activation(oS2[:].rearrange("p b h -> p (b h)"), bank[7][:, 0:64], ACT.Sqrt, scale=1.0 / P,
                         bias=eps_t[:]).then_inc(d_rs, 1)
            act.wait_ge(d_fin, 1)
            a.activation(act_hi[:, :, SEQ:T].rearrange("p h b -> p b h"), oS[:], ACT.Copy).then_inc(d_hi, 1)

            def squares_of_pair(p, n):
                for x in range(2):
                    act.wait_ge(op_added, OP0 + 6 * p + 2 * n + x + 1)
                    square(3, 6 * p + 2 * n + x, 2 * p + x, n)

            for p in range(KT // 2 - 1):
                for n in range(NC):
                    squares_of_pair(p, n)
            norm_after(3, 3, lambda n: squares_of_pair(KT // 2 - 1, n))
            ffn(1)
            norm_after_down(1, 4, 0)

        @block.vector
        def _(dve):
            v_ = nc.vector

            def tt(out, a, b, op):
                return v_.tensor_tensor(out, a, b, op)

            def add_square(v, i, n, wait=None):
                dve.wait_ge(nm_sq, i + (24 * v + 1))
                if wait is not None:
                    dve.wait_ge(nm_add, wait)
                slot = n if v == 1 else i % 3
                tt(acc[:, n, :], acc[:, n, :], sq[:, slot, :], ALU.add).then_inc(nm_add, 1)

            def clear_sums(v):
                if v:
                    dve.wait_ge(nm_ss, 3 * v)
                c.step(v_.memset(acc[:], 0.0))

            def diagonal(v, n):
                dve.wait_ge(nm_std, 3 * v + n + 1)
                c.step(v_.reciprocal(rstd[0:TB, n, :], std[0:TB, n, :]))
                if v or n:
                    dve.wait_ge(nm_bc, 3 * v + n)
                for j in range(4):
                    last = v_.tensor_scalar(diag[:, j, :], ident[0:TB, 0:TB], rstd[0:TB, n, j:j + 1],
                                            None, ALU.mult)
                last.then_inc(nm_diag, 1)

            def scaled(out, k, n, g, sl=None, view=lambda x: x):
                cols = cs(n) if sl is None else sl
                return v_.scalar_tensor_tensor(out, view(X[:, k, cols]), gains[:, g, k:k + 1], view(R[:, cols]),
                                               ALU.mult, ALU.mult)

            def normalise(v, w, g, first, last):
                def low(i):
                    dve.wait_ge(at_hi, 24 * w + i + 1)
                    n, k = i // KT, i % KT
                    tt(act_lo[:, k, cs(n)], tmp[:, i % 4, :], act_hi[:, k, cs(n)].bitcast(F32), ALU.subtract
                       ).then_inc(at_lo, 1)
                for i in range(first, last):
                    n, k = i // KT, i % KT
                    dve.wait_ge(nm_r, 3 * v + n + 1)
                    if w or i >= 4:
                        dve.wait_ge(at_lo, 24 * w + max(i - 3, 0))
                    scaled(tmp[:, i % 4, :], k, n, g).then_inc(at_tmp, 1)
                    if k >= 2:
                        low(i - 2)
                    if k == KT - 1:
                        low(i - 1)
                        low(i)

            def norm_after(v, w, g, chunk):
                chunk(0)
                diagonal(v, 0)
                chunk(1)
                normalise(v, w, g, 0, 4)
                diagonal(v, 1)
                normalise(v, w, g, 4, 8)
                chunk(2)
                normalise(v, w, g, 8, 16)
                diagonal(v, 2)
                normalise(v, w, g, 16, 24)

            def norm_after_down(f, v, normal):
                clear_sums(v)
                base, i0 = 240 + 264 * f, 24 * v

                def square(q):
                    add_square(v, q, q // 8, i0 + q if q % 8 else None)
                for q in range(24):
                    dve.wait_ge(dn_ready, base + (q + 1))
                    x = X[:, q % 8, cs(q // 8)]
                    tt(x, x, bank[q % 6][:, 0:CW], ALU.add).then_inc(dn_added, 1)
                    if q:
                        square(q - 1)
                    if q == 13:
                        diagonal(v, 0)
                    if q >= 16:
                        normal(q - 16, q - 15)
                    if q == 21:
                        diagonal(v, 1)
                square(23)
                normal(8, 16)
                diagonal(v, 2)
                normal(16, 24)

            c = Chain(dve, dve_chain)
            dve.sem_inc(d_red, 1)
            dve.sem_inc(gl_done, GL0)
            dve.sem_inc(dn_added, DN0)
            dve.sem_inc(op_added, OP0)
            dve.wait_ge(const0_in, n_const[0])
            v_.memset(eps_t[:], EPS)
            dve.wait_ge(s5_act, 1)
            dt, lam, ang, qq, rr, tq, th, tl, den, nr, fre, fim, t1, t2 = (sm[:, i, :] for i in range(14))
            a_re, a_im = a_in[:, 0, :], a_in[:, 1, :]
            c.add(tt(lam, dt, a_re, ALU.mult))
            c.step(tt(ang, dt, a_im, ALU.mult))
            S9, SN = [P, PAIRS, NW], [P, PAIRS, NN]
            tt(decay[:], bc(lam, 2, S9), bc(nvec[:, 0:NW], 1, S9), ALU.mult).then_inc(s5_small, 1)
            c.step(v_.tensor_scalar(qq, ang, 1.0 / TWO_PI, MAGIC, ALU.mult, ALU.add))
            c.step(v_.tensor_scalar(qq, qq, MAGIC, None, ALU.subtract))
            c.step(v_.scalar_tensor_tensor(rr, qq, -C1, ang, ALU.mult, ALU.add))
            c.step(v_.scalar_tensor_tensor(rr, qq, -C2, rr, ALU.mult, ALU.add))
            c.step(v_.scalar_tensor_tensor(rr, qq, -C3, rr, ALU.mult, ALU.add))
            c.step(v_.tensor_scalar(tq, rr, 1.0 / TWO_PI, None, ALU.mult))
            c.step(v_.tensor_scalar(th, tq, MAGIC12, MAGIC12, ALU.add, ALU.subtract))
            c.step(tt(tl, tq, th, ALU.subtract))
            c.add(tt(ph[:], bc(th, 2, SN), bc(nvec[:], 1, SN), ALU.mult))
            c.step(tt(pl[:], bc(tl, 2, SN), bc(nvec[:], 1, SN), ALU.mult))
            c.step(v_.tensor_scalar(cosT[:], ph[:], MAGIC, MAGIC, ALU.add, ALU.subtract))
            c.step(tt(ph[:], ph[:], cosT[:], ALU.subtract))
            c.step(tt(ph[:], ph[:], pl[:], ALU.add))
            c.step(v_.tensor_scalar(cosT[:], ph[:], MAGIC, MAGIC, ALU.add, ALU.subtract))
            c.add(tt(sinT[:], ph[:], cosT[:], ALU.subtract))
            c.step(v_.tensor_scalar(pl[:], ph[:], 0.25, None, ALU.add))
            c.step(v_.tensor_scalar(cosT[:], pl[:], MAGIC, MAGIC, ALU.add, ALU.subtract))
            tt(cosT[:], pl[:], cosT[:], ALU.subtract).then_inc(s5_small, 1)
            dve.wait_ge(s5_act, 3)
            c.add(tt(A_re[:], decay[:], cosT[:, :, 0:NW], ALU.mult))
            c.add(tt(A_im[:], decay[:], sinT[:, :, 0:NW], ALU.mult))
            c.add(tt(t1, a_re, a_re, ALU.mult))
            c.step(tt(t2, a_im, a_im, ALU.mult))
            c.step(tt(den, t1, t2, ALU.add))
            c.add(v_.reciprocal(den, den))
            c.step(v_.tensor_scalar(nr, A_re[:, :, 1], 1.0, None, ALU.subtract))
            c.add(tt(t1, nr, a_re, ALU.mult))
            c.step(tt(t2, A_im[:, :, 1], a_im, ALU.mult))
            c.step(tt(fre, t1, t2, ALU.add))
            c.add(tt(fre, fre, den, ALU.mult))
            c.add(tt(t1, A_im[:, :, 1], a_re, ALU.mult))
            c.step(tt(t2, nr, a_im, ALU.mult))
            c.step(tt(fim, t1, t2, ALU.subtract))
            c.step(tt(fim, fim, den, ALU.mult))
            dve.wait_ge(const_in, n_const[1])
            S8 = [P, PAIRS, NS]
            s8 = ph[:].rearrange("p a n -> p (a n)")[:, 0:PAIRS * NS].rearrange("p (a n) -> p a n", n=NS)
            a1r, a1i = bc(A_re[:, :, 1], 2, S8), bc(A_im[:, :, 1], 2, S8)
            c.add(tt(hs[:, 0], a1r, h0[:, 0], ALU.mult))
            c.step(tt(s8, a1i, h0[:, 1], ALU.mult))
            c.step(tt(hs[:, 0], hs[:, 0], s8, ALU.subtract))
            c.add(tt(hs[:, 1], a1r, h0[:, 1], ALU.mult))
            c.step(tt(s8, a1i, h0[:, 0], ALU.mult))
            c.add(tt(hs[:, 1], hs[:, 1], s8, ALU.add))
            v_.tensor_scalar(ncr[:], c_in[:, 0], -1.0, None, ALU.mult).then_inc(s5_glob, 1)
            lp = tmp[:, 0, 0:2 * HD].rearrange("p (a b) -> p a b", a=2)
            lv = lamv[:].rearrange("p (a b) n -> p a b n", a=2)
            c.step(tt(lp, lv[:, :, 0, :], lv[:, :, 1, :], ALU.mult))
            c.add(v_.tensor_scalar(gsub[:], gsub[:], 1.0 - LAM_INIT, None, ALU.mult))
            c.step(v_.reduce_sum(lamt[:, 0:2], lp, axis=AXX))
            v_.memset(dsc[:], 0.0).then_inc(lam_done, 1)
            v_.memset(rstd[:], 0.0).then_inc(s5_small, 1)

            def inputs(n):
                dve.wait_ge(nm_r, n + 1)
                b0, b1 = n * CW // L, min((n + 1) * CW, SEQ) // L
                for k in range(KT):
                    last = v_.scalar_tensor_tensor(
                        U[:, k, 0:SEQ].rearrange("p (s b) -> p b s", s=L)[:, b0:b1, :],
                        X[:, k, b0 * L:b1 * L].rearrange("p (b s) -> p b s", s=L), gains[:, 0, k:k + 1],
                        R[:, b0 * L:b1 * L].rearrange("p (b s) -> p b s", s=L), ALU.mult, ALU.mult)
                    if n == NC - 1:
                        last = scaled(U[:, k, SEQ:T], k, n, 0, slice(SEQ, T))
                        if k == KQ - 1:
                            last.then_inc(u_done, 1)
                last.then_inc(u_done, 1)

            c.add(v_.memset(bpad[:], 0.0))
            c.step(v_.memset(acc[:], 0.0))
            for n in range(NC):
                for k in range(KT):
                    add_square(0, n * KT + k, n, n * KT + k if k else None)
                diagonal(0, n)
                if n:
                    inputs(n - 1)
            inputs(2)
            W4, B3, D3 = [P, PP, L, 16], [P, PP, 16], [16, GP, 16]

            def weights(q):
                pr, bb = slice(q * PP, q * PP + PP), bbar[:, q % 2]
                if q >= 2:
                    dve.wait_ge(s5_k, 4 * (q - 1))
                fr, fi = bc(fre[:, pr], 2, B3), bc(fim[:, pr], 2, B3)
                br, bi = b_in[:, 0, pr, :], b_in[:, 1, pr, :]
                c.add(tt(bb[:, 0], fr, br, ALU.mult))
                c.step(tt(bb[:, 2], fi, bi, ALU.mult))
                c.step(tt(bb[:, 0], bb[:, 0], bb[:, 2], ALU.subtract))
                c.add(tt(bb[:, 1], fr, bi, ALU.mult))
                c.step(tt(bb[:, 2], fi, br, ALU.mult))
                c.step(tt(bb[:, 1], bb[:, 1], bb[:, 2], ALU.add))
                if q:
                    dve.wait_ge(s5_t, 4 * q)
                ar, ai = bc(A_re[:, pr, 0:L], 3, W4), bc(A_im[:, pr, 0:L], 3, W4)
                b_r, b_i = bc(bb[:, 0], 2, W4), bc(bb[:, 1], 2, W4)
                c.add(tt(W_re[:], ar, b_r, ALU.mult))
                c.step(tt(W_t[:], ai, b_i, ALU.mult))
                c.step(tt(W_re[:], W_re[:], W_t[:], ALU.subtract))
                c.add(tt(W_im[:], ar, b_i, ALU.mult))
                c.step(tt(W_t[:], ai, b_r, ALU.mult))
                c.step(tt(W_im[:], W_im[:], W_t[:], ALU.add))
                for g2 in range(2):
                    rows = slice(64 * g2, 64 * g2 + 64)
                    last = v_.tensor_copy(bpad[rows, q % 2, :, :, g2, :], bb[rows, 0:2])
                last.then_inc(s5_w, 1)
                dve.wait_ge(s5_w, q + 1)

            def states(q):
                pr, Hq = slice(q * PP, q * PP + PP), H[q % 2]
                for r in range(4):
                    dve.wait_ge(s5_vs, 4 * q + r + 1)
                    for x in range(2):
                        st = hs[:, x, q * PP + 2 * r:q * PP + 2 * r + 2, :]
                        last = tt(st, st, bank[4 + r][:, 0:4 * NS].rearrange("p (a x b) -> p a x b", a=2, x=2)[:, :, x, :],
                                  ALU.add)
                    last.then_inc(s5_vsd, 1)
                dve.wait_ge(s5_cs, q + 1)
                for m in range(2):
                    dve.wait_ge(s5_v, 2 * q + m + 1)
                    cb = CB[:, 4 * m:4 * m + 4].rearrange("p a i j -> p (a i j)")
                    sb_ = SB[:, 4 * m:4 * m + 4].rearrange("p a i j -> p (a i j)")
                    v0, v1 = (Vp[:, x, 4 * m:4 * m + 4, :].rearrange("p a b -> p (a b)") for x in range(2))
                    w0, w1 = (tw[:, x].rearrange("p a b -> p (a b)") for x in range(2))
                    c.add(tt(v0, bank[2 * m], cb, ALU.mult))
                    c.add(tt(w0, bank[2 * m + 1], sb_, ALU.mult))
                    c.add(tt(v1, bank[2 * m + 1], cb, ALU.mult))
                    tt(w1, bank[2 * m], sb_, ALU.mult).then_inc(s5_ti, 1)
                    dve.wait_ge(s5_ti, 2 * q + m + 1)
                    c.add(tt(v0, v0, w0, ALU.add))
                    c.step(tt(v1, v1, w1, ALU.subtract))
                for pp in range(PP):
                    for x in range(2):
                        row = Vp[:, x, pp, :]
                        c.add(v_.tensor_tensor_scan(row, decay[:, q * PP + pp, NW - 1:NW].to_broadcast([P, NB]),
                                                    row, 0.0, ALU.mult, ALU.add))
                c.sync()
                if q >= 2:
                    dve.wait_ge(s5_y, 8 * (q - 1))
                for m in range(2):
                    cb = CB[:, 4 * m:4 * m + 4].rearrange("p a i j -> p a (i j)")
                    sb_ = SB[:, 4 * m:4 * m + 4].rearrange("p a i j -> p a (i j)")
                    g0, g1 = Vp[:, 0, 4 * m:4 * m + 4, :], Vp[:, 1, 4 * m:4 * m + 4, :]
                    h_r, h_i = (Hq[:, x, 4 * m:4 * m + 4, NS + 1:HW_] for x in range(2))
                    c.add(tt(h_r, g0, cb, ALU.mult))
                    c.add(tt(tw[:, 0], g1, sb_, ALU.mult))
                    c.add(tt(h_i, g0, sb_, ALU.mult))
                    c.step(tt(tw[:, 1], g1, cb, ALU.mult))
                    c.add(tt(h_r, h_r, tw[:, 0], ALU.subtract))
                    c.step(tt(h_i, h_i, tw[:, 1], ALU.add))
                for x in range(2):
                    v_.tensor_copy(Hq[:, x, :, 0:NS], h0[:, x, pr, :])
                    v_.memset(Hq[:, x, :, NS:NS + 1], 0.0)
                    last = v_.tensor_copy(fin[:, x, pr, :], Hq[:, x, :, HW_ - 1:HW_])
                last.then_inc(s5_h, 1)

            def add_direct(q):
                dve.wait_ge(s5_kc, 4 * q + 4)
                c.step(tt(dI[:], bc(ident[0:16, 0:16], 1, D3), bc(d16[:, q * GP:q * GP + GP], 2, D3), ALU.mult))
                tt(Kc[:, :, 0:16], Kc[:, :, 0:16], dI[:], ALU.add).then_inc(s5_kd, 1)

            weights(0)
            weights(1)
            dve.wait_ge(u_stored, 16)
            for q in range(PARTS):
                states(q)
                add_direct(q)
                if q + 2 < PARTS:
                    weights(q + 2)

            for k in range(KT):
                dve.wait_ge(z_hi, k + 1)
                tt(act_lo[:, k, 0:SEQ].rearrange("p (b s) -> p b s", s=L),
                   Z[:, k, 0:SEQ].rearrange("p (s b) -> p b s", s=L),
                   act_hi[:, k, 0:SEQ].bitcast(F32).rearrange("p (b s) -> p b s", s=L), ALU.subtract)
                tt(act_lo[:, k, SEQ:T], Z[:, k, SEQ:T], act_hi[:, k, SEQ:T].bitcast(F32), ALU.subtract
                   ).then_inc(z_lo, 1)
            def glu(m, n, last=False):
                dve.wait_ge(gl_sig, m * 3 + (n + 1))
                if last and n == 2:
                    dve.wait_ge(at_lo, KT)
                tt(tmp[:, n, :], bank[2 * n][:, 0:CW], gate[:, n, :], ALU.mult).then_inc(gl_mul, 1)
                dve.wait_ge(gl_mul, m * 3 + (n + 1))
                x = X[:, ds(m, 1), cs(n)].rearrange("p o t -> p (o t)")
                tt(x, x, tmp[:, n, :], ALU.add).then_inc(gl_done, 1)
                dve.wait_ge(nm_add, m * 3 + (24 + n - 2))
                add_square(1, m * 3 + n, n)

            clear_sums(1)
            with dve.Fori(0, KT - 1) as m:
                for n in range(NC):
                    glu(m, n)

            def hidden(tile, base):
                for n in range(NC):
                    i = base + (3 * tile + n)
                    if tile:
                        dve.wait_ge(hid_lo_s, i - 2)
                    dve.wait_ge(gu_silu, i + 1)
                    tt(tmp[:, n, :], gate[:, n, :], bank[2 * n + 1][:, 0:CW], ALU.mult).then_inc(hid_tmp, 1)
                    dve.wait_ge(hid_hi_s, i + 1)
                    h = (slice(None), (tile // 2) % 2, tile % 2, cs(n))
                    tt(hid_lo[h], tmp[:, n, :], hid_hi[h].bitcast(F32), ALU.subtract).then_inc(hid_lo_s, 1)

            def down(base):
                for q in range(24):
                    dve.wait_ge(dn_ready, base + (q + 1))
                    x = X[:, q % 8, cs(q // 8)]
                    tt(x, x, bank[(6 + q) % 8][:, 0:CW], ALU.add).then_inc(dn_added, 1)

            def ffn(f, v, normal):
                hidden(0, 66 * f)
                hidden(1, 66 * f)
                with dve.Fori(0, (NIT - 1) // 2) as b:
                    for half in range(2):
                        hidden(2 + 2 * half, b * 12 + 66 * f)
                        hidden(3 + 2 * half, b * 12 + 66 * f)
                        down(b * 48 + (24 * half + 264 * f))
                norm_after_down(f, v, normal)

            norm_after(1, 0, 2, lambda n: glu(KT - 1, n, True))
            ffn(0, 2, lambda first, last: normalise(2, 1, 4, first, last))
            for kvq_tile in range(3 * KT):
                if kvq_tile == 2 * KT - 2:
                    for n in range(NC):
                        dve.wait_ge(kv_ready, 3 * KT - 3 + n + 1)
                        normalise(2, 2, 1, n * KT, n * KT + KT)
                dve.wait_ge(kv_evicted, 6 * (kvq_tile // 2) + 6)
                m, keep = kvq_tile % KT, (kS, vS, qS)[kvq_tile // KT]
                slot = slots[kvq_tile][0]
                if slots[kvq_tile][1]:
                    if m == 0:
                        continue
                    x1, x2 = stage[:, slots[kvq_tile - 1][0], :], stage[:, slot, :]
                    dve.wait_ge(rope_in, 32)
                    dve.wait_ge(rope_out, 32 * (kvq_tile // (2 * KT)))
                    c.add(tt(roped[:, 0, :], x1, cosr[:], ALU.mult))
                    c.step(tt(rtmp[:], x2, sinr[:], ALU.mult))
                    c.step(tt(roped[:, 0, :], roped[:, 0, :], rtmp[:], ALU.subtract))
                    c.add(tt(roped[:, 1, :], x2, cosr[:], ALU.mult))
                    c.step(tt(rtmp[:], x1, sinr[:], ALU.mult))
                    c.step(tt(roped[:, 1, :], roped[:, 1, :], rtmp[:], ALU.add))
                    v_.tensor_copy(keep[:, 0:2, :], roped[:, :, SEQ:T]).then_inc(d_smp, 2)
                    v_.memset(dsc[:, 2:3], 0.0).then_inc(kv_roped, 1)
                else:
                    v_.tensor_copy(keep[:, m, :], stage[:, slot, SEQ:T]).then_inc(d_smp, 1)

            dve.wait_ge(act_chain, 1)
            c.step(tt(lamt[:, 4:5], lamt[:, 3:4], lamt[:, 2:3], ALU.subtract))
            c.step(v_.tensor_scalar(lamt[:, 4:5], lamt[:, 4:5], LAM_INIT, None, ALU.subtract))
            neglam = lamt[:, 4:5]

            def row_max(v, c_, x):
                dve.wait_ge(a_s, v * 2 + (x + 1))
                n = (c_ % 8 + 1) * P
                v_.tensor_reduce(nmx[:, c_ % 2, x:x + 1], pair[x][:, 0:n], axis=AXX, op=ALU.max, negate=True
                                 ).then_inc(a_max, 1)

            def out_copy(v, h, c_):
                dve.wait_ge(a_o, v + 1)
                v_.tensor_scalar(O[:, ds(h, 1), c_ % 8, :].rearrange("p o e -> p (o e)"), bank[6 + c_ % 2][:, 0:P],
                                 rinv[:, c_ % 4, 0:1], None, ALU.mult).then_inc(a_oc, 1)

            def key_sums(b, j):
                dve.wait_ge(d_mul, b * 2 + (j + 1))
                v_.reduce_sum(stok[:, j, ds(b * HC, HC)], kpg[:, j, :].rearrange("p (c d) -> p c d", d=HD),
                              axis=AXX).then_inc(d_red, 1)

            def step(v, h, c_):
                n = (c_ % 8 + 1) * P
                if c_ >= 3:
                    out_copy(v - 3, h if c_ % 8 >= 3 else h - 1, c_ - 3)
                if c_ != 63:
                    row_max(v + 1, c_ + 1, 0)
                dve.wait_ge(a_exp, v * 2 + 2)
                v_.reciprocal(rinv[:, c_ % 4, :], sums[:, c_ % 2, :]).then_inc(a_r, 1)
                dve.wait_ge(a_r, v * 2 + 1)
                v_.scalar_tensor_tensor(rho[:, c_ % 2, :], sums[:, c_ % 2, 0:1], neglam, rinv[:, c_ % 4, 1:2],
                                        ALU.mult, ALU.mult).then_inc(a_r, 1)
                dve.wait_ge(a_r, v * 2 + 2)
                if c_ >= 2:
                    dve.wait_ge(a_tr, v - 1)
                v_.scalar_tensor_tensor(wmix[:, c_ % 2, 0:n], prob[:, c_ % 2, 1, 0:n], rho[:, c_ % 2, :],
                                        prob[:, c_ % 2, 0, 0:n], ALU.mult, ALU.add).then_inc(a_mix, 1)
                if c_ != 63:
                    row_max(v + 1, c_ + 1, 1)
                if c_ == 52:
                    dve.wait_ge(on_std, 1)
                    v_.reciprocal(orst[:, 0:48], orst[:, 0:48]).then_inc(on_r, 1)
                if c_ % 8 in (1, 2) and 3 <= c_ <= 50:
                    key_sums(h - 1, c_ % 8 - 1)
                if c_ in (53, 54):
                    key_sums(NS - 2, c_ - 53)
                if c_ in (57, 58):
                    key_sums(NS - 1, c_ - 57)

            row_max(0, 0, 0)
            row_max(0, 0, 1)
            attention_steps(dve, step)
            out_copy(61, 7, 61)
            out_copy(62, 7, 62)
            out_copy(63, 7, 63)
            dve.wait_ge(d_smp, 24)
            pr_ = tmpd[:, 0:64].rearrange("p (m b) -> p m b", m=8)
            c.step(tt(pr_, qS[:], kS[:], ALU.mult))
            c.step(v_.reduce_sum(tmpd[:, 64:72], tmpd[:, 0:64].rearrange("p (m b) -> p b m", m=8), axis=AXX))
            N3 = [P, NS, HC]
            tt(newl[:], bc(tmpd[:, 64:72], 2, N3), bc(sel[:], 1, N3), ALU.mult).then_inc(d_new, 1)
            dve.wait_ge(d_sc, 1)
            v_.tensor_reduce(dsc[:, 0:1], bank[4][:, 0:2 * P + 1], axis=AXX, op=ALU.max, negate=True).then_inc(d_s2, 1)
            dve.wait_ge(d_p2, 1)
            c.add(v_.reciprocal(dsc[:, 3:4], dsc[:, 1:2]))
            c.step(v_.scalar_tensor_tensor(dsc[:, 4:5], evenodd[:, 1:2], neglam, evenodd[:, 0:1], ALU.mult, ALU.add))
            c.step(tt(dsc[:, 5:6], dsc[:, 3:4], dsc[:, 4:5], ALU.mult))
            c.step(v_.tensor_scalar(p2[:], p2[:], dsc[:, 5:6], None, ALU.mult))
            v_.tensor_scalar(wnew[:], ones[:], p2[:, 2 * P:2 * P + 1], None, ALU.mult).then_inc(d_p2n, 1)

            def head_low(h):
                dve.wait_ge(on_hi, h + 1)
                v_.scalar_tensor_tensor(act_lo[:, h, 0:SEQ], pair[h % 2][:], gsub[:],
                                        act_hi[:, h, 0:SEQ].bitcast(F32), ALU.mult, ALU.subtract).then_inc(on_lo, 1)

            head_low(0)
            dve.wait_ge(d_wc, 1)
            for j in range(NPG):
                W5 = [P, NS, NH, NS]
                last = tt(wpad[:, j], bc(wtok[:, j, :].rearrange("p (b h) -> p b h", b=NS), 3, W5),
                          bc(eye8[:].rearrange("p (b m) -> p b m", b=NS), 2, W5), ALU.mult)
            last.then_inc(d_wp, 1)
            head_low(1)
            dve.wait_ge(on_std, 2)
            c.step(v_.reciprocal(orst[:, 48:64], orst[:, 48:64]))
            for h in (6, 7):
                tt(O[:, h], O[:, h], bc(orst[:, 8 * h:8 * h + 8], 2, [P, KT, P]), ALU.mult).then_inc(on_w, 1)
            for h in range(2, NH):
                head_low(h)
            c.step(tt(oS[:], vS[:].rearrange("p h b -> p b h"),
                      wtok[:, 2, :].rearrange("p (b h) -> p b h", b=NS), ALU.mult))
            dve.wait_ge(d_ot, 1)
            c.step(tt(oS[:], oS[:], bank[6][:, 0:64].rearrange("p (h b) -> p b h", b=NS), ALU.add))
            tt(oS2[:], oS[:], oS[:], ALU.mult).then_inc(d_sq, 1)
            dve.wait_ge(d_rs, 1)
            c.step(v_.reciprocal(oS2[:], oS2[:]))
            c.step(tt(oS[:], oS[:], oS2[:], ALU.mult))
            v_.tensor_scalar(oS[:], oS[:], gsub[:], None, ALU.mult).then_inc(d_fin, 1)
            dve.wait_ge(d_hi, 1)
            tt(act_lo[:, :, SEQ:T].rearrange("p h b -> p b h"), oS[:],
               act_hi[:, :, SEQ:T].bitcast(F32).rearrange("p h b -> p b h"), ALU.subtract).then_inc(d_lo, 1)
            clear_sums(3)

            def out_pair(p, n):
                dve.wait_ge(op_ready, 3 * p + n + 1)
                for x in range(2):
                    o = X[:, 2 * p + x, cs(n)]
                    tt(o, o, bank[2 * n + x][:, 0:CW], ALU.add).then_inc(op_added, 1)
                for x in range(2):
                    i = 6 * p + 2 * n + x
                    dve.wait_ge(nm_add, 72 + i)
                    add_square(3, i, n)

            for p in range(KT // 2 - 1):
                for n in range(NC):
                    out_pair(p, n)
            norm_after(3, 3, 3, lambda n: out_pair(KT // 2 - 1, n))

            def final(first, last):
                for i in range(first, last):
                    n, k = i // KT, i % KT
                    dve.wait_ge(nm_r, 3 * 4 + n + 1)
                    scaled(Y[:, k, cs(n)], k, n, 5).then_inc(y_done, 1)

            ffn(1, 4, final)

        @block.tensor
        def _(pe):
            t_ = nc.tensor

            def mm(out, lhsT, rhs, start, stop):
                return t_.matmul(out, lhsT, rhs, start=start, stop=stop)

            def sums(v, n, items):
                pe.wait_ge(nm_add, 24 * v + items)
                if v or n:
                    pe.wait_ge(nm_std, 3 * v + n)
                for j in range(4):
                    last = mm(bank[7][0:TB, 4 * n + j:4 * n + j + 1], acc[:, n, j * TB:(j + 1) * TB],
                              ones[:, 0:1], True, True)
                last.then_inc(nm_ss, 1)

            def spread(v, n):
                pe.wait_ge(nm_diag, 3 * v + n + 1)
                if v or n:
                    pe.wait_ge(nm_r, 3 * v + n)
                for j in range(4):
                    last = mm(bank[6][:, j * TB:(j + 1) * TB], ones[0:TB, :], diag[:, j, :], True, True)
                last.then_inc(nm_bc, 1)

            def norm_beside(v, items):
                return ({(1, 0): lambda: sums(v, 0, items[0]), (1, 1): lambda: spread(v, 0),
                         (2, 0): lambda: sums(v, 1, items[1]), (2, 1): lambda: spread(v, 1)},
                        {(0, 0): lambda: sums(v, 2, 24), (0, 1): lambda: spread(v, 2)})

            def dense(out, slot, n, rhs_hi, rhs_lo, first=False):
                for k in range(KT):
                    wh, wl = (w[:, slot, k * P:(k + 1) * P] for w in (w_hi, w_lo))
                    ah, al = rhs_hi[:, k, cs(n)], rhs_lo[:, k, cs(n)]
                    ins = mm(out, wh, ah, k == 0, False)
                    if first and k == 0:
                        ins.then_inc(w_used, 1)
                    mm(out, wh, al, False, False)
                    last = mm(out, wl, ah, False, k == KT - 1)
                return last

            def pair_of_units(n, u, ready, beside={}, release=True):
                last = dense(bank[2 * n][:, 0:CW], u % 4, n, act_hi, act_lo, n == 0 and release)
                if n == NC - 1:
                    last.then_inc(w_used, 1)
                if (n, 0) in beside:
                    beside[n, 0]()
                dense(bank[2 * n + 1][:, 0:CW], (u + 1) % 4, n, act_hi, act_lo).then_inc(ready, 1)
                if (n, 1) in beside:
                    beside[n, 1]()

            pe.wait_ge(const0_in, n_const[0])
            pe.wait_ge(const_in, n_const[1])
            for n in range(NC):
                sums(0, n, KT * n + KT)
                spread(0, n)

            def inputs(q):
                pe.wait_ge(s5_w, q + 1)
                if q:
                    pe.wait_ge(s5_kc, 4 * q)
                for r in range(4):
                    for x in range(4):
                        src = (W_re, W_im)[x % 2][:, 2 * r + x // 2].rearrange("p n h -> p (n h)")
                        last = t_.transpose(bank[4 + r][:, x * P:(x + 1) * P], src, ident[:])
                    last.then_inc(s5_t, 1)
                pe.wait_ge(u_in[q % 2], 160 * (q // 2 + 1))
                pe.wait_ge(s5_rt, 4 * q + 4)
                if q:
                    pe.wait_ge(s5_ti, 2 * q)
                for m in range(2):
                    for pp in range(4):
                        for x in range(2):
                            for g2 in range(2):
                                pi = 4 * m + pp
                                last = mm(bank[2 * m + x][64 * g2:64 * g2 + 64, pp * NB:(pp + 1) * NB],
                                          RT[:, pi, x, 64 * g2:64 * g2 + 64], ublk[q % 2][:, 2 * pi + g2, NS:BW],
                                          True, True)
                    last.then_inc(s5_v, 1)
                for r in range(4):
                    for y in range(2):
                        for x in range(2):
                            for g2 in range(2):
                                pi = 2 * r + y
                                last = mm(bank[4 + r][64 * g2:64 * g2 + 64, (2 * y + x) * NS:(2 * y + x + 1) * NS],
                                          RT[0:16, pi, x, 64 * g2:64 * g2 + 64], usp[:, 2 * pi + g2, :], True, True)
                    last.then_inc(s5_vs, 1)

            def kernels(q):
                G_re, G_im = G_r[q % 2], G_i[q % 2]
                pe.wait_ge(s5_g, 2 * q + 2)
                for r in range(4):
                    if q:
                        pe.wait_ge(s5_gelu, 8 * (q - 1) + r + 5)
                    else:
                        pe.wait_ge(s5_vsd, r + 1)
                    for x in range(4):
                        pi, g2 = 4 * (r // 2) + x, r % 2
                        out = bank[4 + r][0:16, x * P:(x + 1) * P]
                        mm(out, bpad[:, q % 2, 0, pi, g2, :], G_re[:, pi, 0:L, :].rearrange("p n h -> p (n h)"), True, False)
                        last = mm(out, bpad[:, q % 2, 1, pi, g2, :], G_im[:, pi, 0:L, :].rearrange("p n h -> p (n h)"),
                                  False, True)
                    last.then_inc(s5_k, 1)

            def outputs_s5(q):
                G_re, G_im, Hq = G_r[q % 2], G_i[q % 2], H[q % 2]
                pe.wait_ge(s5_h, q + 1)
                pe.wait_ge(t_in, 128 * q + 128)
                if q + 1 < PARTS:
                    pe.wait_ge(s5_vsd, 4 * q + 8)
                for r in range(8):
                    if r >= 4:
                        pe.wait_ge(s5_gelu, 8 * q + r - 3)
                    for x in range(2):
                        pi, g2 = 2 * (r // 2) + x, r % 2
                        rows = slice(64 * g2, 64 * g2 + 64)
                        out = bank[4 + r % 4][:, x * BW:(x + 1) * BW]
                        mm(out, G_re[rows, pi, 1:NW, :].rearrange("p n h -> p (n h)"), Hq[rows, 0, pi, 0:BW], True, False)
                        mm(out, G_im[rows, pi, 1:NW, :].rearrange("p n h -> p (n h)"), Hq[rows, 1, pi, 0:BW], False, False)
                        last = mm(out, TM[:, 2 * pi + g2, :], ublk[q % 2][:, 2 * pi + g2, :], False, True)
                    last.then_inc(s5_y, 1)

            inputs(0)
            kernels(0)
            for q in range(PARTS):
                if q + 1 < PARTS:
                    inputs(q + 1)
                outputs_s5(q)
                if q + 1 < PARTS:
                    kernels(q + 1)

            pe.wait_ge(z_lo, KT)

            def glu(i, half, beside={}):
                pe.wait_ge(w_split, i * 4 + (2 * half + 2))
                for n in range(NC):
                    pe.wait_ge(gl_done, i * 6 + (GL0 + 3 * half - 3 + n + 1))
                    pair_of_units(n, 2 * half, gl_ready, beside)

            with pe.Fori(0, KT // 2 - 1) as i:
                for half in range(2):
                    glu(i, half)
            glu(KT // 2 - 1, 0)
            last_chunks, first_chunks = norm_beside(1, (22, 23))
            glu(KT // 2 - 1, 1, last_chunks)

            def ffn(f, w, first_chunks, v):
                u0, hb, db = (U_FFN0, U_FFN1)[f], 66 * f, DN0 + 264 * f

                def gate_up(b, u, tile, spare, beside={}):
                    pe.wait_ge(w_split, b * 12 + (u + 2))
                    for n in range(NC):
                        if tile == 0:
                            pe.wait_ge(at_lo, 24 * w + 8 * n + 8)
                        else:
                            pe.wait_ge(hid_tmp, b * 12 + (hb + 3 * tile - 3 + n + 1))
                        if spare is not None:
                            pe.wait_ge(dn_added, b * 48 + (db + spare(n)))
                        pair_of_units(n, u, gu_ready, beside)

                def down(b, u, i):
                    pe.wait_ge(w_split, b * 12 + (u + 2))
                    for q in range(24):
                        n, j = q // 8, q % 8
                        if j == 0:
                            pe.wait_ge(hid_lo_s, b * 12 + (hb + 6 * i + 3 + n + 1))
                        if q >= 8:
                            pe.wait_ge(dn_added, b * 48 + (db + 24 * i + q - 7))
                        elif q >= 2:
                            pe.wait_ge(hid_tmp, b * 12 + (hb + 3 * (2 * i + 3) + (q - 2) // 2 + 1))
                        down_tile(bank[(6 + q) % 8][:, 0:CW], u, i, q)

                def down_tile(out, u, i, q):
                    n, j = q // 8, q % 8
                    for t in range(2):
                        wh, wl = (x[:, (u + t) % 4, j * P:(j + 1) * P] for x in (w_hi, w_lo))
                        hh, hl = (x[:, i % 2, t, cs(n)] for x in (hid_hi, hid_lo))
                        ins = mm(out, wh, hh, t == 0, False)
                        if q == 0 and t == 0:
                            ins.then_inc(w_used, 1)
                        mm(out, wh, hl, False, False)
                        last = mm(out, wl, hh, False, t == 1)
                        if q == 23 and t == 0:
                            last.then_inc(w_used, 1)
                    last.then_inc(dn_ready, 1)

                def down_last(u, i):
                    pe.wait_ge(w_split, u + 2)
                    for q in range(24):
                        if q % 8 == 0:
                            pe.wait_ge(hid_lo_s, hb + 6 * i + 3 + q // 8 + 1)
                        pe.wait_ge(dn_added, db + 24 * i + q - 5)
                        down_tile(bank[q % 6][:, 0:CW], u, i, q)
                        if q == 11:
                            sums(v, 0, 8)
                        if q == 15:
                            spread(v, 0)
                        if q == 19:
                            sums(v, 1, 16)
                        if q == 23:
                            spread(v, 1)

                for t in range(2):
                    gate_up(0, u0 + 2 * t, t, None, first_chunks if t == 0 else {})
                with pe.Fori(0, (NIT - 1) // 2) as b:
                    for half in range(2):
                        u = u0 + 4 + 6 * half
                        for t in range(2):
                            spare = (lambda n: 24 * half - 4 + 2 * n)
                            gate_up(b, u + 2 * t, 2 + 2 * half + t, spare if t == 0 else None)
                        down(b, u + 4, half)
                down_last(u0 + 4 + 60, NIT - 1)

            ffn(0, 0, first_chunks, 2)

            def projections(b, x, w=0, beside={}):
                pe.wait_ge(w_split, b * 4 + (U_KVQ + x + 2))
                for n in range(NC):
                    if w:
                        pe.wait_ge(at_lo, 24 * w + 8 * n + 8)
                    if x >= 2:
                        pe.wait_ge(kv_evicted, b * 12 + (3 * (x - 2) + 2 * n + 2))
                    pair_of_units(n, U_KVQ + x, kv_ready, beside)

            pe.wait_ge(dn_added, DN0 + 264)
            projections(0, 0, 1, {(0, 0): lambda: sums(2, 2, 24), (0, 1): lambda: spread(2, 2)})
            with pe.Fori(0, 3) as b:
                for x in (2, 4):
                    projections(b, x)
            for x in (14, 16, 18, 20, 22):
                projections(0, x, 2 if x == 16 else 0)
            pe.wait_ge(d_smp, 3 * KT)
            for m in range(KT):
                last = t_.transpose(pair[3][0:NS, m * P:(m + 1) * P], qS[:, m, :], ident[:])
                if m == 0:
                    last.then_inc(w_used, 1)
            last.then_inc(d_qt, 1)

            def values(v, h, c):
                par = (c // 8) % 2
                pe.wait_ge(hd_in[par], v * 5 + (80 * (c // 16 + 1) - 5 * c))
                for kb in range(KT):
                    last = t_.transpose(pair[2][:, kb * P:(kb + 1) * P], vT[:, par, kb * P:(kb + 1) * P], ident[:])
                last.then_inc(a_vt, 1)

            def scores(v, c, x):
                i, par = c % 8, (c // 8) % 2
                if c % 8 == 0:
                    pe.wait_ge(hd_in[par], v * 5 + (80 * (c // 16 + 1) - 5 * c))
                if c:
                    pe.wait_ge(a_exp, v * 2 + (x - 1))
                q = qz[:, par, x, i * P:(i + 1) * P]
                n = (i + 1) * P
                for at in range(0, n, 512):
                    end = min(at + 512, n)
                    last = mm(pair[x][:, at:end], q, kh[:, par, at:end], True, end < n)
                last = mm(pair[x][:, n - P:n], identb[:], maskb[:], False, True)
                last.then_inc(a_s, 1)

            def outputs(v, h, c):
                pe.wait_ge(a_wt, v + 1)
                pe.wait_ge(a_v, h + 1)
                if c >= 2:
                    pe.wait_ge(a_oc, v - 1)
                for kb in range(c % 8 + 1):
                    last = mm(bank[6 + c % 2][:, 0:P], wT[:, c % 2, kb * P:(kb + 1) * P],
                              vtok[:, (c // 8) % 2, kb, :], kb == 0, kb == c % 8)
                last.then_inc(a_o, 1)

            def turn(v, h, c):
                pe.wait_ge(a_mix, v + 1)
                if c:
                    pe.wait_ge(a_wt, v)
                pe.wait_ge(a_v, h)
                for kb in range(c % 8 + 1):
                    last = t_.transpose(pair[2][:, kb * P:(kb + 1) * P], wmix[:, c % 2, kb * P:(kb + 1) * P],
                                        ident[:])
                last.then_inc(a_tr, 1)

            def step(v, h, c):
                if c != 63:
                    scores(v + 1, c + 1, 0)
                    scores(v + 1, c + 1, 1)
                if c >= 2:
                    outputs(v - 2, h if c % 8 >= 2 else h - 1, c - 2)
                if c % 8 == 7 and c != 63:
                    values(v + 1, h + 1, c + 1)
                if c >= 1:
                    turn(v - 1, h + (2 if c % 8 == 7 and c != 63 else 1), c - 1)

            pe.wait_ge(kv_evicted, 9 * KT)
            pe.wait_ge(q_zero, 2)
            values(0, 0, 0)
            scores(0, 0, 0)
            scores(0, 0, 1)
            pe.wait_ge(d_qrow, 1)
            attention_steps(pe, step)
            outputs(62, 7, 62)
            turn(63, NH, 63)
            outputs(63, 7, 63)

            pe.wait_ge(d_red, 2 * NS + 1)
            pe.wait_ge(d_new, 1)
            for j in range(NPG):
                t_.transpose(bank[4][:, j * P:(j + 1) * P], stok[:, j, :], ident[:])
            mm(bank[4][:, 2 * P:2 * P + 1], newl[:].rearrange("p b c -> p (b c)"), ones[:, 0:1], True, True
               ).then_inc(d_sc, 1)

            def head(h):
                if h < 6:
                    pe.wait_ge(on_p, h + 1)
                else:
                    pe.wait_ge(on_w, h - 5)
                if h >= 2:
                    pe.wait_ge(on_lo, h - 1)
                for i in range(KT):
                    last = t_.transpose(pair[h % 2][:, i * P:(i + 1) * P], O[:, h, i, :], ident[:])
                last.then_inc(on_tr, 1)

            def sample_values(b):
                for j in range(NPG):
                    pe.wait_ge(vpg_in[2 * (b % 2) + j], 16 * (b // 2) + 16)
                    for h in range(NH):
                        last = mm(pair[2][0:NS, h * P:(h + 1) * P], wpad[:, j, b, h, :],
                                  vpg[:, 2 * (b % 2) + j, h * P:(h + 1) * P],
                                  b == 0 and j == 0 and h % 4 == 0, b == NS - 1 and j == NPG - 1 and h % 4 == 3)
                last.then_inc(d_o, 1)

            head(0)
            head(1)
            pe.wait_ge(d_p2n, 1)
            for j in range(NPG):
                mm(bank[5][:, j * 64:(j + 1) * 64], p2[:, j * P:(j + 1) * P], pairsel[:], True, True)
            mm(bank[5][:, 128:192], wnew[:], pairsel[:], True, True).then_inc(d_w, 1)
            pe.wait_ge(d_wp, 1)
            for b in range(NS):
                sample_values(b)
                if b + 2 < NH:
                    head(b + 2)
            pe.wait_ge(d_row, 1)
            for h in range(NH):
                last = t_.transpose(bank[6][:, h * NS:(h + 1) * NS], orow[:, h * P:(h + 1) * P], ident[0:NS, 0:NS])
            last.then_inc(d_ot, 1)
            pe.wait_ge(d_sq, 1)
            mm(bank[7][:, 0:64], ones[:], oS2[:].rearrange("p b h -> p (b h)"), True, True).then_inc(d_ssq, 1)

            pe.wait_ge(on_lo, NH)
            pe.wait_ge(d_lo, 1)
            last_chunks, first_chunks = norm_beside(3, (20, 22))
            for p in range(KT // 2):
                pe.wait_ge(w_split, U_O + 2 * p + 2)
                for n in range(NC):
                    pe.wait_ge(op_added, OP0 + 6 * (p - 1) + 2 * n + 2)
                    pair_of_units(n, U_O + 2 * p, op_ready, last_chunks if p == KT // 2 - 1 else {}, p > 0)
            ffn(1, 3, first_chunks, 4)
            sums(4, 2, 24)
            spread(4, 2)


def constants():
    f = np.float32
    nvec = np.concatenate([np.arange(NW), L * np.arange(NJ), L * NJ * np.arange(NI)]).astype(f)
    p = np.arange(P)
    inv = (f(500000.0) ** (-np.arange(0, ROT, 2, dtype=f) / f(ROT))).astype(f)
    pos = np.concatenate([np.arange(SEQ), np.full(NS, NPG * PAGE)]).astype(f)
    ang = (pos[None, :] * inv[:, None]).astype(f).astype(np.float64)
    rows = p % 8
    return {
        "c_nvec": np.tile(nvec, (P, 1)),
        "c_ones": np.ones((P, P), f),
        "c_ident": np.eye(P, dtype=f),
        "c_identb": np.eye(P, dtype=f).astype(mybir.dt.np(BF16)),
        "c_maskb": np.where(p[None, :] > p[:, None], f(-1e30), f(0)).astype(mybir.dt.np(BF16)),
        "c_sel": (p[:, None] // 8 == np.arange(HC)[None, :]).astype(f),
        "c_pairsel": (((p // HC) * NH + (p % HC) // 2)[:, None] == np.arange(64)[None, :]).astype(f),
        "c_evenodd": np.stack([p % 2 == 0, p % 2 == 1], 1).astype(f),
        "c_eye8": np.tile(np.eye(NS, dtype=f).reshape(1, 64), (P, 1)),
        "c_cos": np.cos(ang).astype(f)[rows],
        "c_sin": np.sin(ang).astype(f)[rows],
    }


def weight_stream(glu_a, glu_b, w_k, w_v, w_q, w_o, gate, up, down):
    def tiles(w):
        return w.reshape(KT, P, -1, P).transpose(2, 1, 0, 3).reshape(-1, P, DM)

    def by_rotation(w):
        return w.reshape(DM, HC, 8, 8).transpose(0, 2, 1, 3).reshape(DM, DM)

    def ffn(i):
        g, u, dn = tiles(gate[i]), tiles(up[i]), down[i].reshape(FT, P, DM)
        out = [g[0], u[0], g[1], u[1]]
        for it in range(NIT):
            if it + 1 < NIT:
                t = 2 * it + 2
                out += [g[t], u[t], g[t + 1], u[t + 1]]
            out += [dn[2 * it], dn[2 * it + 1]]
        return out

    a, b = tiles(glu_a), tiles(glu_b)
    units = [x for m in range(KT) for x in (a[m], b[m])] + ffn(0)
    units += list(tiles(by_rotation(w_k))) + list(tiles(w_v)) + list(tiles(by_rotation(w_q)))
    units += list(tiles(w_o)) + ffn(1)
    return np.stack(units)


def kernel(x_prompt, x_sample, cache_k, cache_v, state_ssm_re, state_ssm_im, page_table,
           mix_norm, ffn_norm, kv_norm, final_norm,
           ssm_a_re, ssm_a_im, ssm_log_dt, ssm_b_re, ssm_b_im, ssm_c_re, ssm_c_im, ssm_d,
           glu_w_a, glu_w_b, w_q, w_k, w_v, lambda_q1, lambda_k1, lambda_q2, lambda_k2,
           subln, w_o, ffn_w_gate, ffn_w_up, ffn_w_down):
    import concourse.bacc as bacc
    from concourse.bass_utils import run_bass_kernel_spmd

    def np_(x):
        return np.asarray(x)

    def by_state(x):
        x = x.reshape((PAIRS, P) + x.shape[2:])
        return np.moveaxis(x, 1, 0)

    are, aim, ldt = np_(ssm_a_re)[0], np_(ssm_a_im)[0], np_(ssm_log_dt)[0]
    arrays = {
        "x_t": np.concatenate([np_(x_prompt)[0].T, np_(x_sample)[:, 0].T], axis=1),
        "gains": np.stack([np_(mix_norm)[0], np_(mix_norm)[1], np_(ffn_norm)[0], np_(ffn_norm)[1],
                           np_(kv_norm), np_(final_norm)]).reshape(6, KT, P).transpose(2, 0, 1),
        "s_abc": np.stack([by_state(are), by_state(aim),
                           by_state(np.broadcast_to(ldt[:, None], (NG, ST)))], axis=1),
        "s_b": np.stack([by_state(np_(ssm_b_re)[0]), by_state(np_(ssm_b_im)[0])], axis=1),
        "s_c": np.stack([by_state(np_(x)[0].transpose(0, 2, 1)) for x in (ssm_c_re, ssm_c_im)], axis=1),
        "s_h0": np.stack([by_state(np_(x)[0].transpose(1, 2, 0)) for x in (state_ssm_re, state_ssm_im)], axis=1),
        "s_d": np_(ssm_d)[0].reshape(NG, 16).T,
        "lam": np.concatenate([np_(lambda_q1), np_(lambda_k1), np_(lambda_q2), np_(lambda_k2)]),
        "subln": np_(subln)[0][:, None],
        "page_table": np_(page_table).reshape(1, NS * NPG),
        "cache_k": np_(cache_k).reshape(-1, PAGE, DM),
        "cache_v": np_(cache_v).reshape(-1, PAGE, DM),
        "w": weight_stream(np_(glu_w_a)[0], np_(glu_w_b)[0], np_(w_k), np_(w_v), np_(w_q)[0], np_(w_o)[0],
                           np_(ffn_w_gate), np_(ffn_w_up), np_(ffn_w_down)),
    }
    arrays.update(constants())
    outs = {"kt": (KT, P, T), "vt": (KT, P, T), "y_t": (DM, T), "ssm_p": (P, 2, PAIRS, 1),
            "ssm_s": (P, 2, PAIRS, NS)}
    scratch = {"u": (DM, T), "z": (DM, T), "qt": (KT, P, T), "qrow": (NS, DM)}

    nc = bacc.Bacc("TRN2", target_bir_lowering=False, num_devices=1)
    d = {"n_pages": arrays["cache_k"].shape[0]}
    feed = {}
    for name, a in arrays.items():
        feed[name] = np.ascontiguousarray(a)
        d[name] = nc.dram_tensor(name, a.shape, mybir.dt.from_np(a.dtype), kind="ExternalInput").ap()
    for name, shape in outs.items():
        d[name] = nc.dram_tensor(name, shape, F32, kind="ExternalOutput").ap()
    for name, shape in scratch.items():
        d[name] = nc.dram_tensor(name, shape, F32, kind="Internal").ap()
    build(nc, d)
    r = run_bass_kernel_spmd(nc, [feed], core_ids=[0]).results[0]

    k = r["kt"].reshape(KT, NH, 2, 8, T).transpose(4, 1, 2, 0, 3).reshape(T, NH, 2, HD)
    v = r["vt"].transpose(2, 0, 1)
    y = r["y_t"].T

    def states(x, n):
        return x.reshape(P, PAIRS, n).transpose(2, 1, 0).reshape(1, n, NG, ST)

    sp_, ss = r["ssm_p"], r["ssm_s"]
    return (y[None, :SEQ], y[SEQ:, None], k[None, :SEQ], v[None, :SEQ], states(sp_[:, 0], 1), states(sp_[:, 1], 1),
            k[SEQ:, None], v[SEQ:, None], states(ss[:, 0], NS), states(ss[:, 1], NS))
```
